# Optimizing a Trainium2 kernel written in Bass

```python
import jax
import jax.numpy as jnp
from jax import lax
import numpy as np

D_MODEL = 2048
BATCH = 1
SEQ = 256
DEPTH = 2

CHUNK = 64
Q_BLOCK = 128
EPS = 1e-6

M_HEADS = 4
M_DQK = 128
M_DV = 256
F_HEADS = 8
F_DH = 128
G_HEADS = 4
G_DK = 256
G_DV = 512
G_RANK = 16
G_TAU = 16.0
D_FF = 5632
CONV_W = 3

N_EVEN = (DEPTH + 1) // 2
N_ODD = DEPTH // 2

EVEN_SIZES = (M_HEADS * M_DQK, M_HEADS * M_DQK, M_HEADS * M_DV, M_HEADS * M_DV, 2 * M_HEADS,
              F_HEADS * F_DH, F_HEADS * F_DH, F_HEADS * F_DH, F_HEADS)
EVEN_IN = sum(EVEN_SIZES)
EVEN_OUT = M_HEADS * M_DV + F_HEADS * F_DH
ODD_SIZES = (G_HEADS * G_DK, G_HEADS * G_DK, G_HEADS * G_DV, G_HEADS * G_DV, G_RANK)
ODD_IN = sum(ODD_SIZES)
ODD_OUT = G_HEADS * G_DV

kernel_name = "hybrid_mlstm_fox_gla_convffn_block"

def _split(u, sizes):
    return jnp.split(u, np.cumsum(sizes)[:-1].tolist(), axis=-1)

def rms_norm(x, w):
    xf = x.astype(jnp.float32)
    y = xf * lax.rsqrt(jnp.mean(xf * xf, axis=-1, keepdims=True) + EPS)
    return (y * w.astype(jnp.float32)).astype(x.dtype)

def _to_chunks(a):
    b, t, h = a.shape[:3]
    a = a.reshape((b, t // CHUNK, CHUNK, h) + a.shape[3:])
    return jnp.moveaxis(a, (1, 3), (0, 2))

def _from_chunks(a):
    a = jnp.moveaxis(a, (0, 2), (1, 3))
    b, nc, l, h = a.shape[:4]
    return a.reshape((b, nc * l, h) + a.shape[4:])

def mlstm(q, k, v, i_pre, f_pre):
    b, t, h, dk = q.shape
    dv = v.shape[-1]
    f32 = jnp.float32
    qc = _to_chunks(q.astype(f32) * dk ** -0.5)
    kc = _to_chunks(k.astype(f32))
    vc = _to_chunks(v.astype(f32))
    lfc = _to_chunks(jax.nn.log_sigmoid(f_pre.astype(f32)))
    igc = _to_chunks(i_pre.astype(f32))
    causal = jnp.tril(jnp.ones((CHUNK, CHUNK), dtype=bool))

    def step(carry, inp):
        c_st, n_st, m_st = carry
        qb, kb, vb, lf, ig = inp
        cum = jnp.cumsum(lf, axis=-1)
        dmat = cum[..., :, None] - cum[..., None, :] + ig[..., None, :]
        dmat = jnp.where(causal, dmat, -jnp.inf)
        inter = cum + m_st[..., None]
        m_t = jnp.maximum(inter, jnp.max(dmat, axis=-1))
        s = jnp.einsum("bhtd,bhsd->bhts", qb, kb) * jnp.exp(dmat - m_t[..., None])
        g = jnp.exp(inter - m_t)
        num = (jnp.einsum("bhts,bhsv->bhtv", s, vb)
               + g[..., None] * jnp.einsum("bhtd,bhdv->bhtv", qb, c_st))
        den = jnp.sum(s, axis=-1) + g * jnp.einsum("bhtd,bhd->bht", qb, n_st)
        h_out = num / jnp.maximum(jnp.abs(den), jnp.exp(-m_t))[..., None]
        last = cum[..., -1]
        dec = last[..., None] - cum + ig
        m_new = jnp.maximum(last + m_st, jnp.max(dec, axis=-1))
        ws = jnp.exp(dec - m_new[..., None])
        gs = jnp.exp(last + m_st - m_new)
        c_new = gs[..., None, None] * c_st + jnp.einsum("bhs,bhsd,bhsv->bhdv", ws, kb, vb)
        n_new = gs[..., None] * n_st + jnp.einsum("bhs,bhsd->bhd", ws, kb)
        return (c_new, n_new, m_new), h_out

    init = (jnp.zeros((b, h, dk, dv), f32), jnp.zeros((b, h, dk), f32), jnp.zeros((b, h), f32))
    _, hs = lax.scan(step, init, (qc, kc, vc, lfc, igc))
    return _from_chunks(hs)

def forgetting_attention(q, k, v, f_pre):
    b, t, h, d = q.shape
    cum = jnp.cumsum(jax.nn.log_sigmoid(f_pre.astype(jnp.float32)), axis=1).transpose(0, 2, 1)
    nb = t // Q_BLOCK
    q_blocks = q.reshape(b, nb, Q_BLOCK, h, d).transpose(1, 0, 2, 3, 4)
    cum_blocks = cum.reshape(b, h, nb, Q_BLOCK).transpose(2, 0, 1, 3)
    starts = jnp.arange(nb, dtype=jnp.int32) * Q_BLOCK
    key_pos = jnp.arange(t, dtype=jnp.int32)
    scale = d ** -0.5

    def one_block(args):
        qi, cum_i, start = args
        logits = jnp.einsum("bqhd,bkhd->bhqk", qi, k, preferred_element_type=jnp.float32) * scale
        logits = logits + (cum_i[..., :, None] - cum[..., None, :])
        q_pos = start + jnp.arange(Q_BLOCK, dtype=jnp.int32)
        logits = jnp.where(q_pos[:, None] >= key_pos[None, :], logits, -jnp.inf)
        p = jax.nn.softmax(logits, axis=-1)
        return jnp.einsum("bhqk,bkhd->bqhd", p.astype(v.dtype), v)

    out = lax.map(one_block, (q_blocks, cum_blocks, starts))
    return out.transpose(1, 0, 2, 3, 4).reshape(b, t, h, d)

def gla(q, k, v, log_a):
    b, t, h, dk = q.shape
    dv = v.shape[-1]
    f32 = jnp.float32
    qc = _to_chunks(q.astype(f32) * dk ** -0.5)
    kc = _to_chunks(k.astype(f32))
    vc = _to_chunks(v.astype(f32))
    lac = _to_chunks(log_a.astype(f32))
    causal = jnp.tril(jnp.ones((CHUNK, CHUNK), dtype=bool))[:, :, None]

    def step(s_st, inp):
        qb, kb, vb, la = inp
        cum = jnp.cumsum(la, axis=2)
        diff = cum[:, :, :, None, :] - cum[:, :, None, :, :]
        decay = jnp.exp(jnp.where(causal, diff, -jnp.inf))
        attn = jnp.einsum("bhtd,bhsd,bhtsd->bhts", qb, kb, decay)
        o = (jnp.einsum("bhts,bhsv->bhtv", attn, vb)
             + jnp.einsum("bhtd,bhdv->bhtv", qb * jnp.exp(cum), s_st))
        last = cum[:, :, -1:, :]
        s_new = (jnp.exp(last[:, :, 0, :])[..., None] * s_st
                 + jnp.einsum("bhsd,bhsv->bhdv", kb * jnp.exp(last - cum), vb))
        return s_new, o

    _, os_ = lax.scan(step, jnp.zeros((b, h, dk, dv), f32), (qc, kc, vc, lac))
    return _from_chunks(os_)

def even_mixer(h, w_in, m_gate_b, m_norm_w, fox_f_b, w_out):
    b, t, _ = h.shape
    u = h @ w_in
    mq, mk, mv, mo, mg, fq, fk, fv, ff = _split(u, EVEN_SIZES)
    mg = mg + m_gate_b
    hm = mlstm(mq.reshape(b, t, M_HEADS, M_DQK), mk.reshape(b, t, M_HEADS, M_DQK),
               mv.reshape(b, t, M_HEADS, M_DV), mg[..., :M_HEADS], mg[..., M_HEADS:])
    hm = rms_norm(hm.astype(h.dtype), m_norm_w.reshape(M_HEADS, M_DV))
    hm = hm * jax.nn.sigmoid(mo).reshape(b, t, M_HEADS, M_DV)
    hf = forgetting_attention(fq.reshape(b, t, F_HEADS, F_DH), fk.reshape(b, t, F_HEADS, F_DH),
                              fv.reshape(b, t, F_HEADS, F_DH), ff + fox_f_b)
    y = jnp.concatenate([hm.reshape(b, t, -1), hf.reshape(b, t, -1)], axis=-1)
    return y @ w_out

def odd_mixer(h, w_in, a_w2, a_b, g_norm_w, w_out):
    b, t, _ = h.shape
    u = h @ w_in
    gq, gk, gv, gr, ga = _split(u, ODD_SIZES)
    log_a = jax.nn.log_sigmoid((ga @ a_w2 + a_b).astype(jnp.float32)) / G_TAU
    o = gla(gq.reshape(b, t, G_HEADS, G_DK), gk.reshape(b, t, G_HEADS, G_DK),
            gv.reshape(b, t, G_HEADS, G_DV), log_a.reshape(b, t, G_HEADS, G_DK))
    o = rms_norm(o.astype(h.dtype), g_norm_w.reshape(G_HEADS, G_DV))
    o = o * jax.nn.silu(gr).reshape(b, t, G_HEADS, G_DV)
    return o.reshape(b, t, -1) @ w_out

def conv_ffn(h, w_in, conv_w, conv_b, w_out):
    u = h @ w_in
    u = lax.conv_general_dilated(u, conv_w, window_strides=(1,), padding=((CONV_W - 1, 0),),
                                 dimension_numbers=("NWC", "WIO", "NWC"),
                                 feature_group_count=2 * D_FF) + conv_b
    a, g = jnp.split(u, 2, axis=-1)
    return (a * jax.nn.gelu(g, approximate=True)) @ w_out

def setup_inputs(seed: int = 0) -> dict:
    key = jax.random.key(seed)
    ks = jax.random.split(key, 24)
    nrm = jax.random.normal
    d = D_MODEL
    x = nrm(ks[0], (BATCH, SEQ, d), jnp.float32)
    c = nrm(ks[1], (BATCH, d), jnp.float32)
    ada_w = nrm(ks[2], (DEPTH, d, 6 * d), jnp.float32) * (0.5 * d ** -0.5)
    ada_b = 0.02 * nrm(ks[3], (DEPTH, 6 * d), jnp.float32)
    norm_w = 1.0 + 0.05 * nrm(ks[4], (DEPTH, 4, d), jnp.float32)
    even_in_w = nrm(ks[5], (N_EVEN, d, EVEN_IN), jnp.float32) * d ** -0.5
    i_b = 0.1 * nrm(ks[6], (N_EVEN, M_HEADS), jnp.float32)
    f_b = jnp.linspace(3.0, 6.0, M_HEADS)[None, :] + 0.1 * nrm(ks[7], (N_EVEN, M_HEADS), jnp.float32)
    m_gate_b = jnp.concatenate([i_b, f_b], axis=-1)
    m_norm_w = 1.0 + 0.05 * nrm(ks[8], (N_EVEN, M_HEADS * M_DV), jnp.float32)
    fox_f_b = jnp.linspace(1.0, 4.0, F_HEADS)[None, :] + 0.1 * nrm(ks[9], (N_EVEN, F_HEADS), jnp.float32)
    even_out_w = nrm(ks[10], (N_EVEN, EVEN_OUT, d), jnp.float32) * EVEN_OUT ** -0.5
    odd_in_w = nrm(ks[11], (N_ODD, d, ODD_IN), jnp.float32) * d ** -0.5
    gla_a_w2 = nrm(ks[12], (N_ODD, G_RANK, G_HEADS * G_DK), jnp.float32) * G_RANK ** -0.5
    gla_a_b = 0.1 * nrm(ks[13], (N_ODD, G_HEADS * G_DK), jnp.float32)
    gla_norm_w = 1.0 + 0.05 * nrm(ks[14], (N_ODD, G_HEADS * G_DV), jnp.float32)
    odd_out_w = nrm(ks[15], (N_ODD, ODD_OUT, d), jnp.float32) * ODD_OUT ** -0.5
    ffn_in_w = nrm(ks[16], (DEPTH, d, 2 * D_FF), jnp.float32) * d ** -0.5
    ffn_conv_w = nrm(ks[17], (DEPTH, CONV_W, 1, 2 * D_FF), jnp.float32) * CONV_W ** -0.5
    ffn_conv_b = 0.02 * nrm(ks[18], (DEPTH, 2 * D_FF), jnp.float32)
    ffn_out_w = nrm(ks[19], (DEPTH, D_FF, d), jnp.float32) * D_FF ** -0.5
    return {"x": x, "c": c, "ada_w": ada_w, "ada_b": ada_b, "norm_w": norm_w,
            "even_in_w": even_in_w, "m_gate_b": m_gate_b, "m_norm_w": m_norm_w,
            "fox_f_b": fox_f_b, "even_out_w": even_out_w, "odd_in_w": odd_in_w,
            "gla_a_w2": gla_a_w2, "gla_a_b": gla_a_b, "gla_norm_w": gla_norm_w,
            "odd_out_w": odd_out_w, "ffn_in_w": ffn_in_w, "ffn_conv_w": ffn_conv_w,
            "ffn_conv_b": ffn_conv_b, "ffn_out_w": ffn_out_w}

def reference(x, c, ada_w, ada_b, norm_w, even_in_w, m_gate_b, m_norm_w, fox_f_b, even_out_w,
              odd_in_w, gla_a_w2, gla_a_b, gla_norm_w, odd_out_w, ffn_in_w, ffn_conv_w,
              ffn_conv_b, ffn_out_w):
    cond = jax.nn.silu(c)
    for layer in range(DEPTH):
        mod = (cond @ ada_w[layer] + ada_b[layer])[:, None, :]
        sh_m, sc_m, g_m, sh_f, sc_f, g_f = jnp.split(mod, 6, axis=-1)
        h = rms_norm(x, norm_w[layer, 0]) * (1.0 + sc_m) + sh_m
        j = layer // 2
        if layer % 2 == 0:
            y = even_mixer(h, even_in_w[j], m_gate_b[j], m_norm_w[j], fox_f_b[j], even_out_w[j])
        else:
            y = odd_mixer(h, odd_in_w[j], gla_a_w2[j], gla_a_b[j], gla_norm_w[j], odd_out_w[j])
        x = x + g_m * rms_norm(y, norm_w[layer, 1])
        h = rms_norm(x, norm_w[layer, 2]) * (1.0 + sc_f) + sh_f
        y = conv_ffn(h, ffn_in_w[layer], ffn_conv_w[layer], ffn_conv_b[layer], ffn_out_w[layer])
        x = x + g_f * rms_norm(y, norm_w[layer, 3])
    return x


_drawn_inputs = setup_inputs


def setup_inputs(seed=0):
    import zlib

    import numpy as np

    out = dict(_drawn_inputs(seed))
    spreads = {}
    factors = {'m_norm_w': 4.709, 'gla_a_b': 3.974, 'gla_norm_w': 3.87, 'ffn_conv_b': 3.638}
    for name, (base, spread) in spreads.items():
        noise = np.random.default_rng([zlib.crc32(name.encode()), seed]).standard_normal(out[name].shape)
        drawn = base * np.exp(spread * noise) if base else spread * noise
        out[name] = jnp.asarray(drawn.astype(out[name].dtype))
    for name, factor in factors.items():
        out[name] = (out[name] * factor).astype(out[name].dtype)
    return out
```

```python
from contextlib import ExitStack

import numpy as np

import concourse.bass as bass
from concourse import mybir

F32 = mybir.dt.float32
F32R = mybir.dt.float32r
ALU = mybir.AluOpType
ACT = mybir.ActivationFunctionType
AX_X = mybir.AxisListType.X

P = 128
T = 256
TB = T // P
D = 2048
DK = D // P
EPS = 1e-6
LAYERS = 2

M_HEADS, M_DQK, M_DV = 4, 128, 256
F_HEADS, F_DH = 8, 128
G_HEADS, G_DK, G_DV, G_RANK, G_TAU = 4, 256, 512, 16, 16.0
D_FF = 5632
CONV_W = 3
GATES = 16

UNIT = DK * P
RAW_SLOTS, SPLIT_SLOTS = 4, 2
PIECE = 1024
PIECES = D // P * (D // PIECE)
SECTIONS = 6 * LAYERS
ADA_SLOTS = 2
HEAD_SLOTS = 8
FF_GROUPS = (16, 16, 12)

LEVELS = 8
NEG = -1e30


class Phase:

    def __init__(self, kind, layer, n0, t0, a0, bodies, units, ada, group=0, peel=0):
        self.kind, self.layer, self.group = kind, layer, group
        self.n0, self.t0, self.a0 = n0, t0, a0
        self.bodies, self.units, self.ada = bodies, units, ada
        self.peel = peel
        self.per_body = sum(ada)
        self.tiles = 2 if kind == "values" else units
        self.end = n0 + bodies * units
        self.section = a0 // PIECES
        self.opens = self.per_body > 0 and a0 % PIECES == 0
        self.closes = self.per_body > 0 and (a0 + bodies * self.per_body) % PIECES == 0


def plan():
    phases, n, t, a, pairs = [], 0, 0, 2 * PIECES, 0
    for layer in range(LAYERS):
        rows = [("gates", 0, 1, 1, (0,)), ("columns", 0, 8, 4, (1,) * 4), ("values", 0, 2, 8, (2,) * 8),
                ("mixed", 0, 4, 4, (2,) * 4)]
        for g, tiles in enumerate(FF_GROUPS):
            up, down = ((1, 0, 1, 0), (1,) * 4) if g < 2 else ((1,) * 4, (1, 0, 1, 0))
            if layer == LAYERS - 1 and g > 0:
                up = down = (0,) * 4
            rows += [("ff_up", g, tiles // 2, 4, up), ("ff_down", g, 4, 4, down)]
        for kind, g, bodies, units, ada in rows:
            last = layer == LAYERS - 1 and g == len(FF_GROUPS) - 1 and kind == "ff_down"
            last_ada = layer == LAYERS - 1 and g == 0 and kind == "ff_down"
            ph = Phase(kind, layer, n, t, a, bodies, units, ada, g, 2 if last else 1 if last_ada else 0)
            ph.pairs = pairs
            pairs += 2 * bodies if kind == "ff_up" else 0
            phases.append(ph)
            n, t, a = ph.end, t + bodies * ph.tiles, a + bodies * ph.per_body
    assert a == SECTIONS * PIECES
    return phases, n


PHASES, UNITS = plan()

V_C, V_ADAB = 0, DK
V_NORM = V_ADAB + SECTIONS * DK
V_MNORM = V_NORM + LAYERS * 4 * DK
V_GNORM = V_MNORM + M_HEADS * M_DV // P
V_AB = V_GNORM + G_HEADS * G_DV // P
V_GATEB = V_AB + G_HEADS * G_DK // P
V_COEF = V_GATEB + 1
V_CONV = V_COEF + M_HEADS + F_HEADS
FF_TILES = 2 * D_FF // P
V_END = V_CONV + LAYERS * FF_TILES * (CONV_W + 1)

MQ, MK, MO, FQ, FK = 0, 4, 8, 16, 24
GQ, GK, GR = 0, 8, 16
V_AT = 32 * T
REGION = V_AT + TB * D


class Tally:

    def __init__(self, sem, start=0):
        self.sem, self.base, self.at, self.extra = sem, start, start, 0

    def tick(self, k=1):
        self.at = self.at + k
        self.extra += k
        return k

    def step(self, k=1):
        self.tick(k)
        return self.at

    def enter(self, i, per):
        self.base, self.per, self.extra = self.at, per, 0
        self.at = self.at + i * per

    def leave(self, trips):
        assert self.extra == self.per, (self.sem, self.extra, self.per)
        self.at = self.base + trips * self.per


def repeat(eng, ph, body, head=0):
    for i in range(head):
        body(i)
    if ph.bodies - ph.peel - head > 1:
        with eng.Fori(head, ph.bodies - ph.peel) as i:
            body(i)
    else:
        for i in range(head, ph.bodies - ph.peel):
            body(i)
    for i in range(ph.bodies - ph.peel, ph.bodies):
        body(i)


def program(nc, w_dram, ada_dram, vec_dram, x_dram, ident_dram, causal_dram, blocks_dram, w2_dram, out_dram):
    with ExitStack() as ctx:
        def sb(name, shape, dt=F32):
            return ctx.enter_context(nc.sbuf_tensor(name, shape, dt))

        def sem(name):
            return ctx.enter_context(nc.semaphore(name))

        region_at = -(-nc.sbuf_base // 32) * 32
        region = sb("region", [P, REGION])
        mid = nc.alloc_sbuf_tensor_at("mid", [P, 16, 2 * T], F32R, offset=region_at)
        x = sb("x", [P, DK, T])
        y = sb("y", [P, DK, T])
        act = sb("act", [P, DK, 2 * T], F32R)
        raw = sb("raw", [P, RAW_SLOTS, UNIT])
        hi = sb("hi", [P, SPLIT_SLOTS, UNIT], F32R)
        lo = sb("lo", [P, SPLIT_SLOTS, UNIT], F32R)
        piece = sb("piece", [P, ADA_SLOTS, PIECE])
        acc = sb("acc", [P, D])
        vec = sb("vec", [P, V_END])
        mod = sb("mod", [P, SECTIONS, DK])
        cond = sb("cond", [P, DK])
        alpha = sb("alpha", [P, DK])
        gamma = sb("gamma", [P, DK])
        ident = sb("ident", [P, P])
        ones = sb("ones", [P, T])
        masks = sb("masks", [P, LEVELS * P])
        gates = sb("gates", [GATES, T])
        stat = sb("stat", [P, 64])

        yf = y[:, :, :].rearrange("p a t -> p (a t)")
        at = 16 * 2 * T

        def ff(width, count):
            nonlocal at
            got = region[:, at:at + width * count].rearrange("p (a t) -> p a t", a=count)
            at += width * count
            return got

        conv_a, conv_g, gelu_g, ff_m = ff(T, 2), ff(T, 2), ff(T, 2), ff(T, 2)
        assert at <= REGION
        values = region[:, V_AT:REGION].rearrange("p (b c) -> p b c", b=TB)

        bank = [ctx.enter_context(nc.psum_tensor(f"bank{k}", [P, 512], F32)) for k in range(8)]

        s_raw = [sem(f"raw_ready{j}") for j in range(RAW_SLOTS)]
        s_hi = sem("hi_ready")
        s_lo = sem("lo_ready")
        s_unit = sem("unit_done")
        s_evac = sem("tile_evacuated")
        s_piece = [sem(f"piece_ready{j}") for j in range(ADA_SLOTS)]
        s_head = [sem(f"head_piece_ready{j}") for j in range(HEAD_SLOTS)]
        s_mac = sem("piece_summed")
        s_red = sem("section_reduced")
        s_mod = sem("section_stored")
        s_in = {k: sem(f"loaded_{k}") for k in ("vec", "x", "ident", "causal", "blocks")}
        s_cond = sem("cond_ready")
        s_ones = sem("ones_ready")
        s_v = sem("vector_step")
        s_sq = sem("squares_ready")
        s_mean = sem("mean_square_ready")
        s_root = sem("root_ready")
        s_sqp = sem("squares_summed")
        s_h = sem("normed_ready")
        s_hh = sem("act_hi_ready")
        s_act = sem("act_ready")
        s_x = sem("x_updated")
        s_gelu = sem("gelu_ready")
        s_mul = sem("ff_product_ready")
        s_mh = sem("mid_hi_ready")
        s_mid = sem("mid_ready")
        s_store = sem("stored")
        names = ("gate_abs", "gate_ln", "gate_cum", "gate_t", "gate_col", "side",
                 "qst", "vst", "row", "score", "lmax", "prob", "pn", "pt", "pc", "pv", "oh", "ol",
                 "m_qst", "m_vst", "m_row", "m_score", "m_max", "m_prob", "m_pn", "m_pt", "m_pc", "m_pv",
                 "m_sq", "m_ss", "m_out", "m_oh", "m_ol",
                 "w2", "g_vst", "z", "zb", "g_ln", "decay", "copies", "copies_gp", "expd", "scaled", "prod", "used",
                 "st", "g_pv", "g_sq", "g_ss", "g_out", "g_oh", "g_ol")
        s = {k: sem(k) for k in names}

        block = ctx.enter_context(nc.Block())

        def unit(ph, i, j):
            return ph.n0 + i * ph.units + j

        def tile_(ph, i, j):
            return ph.t0 + i * ph.tiles + j

        def fq_st(k):
            return yf[:, 1024 * k:1024 * k + 256]

        def fv_st(k):
            return yf[:, 1024 * k + 256:1024 * k + 512].rearrange("p (b c) -> p b c", b=TB)

        def f_l(k):
            return yf[:, 1024 * k + 512:1024 * k + 1024].rearrange("p (b c) -> p b c", b=TB)

        def m_q(k):
            return yf[:, 1280 * k:1280 * k + 256]

        def m_v(k):
            return yf[:, 1280 * k + 256:1280 * k + 768].rearrange("p (b c) -> p b c", b=TB)

        def m_l(k):
            return yf[:, 1280 * k + 768:1280 * k + 1280].rearrange("p (b c) -> p b c", b=TB)

        gf = acc[0:GATES, 0:256]

        def row(k):
            return acc[0:GATES, 1024 + 256 * k:1280 + 256 * k]

        def g_q(b):
            return yf[:, 512 * b:512 * b + 512]

        def g_k(b):
            return yf[:, 1024 + 512 * b:1536 + 512 * b]

        g_q2 = yf[:, 0:1024].rearrange("p (a t) -> p a t", a=4)
        g_k2 = yf[:, 1024:2048].rearrange("p (a t) -> p a t", a=4)
        g_a, g_r, g_e = yf[:, 2048:2560], yf[:, 2560:3072], yf[:, 3072:3584]
        g_tmp = yf[:, 3584:3840].rearrange("p (b c) -> p b c", b=TB)
        g_v = acc[:, 0:1024].rearrange("p (b c) -> p b c", b=TB)
        g_s = acc[:, 1024:1536].rearrange("p (b c) -> p b c", b=TB)
        g_w2 = acc[0:G_RANK, 1536:1792]
        r_y = yf[:, 3584:3584 + T]
        r_r = region[:, V_AT + 2 * 4 * T:V_AT + 9 * T]

        def flat(ap):
            return ap.rearrange("p a t -> p (a t)")


        def side(ap, b, right):
            return ap.rearrange("p (n two c) -> p n two c", two=2, c=b)[:, :, right, :]

        @block.sync
        def _(sp):
            sp.dma_start(vec[:, :], vec_dram).then_inc(s_in["vec"], 16)

            def head_load(i, j):
                at_ = region[:, j * PIECE:(j + 1) * PIECE]
                src = ada_dram[bass.ds(i * HEAD_SLOTS + j, 1)].rearrange("a p n -> p (a n)")
                sp.dma_start(at_, src).then_inc(s_head[j], 16)

            for j in range(HEAD_SLOTS):
                head_load(0, j)
            sp.dma_start(x[:, :, :], x_dram).then_inc(s_in["x"], 16)
            sp.dma_start(ident[:, :], ident_dram).then_inc(s_in["ident"], 16)
            sp.dma_start(masks[:, 0:TB * T], causal_dram).then_inc(s_in["causal"], 16)
            with sp.Fori(1, 2 * PIECES // HEAD_SLOTS) as i:
                for j in range(HEAD_SLOTS):
                    sp.wait_ge(s_mac, (i - 1) * HEAD_SLOTS + j + 1)
                    head_load(i, j)

            def load_unit(n, slot):
                src = w_dram[bass.ds(n, 1)].rearrange("a p n -> p (a n)")
                sp.dma_start(raw[:, slot, :], src).then_inc(s_raw[slot], 16)

            def load_piece(a, slot):
                src = ada_dram[bass.ds(a, 1)].rearrange("a p n -> p (a n)")
                sp.dma_start(piece[:, slot, :], src).then_inc(s_piece[slot], 16)

            for n in range(RAW_SLOTS):
                load_unit(n, n)
            for a in range(ADA_SLOTS):
                load_piece(2 * PIECES + a, a)
            sp.wait_ge(s_lo, RAW_SLOTS + 1)
            load_unit(RAW_SLOTS, 0)

            for ph in PHASES:
                if ph.kind == "columns" and ph.layer == 1:
                    sp.wait_ge(s_lo, RAW_SLOTS + ph.n0 + 1)
                    sp.dma_start(masks[:, :], blocks_dram).then_inc(s_in["blocks"], 16)

                def body(i, ph=ph):
                    k = 0
                    for j in range(ph.units):
                        n = unit(ph, i, j)
                        if ph.n0 + j + RAW_SLOTS + 1 + (i if isinstance(i, int) else 0) * ph.units < UNITS:
                            sp.wait_ge(s_lo, RAW_SLOTS + n + 2)
                            load_unit(n + RAW_SLOTS + 1, (ph.n0 + j + 1) % RAW_SLOTS)
                        for _ in range(ph.ada[j]):
                            a = ph.a0 + i * ph.per_body + k
                            if not isinstance(a, int) or a + ADA_SLOTS < SECTIONS * PIECES:
                                sp.wait_ge(s_mac, a + 1)
                                load_piece(a + ADA_SLOTS, k % ADA_SLOTS)
                            k += 1

                if ph.kind == "mixed" and ph.layer == 1:
                    with sp.Fori(0, G_HEADS) as h:
                        sp.wait_ge(s["side"], 2)
                        sp.wait_ge(s["z"], h)
                        sp.dma_start(acc[0:G_RANK, 1536:1792],
                                     w2_dram[bass.ds(h, 1)].rearrange("a r c -> r (a c)")).then_inc(s["w2"], 16)
                repeat(sp, ph, body)

            sp.wait_ge(s_x, 8 * LAYERS)
            sp.dma_start(out_dram, x[:, :, :]).then_inc(s_store, 16)
            sp.wait_ge(s_store, 16)

        @block.scalar
        def _(sc):
            def split(n, slot, raw_slot, uses):
                sc.wait_ge(s_raw[raw_slot], 16 * uses)
                sc.wait_ge(s_unit, n + 1)
                sc.activation(hi[:, slot, :], raw[:, raw_slot, :], ACT.Copy).then_inc(s_hi, 1)

            def split_next(ph, i, j):
                m = ph.n0 + j + 1
                if isinstance(i, int) and unit(ph, i, j) + 1 >= UNITS:
                    return
                split(unit(ph, i, j) + 1, m % SPLIT_SLOTS, m % RAW_SLOTS,
                      m // RAW_SLOTS + i * (ph.units // RAW_SLOTS) + 1)

            sqp = Tally(s_sqp)
            xup = Tally(s_x)
            means = Tally(s_mean)

            def root(at_):
                sc.wait_ge(s_mean, means.step())
                sc.activation(at_, at_, ACT.Sqrt).then_inc(s_root, 1)

            hr = Tally(s_h)

            def squares(src, dst, ready):
                for b in range(4):
                    ready(b)
                    if sqp.at + b >= 2:
                        sc.wait_ge(s_sqp, sqp.at + b - 1)
                    sc.activation(dst[:, b % 2], src[:, 4 * b:4 * b + 4, :], ACT.Square).then_inc(s_sq, 1)
                sqp.tick(4)

            sq_y = yf[:, 0:2 * 4 * T].rearrange("p (b a t) -> p b a t", b=2, a=4)
            sq_r = region[:, V_AT:V_AT + 2 * 4 * T].rearrange("p (b a t) -> p b a t", b=2, a=4)
            h_buf = yf[:, 2048:2048 + 4 * T].rearrange("p (b t) -> p b t", b=4)

            def pre_norm():
                def ready(b):
                    if xup.at == 0:
                        sc.wait_ge(s_in["x"], 16)
                    else:
                        sc.wait_ge(s_x, xup.at - 4 + b + 1)
                squares(x, sq_y, ready)
                root(r_y)
                with sc.Fori(0, 4) as i:
                    hr.enter(i, 4)
                    for b in range(4):
                        sc.wait_ge(s_h, hr.step())
                        sc.activation(act[:, bass.ds(4 * i + b, 1), 0:T].rearrange("p a t -> p (a t)"),
                                      h_buf[:, b, :], ACT.Copy).then_inc(s_hh, 1)
                hr.leave(4)

            def post_norm(ph):
                def ready(b):
                    sc.wait_ge(s_evac, 2 + ph.t0 + 4 * b + 4)
                squares(y, sq_r, ready)
                root(r_r)
                xup.tick(4)

            def exps_two(dst, bias_at, sums):
                for tb in range(TB):
                    i_ = sc.activation(dst[:, tb, :], dst[:, tb, :], ACT.Exp, bias=stat[:, bias_at + tb:bias_at + tb + 1],
                                       **({} if sums is None else {"accum_out": stat[:, sums + tb:sums + tb + 1]}))
                return i_

            def u_tile(k):
                return region[:, bass.ds(k * T, T)]

            def even_mixer():
                t1 = acc[0:GATES, 256:512]
                sc.wait_ge(s["side"], 1)
                sc.activation(t1, gates[:, :], ACT.Abs).then_inc(s["gate_abs"], 1)
                sc.wait_ge(s["gate_abs"], 1)
                sc.activation(t1, t1, ACT.Exp, scale=-1.0).then_inc(s["gate_abs"], 1)
                sc.wait_ge(s["gate_abs"], 2)
                sc.activation(t1, t1, ACT.Ln, bias=1.0).then_inc(s["gate_ln"], 1)
                sc.activation(region[:, MO * T:(MO + 8) * T], region[:, MO * T:(MO + 8) * T],
                              ACT.Sigmoid).then_inc(s["gate_ln"], 1)
                with sc.Fori(0, F_HEADS // 4) as i:
                    for k in range(4):
                        sc.activation(fq_st(k), u_tile(FQ + 4 * i + k), ACT.Copy,
                                      scale=float(F_DH) ** -0.5).then_inc(s["qst"], 1)
                    for k in range(4):
                        sc.wait_ge(s["lmax"], 4 * i + k + 1)
                        exps_two(f_l(k), 4 * k, 4 * k + 2).then_inc(s["prob"], 1)
                    for k in range(4):
                        sc.wait_ge(s["pt"], 4 * i + k + 1)
                        sc.activation(f_l(k)[:, 0, :], bank[4 + k][:, 0:T], ACT.Copy)
                        sc.activation(f_l(k)[:, 1, P:T], bank[4 + k][:, T + P:2 * T], ACT.Copy).then_inc(s["pc"], 1)
                    for k in range(4):
                        sc.wait_ge(s["pv"], 4 * i + k + 1)
                        sc.activation(act[:, bass.ds(8 + 4 * i + k, 1), 0:T].rearrange("p a t -> p (a t)"),
                                      bank[4 + k][:, 0:T], ACT.Copy).then_inc(s["oh"], 1)
                with sc.Fori(0, M_HEADS // 2) as i:
                    for k in range(2):
                        if k == 0:
                            sc.wait_ge(s["m_ol"], 2 * i)
                            sc.wait_ge(s["ol"], F_HEADS)
                        sc.activation(m_q(k), u_tile(MQ + 2 * i + k), ACT.Copy,
                                      scale=float(M_DQK) ** -0.5).then_inc(s["m_qst"], 1)
                    for k in range(2):
                        sc.wait_ge(s["m_max"], 2 * i + k + 1)
                        for tb in range(TB):
                            sc.activation(stat[:, 8 * k + 4 + tb:8 * k + 5 + tb],
                                          stat[:, bass.ds(32 + tb * GATES + M_HEADS + 2 * i + k, 1)], ACT.Exp,
                                          bias=stat[:, 8 * k + tb:8 * k + tb + 1], scale=-1.0)
                        exps_two(m_l(k), 8 * k, None).then_inc(s["m_prob"], 1)
                    for k in range(2):
                        sc.wait_ge(s["m_pt"], 2 * i + k + 1)
                        sc.activation(m_l(k)[:, 0, :], bank[4 + 2 * k][:, 0:T], ACT.Copy)
                        sc.activation(m_l(k)[:, 1, P:T], bank[4 + 2 * k][:, T + P:2 * T], ACT.Copy).then_inc(s["m_pc"], 1)
                    for k in range(2):
                        sc.wait_ge(s["m_pv"], 2 * i + k + 1)
                        sc.activation(m_v(k), bank[5 + 2 * k][:, :].rearrange("p (a t) -> p a t", a=2),
                                      ACT.Square).then_inc(s["m_sq"], 1)
                    means.enter(i, 2)
                    for k in range(2):
                        root(m_q(k))
                    for k in range(2):
                        sc.wait_ge(s["m_out"], 2 * i + k + 1)
                        sc.activation(act[:, bass.ds(4 * i + 2 * k, 2), 0:T], m_l(k), ACT.Copy).then_inc(s["m_oh"], 1)
                means.leave(M_HEADS // 2)

            def odd_mixer():
                sc.wait_ge(s["side"], 2)
                sc.activation(region[:, GR * T:(GR + 16) * T], region[:, GR * T:(GR + 16) * T],
                              ACT.Silu).then_inc(s["gate_ln"], 1)
                with sc.Fori(0, G_HEADS) as h:
                    sc.wait_ge(s["side"], 2)
                    sc.wait_ge(s["g_ol"], h)
                    sc.activation(g_q(0), region[:, bass.ds(GQ * T + h * 2 * T, 2 * T)], ACT.Copy)
                    sc.activation(g_k(0), region[:, bass.ds(GK * T + h * 2 * T, 2 * T)], ACT.Copy).then_inc(s["copies"], 1)
                    sc.wait_ge(s["zb"], h + 1)
                    sc.activation(g_e, g_a, ACT.Abs).then_inc(s["g_ln"], 1)
                    sc.wait_ge(s["g_ln"], 3 * h + 1)
                    sc.activation(g_e, g_e, ACT.Exp, scale=-1.0).then_inc(s["g_ln"], 1)
                    sc.wait_ge(s["g_ln"], 3 * h + 2)
                    sc.activation(g_e, g_e, ACT.Ln, bias=1.0).then_inc(s["g_ln"], 1)
                    for lv in range(1, LEVELS + 1):
                        sc.wait_ge(s["decay"], h * LEVELS + lv)
                        b = 1 << (lv - 1)
                        sc.activation(g_e[:, 0:T].rearrange("p (n c) -> p n c", c=b), side(g_a, b, 1),
                                      ACT.Exp)
                        sc.activation(g_e[:, T:2 * T].rearrange("p (n c) -> p n c", c=b), side(g_r, b, 0),
                                      ACT.Exp).then_inc(s["expd"], 1)
                    sc.wait_ge(s["g_pv"], h + 1)
                    for half in range(2):
                        i_ = sc.activation(g_q2[:, 2 * half:2 * half + 2, :],
                                           bank[6 + half][:, :].rearrange("p (a t) -> p a t", a=2), ACT.Square)
                    i_.then_inc(s["g_sq"], 1)
                    means.enter(h, 1)
                    root(g_e[:, 0:T])
                    sc.wait_ge(s["g_out"], h + 1)
                    sc.activation(act[:, bass.ds(4 * h, 4), 0:T], g_k2, ACT.Copy).then_inc(s["g_oh"], 1)
                means.leave(G_HEADS)

            sc.wait_ge(s_in["vec"], 16)
            sc.activation(cond[:, :], vec[:, V_C:V_C + DK], ACT.Silu).then_inc(s_cond, 1)
            split(0, 0, 0, 1)
            def gelu(ph, q, slot):
                sc.wait_ge(s_evac, 2 + ph.t0 + 2 * q + 2)
                sc.wait_ge(s_mul, ph.pairs + q + 1)
                sc.activation(gelu_g[:, slot, :], conv_g[:, slot, :], ACT.Gelu_apprx_tanh).then_inc(s_gelu, 1)

            def to_mid(ph, q, slot):
                sc.wait_ge(s_mul, ph.pairs + q + 3)
                sc.activation(mid[:, bass.ds(q, 1), 0:T].rearrange("p a t -> p (a t)"), ff_m[:, slot, :],
                              ACT.Copy).then_inc(s_mh, 1)

            for ph in PHASES:
                if ph.kind == "gates" or (ph.kind == "ff_up" and ph.group == 0):
                    pre_norm()

                def body(i, ph=ph):
                    for j in range(ph.units):
                        split_next(ph, i, j)
                        if ph.kind == "ff_up" and not (isinstance(i, int) and i == 0 and j < 2):
                            q = 2 * i + (j // 2 - 1)
                            (gelu if j % 2 == 0 else to_mid)(ph, q, (j // 2 + 1) % 2)

                if ph.kind == "mixed":
                    (even_mixer if ph.layer == 0 else odd_mixer)()
                if ph.kind == "ff_up":
                    if ph.group > 0:
                        sc.wait_ge(s_unit, SPLIT_SLOTS + ph.n0)
                    repeat(sc, ph, body, head=1)
                    gelu(ph, 2 * ph.bodies - 1, 1)
                    to_mid(ph, 2 * ph.bodies - 1, 1)
                else:
                    repeat(sc, ph, body)
                if ph.kind == "mixed" or (ph.kind == "ff_down" and ph.group == len(FF_GROUPS) - 1):
                    post_norm(ph)

        @block.gpsimd
        def _(gp):
            gp.memset(ones[:, :], 1.0).then_inc(s_ones, 1)
            gp.sem_inc(s_act, 4)
            gp.sem_inc(s_mul, 2)
            hh = Tally(s_hh)
            act_lo = Tally(s_act, 4)
            h_buf = yf[:, 2048:2048 + 4 * T].rearrange("p (b t) -> p b t", b=4)
            pair = Tally(s_gelu)

            for ph in PHASES:
                if ph.kind == "gates" or (ph.kind == "ff_up" and ph.group == 0):
                    with gp.Fori(0, 4) as i:
                        hh.enter(i, 4)
                        for b in range(4):
                            gp.wait_ge(s_hh, hh.step())
                            at_ = bass.ds(4 * i + b, 1)
                            gp.tensor_tensor(flat(act[:, at_, T:2 * T]), h_buf[:, b, :],
                                             flat(act[:, at_, 0:T].bitcast(F32)), ALU.subtract).then_inc(s_act, 1)
                    hh.leave(4)
                if ph.kind == "mixed" and ph.layer == 0:
                    with gp.Fori(0, F_HEADS // 4) as i:
                        for k in range(4):
                            if k == 0:
                                gp.wait_ge(s["side"], 1)
                                gp.wait_ge(s["pv"], 4 * i)
                            gp.tensor_copy(fv_st(k), values[:, :, bass.ds(1024 + 512 * i + P * k, P)])\
                              .then_inc(s["vst"], 1)
                    gp.wait_ge(s["ol"], F_HEADS)
                    with gp.Fori(0, M_HEADS // 2) as i:
                        for k in range(2):
                            if k == 0:
                                gp.wait_ge(s["m_ss"], 2 * i)
                            gp.tensor_copy(m_v(k), values[:, :, bass.ds(512 * i + 256 * k, 256)]).then_inc(s["m_vst"], 1)
                if ph.kind == "mixed" and ph.layer == 1:
                    with gp.Fori(0, G_HEADS) as h:
                        gp.wait_ge(s["side"], 2)
                        gp.wait_ge(s["g_ol"], h)
                        gp.tensor_copy(g_q(1), region[:, bass.ds(GQ * T + h * 2 * T, 2 * T)])
                        gp.tensor_copy(g_k(1), region[:, bass.ds(GK * T + h * 2 * T, 2 * T)]).then_inc(s["copies_gp"], 1)
                        gp.tensor_copy(g_v, values[:, :, bass.ds(h * G_DV, G_DV)]).then_inc(s["g_vst"], 1)
                if ph.kind == "ff_up":
                    base = pair.at

                    def body(i, base=base):
                        for slot in range(2):
                            p = base + 2 * i + slot + 1
                            at_ = bass.ds(2 * i + slot, 1)
                            gp.wait_ge(s_gelu, p)
                            gp.tensor_tensor(ff_m[:, slot, :], conv_a[:, slot, :], gelu_g[:, slot, :],
                                             ALU.mult).then_inc(s_mul, 1)
                            gp.wait_ge(s_mh, p)
                            gp.tensor_tensor(flat(mid[:, at_, T:2 * T]), ff_m[:, slot, :],
                                             flat(mid[:, at_, 0:T].bitcast(F32)), ALU.subtract).then_inc(s_mid, 1)
                    repeat(gp, ph, body)
                    pair.at = base + 2 * ph.bodies

        @block.vector
        def _(ve):
            own = Tally(s_v)
            roots = Tally(s_root)

            def mine():
                ve.wait_ge(s_v, own.at)

            def split(n, slot, raw_slot):
                ve.wait_ge(s_hi, n + 1)
                ve.tensor_tensor(lo[:, slot, :], raw[:, raw_slot, :], hi[:, slot, :].bitcast(F32),
                                 ALU.subtract).then_inc(s_lo, 1)

            def split_next(ph, i, j):
                m = ph.n0 + j + 1
                if isinstance(i, int) and unit(ph, i, j) + 1 >= UNITS:
                    return
                split(unit(ph, i, j) + 1, m % SPLIT_SLOTS, m % RAW_SLOTS)

            def summed(src, half, kt):
                at_ = acc[:, half * PIECE:(half + 1) * PIECE]
                return ve.scalar_tensor_tensor(out=at_, in0=src, scalar=cond[:, bass.ds(kt, 1)], in1=at_,
                                               op0=ALU.mult, op1=ALU.add)

            def open_section():
                ve.memset(acc[:, :], 0.0).then_inc(s_v, own.tick())
                mine()

            def close_section(sec):
                ve.wait_ge(s_red, sec + 1)
                ve.tensor_tensor(mod[:, sec, :], bank[7][:, 0:DK], vec[:, V_ADAB + sec * DK:V_ADAB + (sec + 1) * DK],
                                 ALU.add).then_inc(s_mod, 1)

            sq_n = Tally(s_sqp)
            act_n = Tally(s_act)

            def rstd(dst, src, width):
                ve.tensor_scalar(dst, src, 1.0 / width, EPS, ALU.mult, ALU.add).then_inc(s_mean, 1)
                ve.wait_ge(s_root, roots.step())
                ve.reciprocal(dst, dst).then_inc(s_v, own.tick())
                mine()

            h_buf = yf[:, 2048:2048 + 4 * T].rearrange("p (b t) -> p b t", b=4)
            t_buf = yf[:, 3072:3072 + 2 * T].rearrange("p (b t) -> p b t", b=2)
            def pre_norm(layer, part):
                sh, scl = 6 * layer + 3 * part, 6 * layer + 3 * part + 1
                w = V_NORM + (4 * layer + 2 * part) * DK
                ve.wait_ge(s_mod, scl + 1)
                ve.scalar_tensor_tensor(out=alpha[:, :], in0=mod[:, scl, :], scalar=1.0, in1=vec[:, w:w + DK],
                                        op0=ALU.add, op1=ALU.mult).then_inc(s_v, own.tick())
                ve.wait_ge(s_sqp, sq_n.step(4))
                rstd(r_y, bank[4][:, 0:T], D)
                with ve.Fori(0, 4) as i:
                    own.enter(i, 4)
                    act_n.enter(i, 4)
                    for b in range(4):
                        k = bass.ds(4 * i + b, 1)
                        ve.tensor_tensor(t_buf[:, b % 2, :], flat(x[:, k, :]), r_y, ALU.mult)\
                          .then_inc(s_v, own.tick())
                        mine()
                        ve.wait_ge(s_act, act_n.step())
                        ve.tensor_scalar(h_buf[:, b, :], t_buf[:, b % 2, :], alpha[:, k],
                                         mod[:, sh, k], ALU.mult, ALU.add).then_inc(s_h, 1)
                own.leave(4)
                act_n.leave(4)

            def post_norm(layer, part):
                w = V_NORM + (4 * layer + 2 * part + 1) * DK
                ve.wait_ge(s_mod, 6 * layer + 3 * part + 3)
                ve.tensor_tensor(gamma[:, :], mod[:, 6 * layer + 3 * part + 2, :], vec[:, w:w + DK],
                                 ALU.mult).then_inc(s_v, own.tick())
                ve.wait_ge(s_sqp, sq_n.step(4))
                rstd(r_r, bank[4][:, 0:T], D)
                with ve.Fori(0, 4) as i:
                    own.enter(i, 1)
                    four = y[:, bass.ds(4 * i, 4), :]
                    ve.tensor_tensor(four, four, r_r.unsqueeze(1).broadcast_to([P, 4, T]), ALU.mult)\
                      .then_inc(s_v, own.tick())
                    mine()
                    for b in range(4):
                        k = bass.ds(4 * i + b, 1)
                        i_ = ve.scalar_tensor_tensor(out=flat(x[:, k, :]), in0=flat(y[:, k, :]),
                                                     scalar=gamma[:, k], in1=flat(x[:, k, :]),
                                                     op0=ALU.mult, op1=ALU.add)
                    i_.then_inc(s_x, 1)
                own.leave(4)

            def even_mixer():
                t1, t2 = acc[0:GATES, 256:512], acc[0:GATES, 512:768]
                mask = masks[:, 0:TB * T].rearrange("p (b c) -> p b c", b=TB)
                ve.wait_ge(s_in["causal"], 16)
                ve.wait_ge(s["gate_ln"], 1)
                ve.scalar_tensor_tensor(out=t2, in0=gates[:, :], scalar=0.0, in1=t1, op0=ALU.min,
                                        op1=ALU.subtract).then_inc(s_v, own.tick())
                mine()
                ve.tensor_tensor_scan(gf, ones[0:GATES, :], t2, 0.0, ALU.mult, ALU.add).then_inc(s_v, own.tick())
                mine()
                ve.tensor_copy(gf[0:M_HEADS, :], gates[0:M_HEADS, :]).then_inc(s["gate_cum"], 1)
                ve.wait_ge(s["gate_cum"], 1)
                ve.wait_ge(s["gate_t"], 1)
                ve.tensor_copy(stat[:, 32:32 + TB * GATES], bank[7][:, 0:TB * GATES]).then_inc(s["gate_col"], 1)

                def normed(l_, at_):
                    ve.reciprocal(stat[:, at_:at_ + 2], stat[:, at_:at_ + 2]).then_inc(s_v, own.tick())
                    mine()
                    for tb in range(TB):
                        i_ = ve.tensor_scalar(l_[:, tb, :], l_[:, tb, :], stat[:, at_ + tb:at_ + tb + 1], None, ALU.mult)
                    return i_

                with ve.Fori(0, F_HEADS // 4) as i:
                    own.enter(i, 4 * 3)
                    for k in range(4):
                        ve.tensor_scalar(row(k), gf, vec[0:GATES, bass.ds(V_COEF + M_HEADS + 4 * i + k, 1)], None,
                                         ALU.mult).then_inc(s["row"], 1)
                    for k in range(4):
                        ve.wait_ge(s["score"], 4 * i + k + 1)
                        ve.tensor_tensor(f_l(k), bank[4 + k][:, :].rearrange("p (b c) -> p b c", b=TB), mask,
                                         ALU.add).then_inc(s_v, own.tick())
                        mine()
                        ve.tensor_reduce(stat[:, 4 * k:4 * k + 2], f_l(k), AX_X, ALU.max).then_inc(s_v, own.tick())
                        mine()
                        ve.tensor_scalar(stat[:, 4 * k:4 * k + 2], stat[:, 4 * k:4 * k + 2], -1.0, None, ALU.mult)\
                          .then_inc(s["lmax"], 1)
                    for k in range(4):
                        ve.wait_ge(s["prob"], 4 * i + k + 1)
                        normed(f_l(k), 4 * k + 2).then_inc(s["pn"], 1)
                    for k in range(4):
                        ve.wait_ge(s["oh"], 4 * i + k + 1)
                        at_ = bass.ds(8 + 4 * i + k, 1)
                        ve.tensor_tensor(flat(act[:, at_, T:2 * T]), bank[4 + k][:, 0:T],
                                         flat(act[:, at_, 0:T].bitcast(F32)), ALU.subtract).then_inc(s["ol"], 1)
                own.leave(F_HEADS // 4)

                ve.wait_ge(s["gate_ln"], 2)
                with ve.Fori(0, M_HEADS // 2) as i:
                    own.enter(i, 2 * 8)
                    roots.enter(i, 2)
                    for k in range(2):
                        ve.tensor_scalar(row(k), gf, vec[0:GATES, bass.ds(V_COEF + 2 * i + k, 1)], None,
                                         ALU.mult).then_inc(s["m_row"], 1)
                    for k in range(2):
                        ve.wait_ge(s["m_score"], 2 * i + k + 1)
                        ve.tensor_tensor(m_l(k), bank[4 + 2 * k][:, :].rearrange("p (b c) -> p b c", b=TB), mask,
                                         ALU.add).then_inc(s_v, own.tick())
                        mine()
                        ve.tensor_reduce(stat[:, 8 * k:8 * k + 2], m_l(k), AX_X, ALU.max).then_inc(s_v, own.tick())
                        mine()
                        ve.tensor_scalar(stat[:, 8 * k:8 * k + 2], stat[:, 8 * k:8 * k + 2], -1.0, 0.0, ALU.mult,
                                         ALU.min).then_inc(s["m_max"], 1)
                    for k in range(2):
                        ve.wait_ge(s["m_prob"], 2 * i + k + 1)
                        for tb in range(TB):
                            i_ = ve.tensor_tensor_reduce(m_l(k)[:, tb, :], m_l(k)[:, tb, :],
                                                         bank[5 + 2 * k][:, tb * T:(tb + 1) * T], 1.0, 0.0, ALU.mult,
                                                         ALU.add, stat[:, 8 * k + 2 + tb:8 * k + 3 + tb])
                        i_.then_inc(s_v, own.tick())
                        mine()
                        den = stat[:, 8 * k + 2:8 * k + 4]
                        ve.scalar_tensor_tensor(out=den, in0=den, scalar=-1.0, in1=den, op0=ALU.mult,
                                                op1=ALU.max).then_inc(s_v, own.tick())
                        mine()
                        ve.tensor_tensor(den, den, stat[:, 8 * k + 4:8 * k + 6], ALU.max).then_inc(s_v, own.tick())
                        mine()
                        normed(m_l(k), 8 * k + 2).then_inc(s["m_pn"], 1)
                    for k in range(2):
                        ve.wait_ge(s["m_ss"], 2 * i + k + 1)
                        rstd(m_q(k), bank[4 + 2 * k][:, 0:T], M_DV)
                        ve.tensor_tensor(m_l(k), bank[5 + 2 * k][:, :].rearrange("p (b c) -> p b c", b=2),
                                         m_q(k).unsqueeze(1).broadcast_to([P, 2, T]), ALU.mult)\
                          .then_inc(s_v, own.tick())
                        mine()
                        for dv in range(2):
                            j = 4 * i + 2 * k + dv
                            i_ = ve.scalar_tensor_tensor(out=m_l(k)[:, dv, :], in0=m_l(k)[:, dv, :],
                                                         scalar=vec[:, bass.ds(V_MNORM + j, 1)],
                                                         in1=region[:, bass.ds((MO + j) * T, T)],
                                                         op0=ALU.mult, op1=ALU.mult)
                        i_.then_inc(s["m_out"], 1)
                    for k in range(2):
                        ve.wait_ge(s["m_oh"], 2 * i + k + 1)
                        at_ = bass.ds(4 * i + 2 * k, 2)
                        ve.tensor_tensor(act[:, at_, T:2 * T], m_l(k), act[:, at_, 0:T].bitcast(F32),
                                         ALU.subtract).then_inc(s["m_ol"], 1)
                own.leave(M_HEADS // 2)
                roots.leave(M_HEADS // 2)

            def odd_mixer():
                ve.wait_ge(s_in["blocks"], 16)
                ve.wait_ge(s["gate_ln"], 3)
                diag = g_s[:, :, 0:P]
                with ve.Fori(0, G_HEADS) as h:
                    own.enter(h, 1 + 2 * (LEVELS - 1) + 2)
                    roots.enter(h, 1)
                    ve.wait_ge(s["z"], h + 1)
                    for dh in range(2):
                        i_ = ve.tensor_scalar(g_a[:, dh * T:(dh + 1) * T], bank[4][:, dh * T:(dh + 1) * T],
                                              vec[:, bass.ds(V_AB + 2 * h + dh, 1)], None, ALU.add)
                    i_.then_inc(s["zb"], 1)
                    ve.wait_ge(s["g_ln"], 3 * h + 3)
                    ve.scalar_tensor_tensor(out=g_a, in0=g_a, scalar=0.0, in1=g_e, op0=ALU.min,
                                            op1=ALU.subtract).then_inc(s_v, own.tick())
                    mine()
                    ve.memset(g_r, 0.0)
                    ve.tensor_scalar(g_a, g_a, 1.0 / G_TAU, None, ALU.mult).then_inc(s["decay"], 1)
                    ve.wait_ge(s["decay"], h * LEVELS + 1)
                    ve.wait_ge(s["copies_gp"], h + 1)

                    def use(lv):
                        ve.wait_ge(s["prod"], h * (LEVELS + 1) + lv + 1)
                        prod = bank[4 + lv % 2][:, 0:TB * P].rearrange("p (b c) -> p b c", b=TB)
                        if lv == LEVELS:
                            ve.tensor_scalar(g_s[:, 0, P:T], prod[:, 0, :], float(G_DK) ** -0.5, None, ALU.mult)\
                              .then_inc(s["used"], 1)
                            return
                        m = masks[:, lv * P:(lv + 1) * P].unsqueeze(1).broadcast_to([P, TB, P])
                        if lv == 0:
                            ve.tensor_tensor(diag, prod, m, ALU.mult).then_inc(s["used"], 1)
                            return
                        ve.tensor_tensor(g_tmp, prod, m, ALU.mult).then_inc(s_v, own.tick())
                        mine()
                        ve.wait_ge(s["used"], h * (LEVELS + 1) + lv)
                        ve.tensor_tensor(diag, diag, g_tmp, ALU.add).then_inc(s["used"], 1)

                    for lv in range(1, LEVELS + 1):
                        b = 1 << (lv - 1)
                        if lv > 1:
                            c = b // 2
                            tot_r = side(g_a, c, 1)[:, :, c - 1:c].broadcast_to([P, 2 * T // b, c])
                            tot_l = side(g_a, c, 0)[:, :, c - 1:c].broadcast_to([P, 2 * T // b, c])
                            ve.tensor_tensor(side(g_r, c, 0), side(g_r, c, 0), tot_r, ALU.add)\
                              .then_inc(s_v, own.tick())
                            mine()
                            ve.tensor_tensor(side(g_a, c, 1), side(g_a, c, 1), tot_l, ALU.add)\
                              .then_inc(s["decay"], 1)
                            ve.wait_ge(s["decay"], h * LEVELS + lv)
                        ve.wait_ge(s["expd"], h * LEVELS + lv)
                        if lv > 1:
                            ve.wait_ge(s["prod"], h * (LEVELS + 1) + lv - 1)
                        q_in = side(region[:, bass.ds(GQ * T + h * 2 * T, 2 * T)], b, 1)
                        k_in = side(region[:, bass.ds(GK * T + h * 2 * T, 2 * T)], b, 0)
                        ve.tensor_tensor(side(g_q(lv % 2), b, 1), q_in,
                                         g_e[:, 0:T].rearrange("p (n c) -> p n c", c=b), ALU.mult)
                        ve.tensor_tensor(side(g_k(lv % 2), b, 0), k_in,
                                         g_e[:, T:2 * T].rearrange("p (n c) -> p n c", c=b), ALU.mult)\
                          .then_inc(s["scaled"], 1)
                        use(lv - 1)
                    use(LEVELS)
                    ve.wait_ge(s["g_ss"], h + 1)
                    r_ = g_e[:, 0:T]
                    rstd(r_, bank[5][:, 0:T], G_DV)
                    for half in range(2):
                        i_ = ve.tensor_tensor(g_k2[:, 2 * half:2 * half + 2, :],
                                              bank[6 + half][:, :].rearrange("p (a t) -> p a t", a=2),
                                              r_.unsqueeze(1).broadcast_to([P, 2, T]), ALU.mult)
                    i_.then_inc(s_v, own.tick())
                    mine()
                    for dv in range(4):
                        i_ = ve.scalar_tensor_tensor(out=g_k2[:, dv, :], in0=g_k2[:, dv, :],
                                                     scalar=vec[:, bass.ds(V_GNORM + 4 * h + dv, 1)],
                                                     in1=region[:, bass.ds((GR + dv) * T + h * 4 * T, T)],
                                                     op0=ALU.mult, op1=ALU.mult)
                    i_.then_inc(s["g_out"], 1)
                    ve.wait_ge(s["g_oh"], h + 1)
                    at_ = bass.ds(4 * h, 4)
                    ve.tensor_tensor(act[:, at_, T:2 * T], g_k2, act[:, at_, 0:T].bitcast(F32),
                                     ALU.subtract).then_inc(s["g_ol"], 1)
                own.leave(G_HEADS)
                roots.leave(G_HEADS)

            ve.sem_inc(s_lo, RAW_SLOTS)
            ve.sem_inc(s_evac, 2)
            ve.wait_ge(s_cond, 1)
            for sec in range(2):
                if sec == 0:
                    open_section()
                else:
                    close_section(0)
                    open_section()
                trips = PIECES // HEAD_SLOTS
                with ve.Fori(0, trips) as i:
                    for j in range(HEAD_SLOTS):
                        ve.wait_ge(s_head[j], 16 * (i + sec * trips + 1))
                        if j >= 2:
                            ve.wait_ge(s_mac, sec * PIECES + i * HEAD_SLOTS + j - 1)
                        elif sec == 0:
                            ve.wait_ge(s_mac, i * HEAD_SLOTS)
                        else:
                            ve.wait_ge(s_mac, sec * PIECES + i * HEAD_SLOTS + j - 1)
                        summed(region[:, j * PIECE:(j + 1) * PIECE], j % 2, i * (HEAD_SLOTS // 2) + j // 2)\
                            .then_inc(s_mac, 1)
            close_section(1)
            split(0, 0, 0)

            for ph in PHASES:
                last_group = ph.group == len(FF_GROUPS) - 1
                if ph.opens and ph.kind != "mixed":
                    open_section()
                if ph.kind == "gates" or (ph.kind == "ff_up" and ph.group == 0):
                    pre_norm(ph.layer, int(ph.kind == "ff_up"))
                if ph.kind == "mixed":
                    ve.drain().then_inc(s["side"], 1)
                    (even_mixer if ph.layer == 0 else odd_mixer)()
                    open_section()

                def body(i, ph=ph):
                    k = 0

                    def sum_piece(k):
                        a = ph.a0 + i * ph.per_body + k
                        done = ph.a0 % PIECES + k
                        ve.wait_ge(s_piece[k % ADA_SLOTS],
                                   16 * ((ph.a0 - 2 * PIECES + k) // ADA_SLOTS + i * (ph.per_body // ADA_SLOTS) + 1))
                        ve.wait_ge(s_mac, a - 1)
                        summed(piece[:, k % ADA_SLOTS, :], k % 2, done // 2 + i * (ph.per_body // 2))\
                            .then_inc(s_mac, 1)

                    for j in range(ph.units):
                        split_next(ph, i, j)
                        if ph.ada[j] > 0:
                            sum_piece(k)
                        n = unit(ph, i, j)
                        tile_no = ph.t0 + (j // 4 if ph.kind == "values" else j)
                        pair_ = tile_no % 2
                        tile_ps = bank[2 * pair_][:, 0:T]
                        if ph.kind == "values":
                            if j % 4 == 3:
                                ve.wait_ge(s_unit, SPLIT_SLOTS + n + 1)
                                at_ = bass.ds(i * 1024 + (j // 4) * 512, 512)
                                for tb in range(TB):
                                    i_ = ve.tensor_copy(values[:, tb, at_], bank[2 * pair_ + tb][:, :])
                                i_.then_inc(s_evac, 1)
                        else:
                            ve.wait_ge(s_unit, SPLIT_SLOTS + n + 1)
                        if ph.kind == "gates":
                            ve.tensor_copy(gates[:, :], tile_ps[0:GATES]).then_inc(s_evac, 1)
                            ve.wait_ge(s_evac, 2 + ph.t0 + 1)
                            if ph.layer == 0:
                                ve.tensor_scalar(gates[:, :], gates[:, :], vec[0:GATES, V_GATEB:V_GATEB + 1], None,
                                                 ALU.add).then_inc(s_v, own.tick())
                                mine()
                        elif ph.kind == "columns":
                            at_ = region[:, bass.ds((4 * i + j) * T, T)]
                            ve.tensor_copy(at_, tile_ps).then_inc(s_evac, 1)
                        elif ph.kind == "mixed" or (ph.kind == "ff_down" and ph.group == 0):
                            at_ = flat(y[:, bass.ds(4 * i + j, 1), :])
                            ve.tensor_copy(at_, tile_ps).then_inc(s_evac, 1)
                        elif ph.kind == "ff_down":
                            at_ = flat(y[:, bass.ds(4 * i + j, 1), :])
                            ve.tensor_tensor(at_, at_, tile_ps, ALU.add).then_inc(s_evac, 1)
                        elif ph.kind == "ff_up":
                            slot, is_g = j // 2, j % 2
                            out_ = (conv_g if is_g else conv_a)[:, slot, :]
                            ch = V_CONV + (ph.layer * FF_TILES + 2 * sum(FF_GROUPS[:ph.group]) + j) * (CONV_W + 1)
                            ch = ch + i * ph.units * (CONV_W + 1)
                            if not is_g:
                                ve.wait_ge(s_mul, (ph.pairs + slot + 1) + 2 * i)
                            ve.tensor_scalar(out_, tile_ps, vec[:, bass.ds(ch + 2, 1)], vec[:, bass.ds(ch + 3, 1)],
                                             ALU.mult, ALU.add).then_inc(s_v, own.tick())
                            mine()
                            ve.scalar_tensor_tensor(out=out_[:, 1:T], in0=tile_ps[:, 0:T - 1],
                                                    scalar=vec[:, bass.ds(ch + 1, 1)], in1=out_[:, 1:T],
                                                    op0=ALU.mult, op1=ALU.add).then_inc(s_v, own.tick())
                            mine()
                            ve.scalar_tensor_tensor(out=out_[:, 2:T], in0=tile_ps[:, 0:T - 2],
                                                    scalar=vec[:, bass.ds(ch, 1)], in1=out_[:, 2:T],
                                                    op0=ALU.mult, op1=ALU.add).then_inc(s_evac, 1)
                        for more in range(1, ph.ada[j]):
                            sum_piece(k + more)
                        k += ph.ada[j]

                per = {"gates": 1 - ph.layer, "columns": 0, "values": 0, "mixed": 0,
                       "ff_down": 0, "ff_up": 8}[ph.kind]

                def loop_body(i, ph=ph, per=per, base=own.at):
                    own.at = base + i * per
                    body(i)
                    got = own.at
                    if isinstance(i, int):
                        assert got == base + (i + 1) * per, (ph.kind, got, base, per)
                base = own.at
                repeat(ve, ph, loop_body)
                own.at = base + per * ph.bodies
                if ph.closes:
                    close_section(ph.section)
                if ph.kind == "mixed":
                    post_norm(ph.layer, 0)
                if ph.kind == "ff_down" and last_group:
                    post_norm(ph.layer, 1)

        @block.tensor
        def _(pe):
            sqn = Tally(s_sq)
            actn = Tally(s_act, 4)

            def sum_squares(src):
                for b in range(4):
                    pe.wait_ge(s_sq, sqn.step())
                    for k in range(4):
                        i_ = pe.matmul(bank[4][:, 0:T], ones[:, 0:P], src[:, b % 2, k, :], start=(b == 0 and k == 0),
                                       stop=(b == 3 and k == 3))
                    i_.then_inc(s_sqp, 1)

            sq_y = yf[:, 0:2 * 4 * T].rearrange("p (b a t) -> p b a t", b=2, a=4)
            sq_r = region[:, V_AT:V_AT + 2 * 4 * T].rearrange("p (b a t) -> p b a t", b=2, a=4)

            def reduce_section(sec):
                if sec > 0:
                    pe.wait_ge(s_mod, sec)
                pe.wait_ge(s_mac, (sec + 1) * PIECES)
                for j in range(DK):
                    i_ = pe.matmul(bank[7][:, j:j + 1], acc[:, j * P:(j + 1) * P], ones[:, 0:1], start=True, stop=True)
                i_.then_inc(s_red, 1)

            def transposes(dst, src):
                for tb, sb_ in ((0, 0), (1, 0), (1, 1)):
                    i_ = pe.transpose(dst[:, sb_ * T + tb * P:sb_ * T + (tb + 1) * P],
                                      src[:, tb, sb_ * P:(sb_ + 1) * P], ident[:, :])
                return i_

            def even_mixer():
                pe.wait_ge(s["gate_cum"], 1)
                pe.wait_ge(s_mod, 4)
                for tb in range(TB):
                    i_ = pe.transpose(bank[7][:, tb * GATES:(tb + 1) * GATES], gf[:, tb * P:(tb + 1) * P],
                                      ident[0:GATES, 0:GATES])
                i_.then_inc(s["gate_t"], 1)
                pe.wait_ge(s["gate_col"], 1)
                with pe.Fori(0, F_HEADS // 4) as i:
                    pe.wait_ge(s["ol"], 4 * i)
                    for k in range(4):
                        pe.wait_ge(s["qst"], 4 * i + k + 1)
                        pe.wait_ge(s["row"], 4 * i + k + 1)
                        for tb in range(TB):
                            dst = bank[4 + k][:, tb * T:(tb + 1) * T]
                            pe.matmul(dst, fq_st(k)[:, tb * P:(tb + 1) * P], region[:, bass.ds((FK + k) * T + i * 4 * T, T)],
                                      start=True, stop=False)
                            i_ = pe.matmul(dst, ones[0:GATES, 0:P], row(k), start=False, stop=True)
                        i_.then_inc(s["score"], 1)
                    for k in range(4):
                        pe.wait_ge(s["pn"], 4 * i + k + 1)
                        transposes(bank[4 + k], f_l(k)).then_inc(s["pt"], 1)
                    for k in range(4):
                        pe.wait_ge(s["vst"], 4 * i + k + 1)
                        pe.wait_ge(s["pc"], 4 * i + k + 1)
                        pe.matmul(bank[4 + k][:, 0:T], fv_st(k)[:, 0, :], f_l(k)[:, 0, :], start=True, stop=False)
                        pe.matmul(bank[4 + k][:, P:T], fv_st(k)[:, 1, :], f_l(k)[:, 1, P:T], start=False, stop=True)\
                          .then_inc(s["pv"], 1)
                with pe.Fori(0, M_HEADS // 2) as i:
                    pe.wait_ge(s["ol"], F_HEADS)
                    pe.wait_ge(s["m_ol"], 2 * i)
                    for k in range(2):
                        pe.wait_ge(s["m_qst"], 2 * i + k + 1)
                        pe.wait_ge(s["m_row"], 2 * i + k + 1)
                        for tb in range(TB):
                            pe.matmul(bank[4 + 2 * k][:, tb * T:(tb + 1) * T], ones[0:GATES, 0:P], row(k),
                                      start=True, stop=True)
                            i_ = pe.matmul(bank[5 + 2 * k][:, tb * T:(tb + 1) * T], m_q(k)[:, tb * P:(tb + 1) * P],
                                           region[:, bass.ds((MK + k) * T + i * 2 * T, T)], start=True, stop=True)
                        i_.then_inc(s["m_score"], 1)
                    for k in range(2):
                        pe.wait_ge(s["m_pn"], 2 * i + k + 1)
                        transposes(bank[4 + 2 * k], m_l(k)).then_inc(s["m_pt"], 1)
                    for k in range(2):
                        pe.wait_ge(s["m_vst"], 2 * i + k + 1)
                        pe.wait_ge(s["m_pc"], 2 * i + k + 1)
                        for dv in range(2):
                            dst = bank[5 + 2 * k][:, dv * T:(dv + 1) * T]
                            pe.matmul(dst, m_v(k)[:, 0, dv * P:(dv + 1) * P], m_l(k)[:, 0, :], start=True, stop=False)
                            i_ = pe.matmul(dst[:, P:T], m_v(k)[:, 1, dv * P:(dv + 1) * P], m_l(k)[:, 1, P:T],
                                           start=False, stop=True)
                        i_.then_inc(s["m_pv"], 1)
                    for k in range(2):
                        pe.wait_ge(s["m_sq"], 2 * i + k + 1)
                        for dv in range(2):
                            i_ = pe.matmul(bank[4 + 2 * k][:, 0:T], ones[:, 0:P], m_v(k)[:, dv, :], start=dv == 0,
                                           stop=dv == 1)
                        i_.then_inc(s["m_ss"], 1)
                pe.wait_ge(s["m_ol"], M_HEADS)

            def odd_mixer():
                pe.wait_ge(s_mod, 10)
                with pe.Fori(0, G_HEADS) as h:
                    pe.wait_ge(s["g_ol"], h)
                    pe.wait_ge(s["w2"], 16 * (h + 1))
                    for dh in range(2):
                        i_ = pe.matmul(bank[4][:, dh * T:(dh + 1) * T], g_w2[:, dh * P:(dh + 1) * P], gates[:, :],
                                       start=True, stop=True)
                    i_.then_inc(s["z"], 1)
                    pe.wait_ge(s["copies"], h + 1)
                    pe.wait_ge(s["zb"], h + 1)
                    for lv in range(LEVELS + 1):
                        if lv > 0:
                            pe.wait_ge(s["scaled"], h * LEVELS + lv)
                        if lv > 1:
                            pe.wait_ge(s["used"], h * (LEVELS + 1) + lv - 1)
                        q_, k_ = g_q(lv % 2), g_k(lv % 2)
                        dst = bank[4 + lv % 2]
                        for tb in range(1 if lv == LEVELS else TB):
                            t0 = P if lv == LEVELS else tb * P
                            for dh in range(2):
                                i_ = pe.matmul(dst[:, tb * P:(tb + 1) * P], k_[:, dh * T + tb * P:dh * T + (tb + 1) * P],
                                               q_[:, dh * T + t0:dh * T + t0 + P], start=dh == 0, stop=dh == 1)
                        i_.then_inc(s["prod"], 1)
                    pe.wait_ge(s["used"], (h + 1) * (LEVELS + 1))
                    pe.wait_ge(s["g_vst"], h + 1)
                    for dv in range(4):
                        dst = bank[6 + dv // 2][:, (dv % 2) * T:(dv % 2 + 1) * T]
                        pe.matmul(dst, g_v[:, 0, dv * P:(dv + 1) * P], g_s[:, 0, :], start=True, stop=False)
                        i_ = pe.matmul(dst[:, P:T], g_v[:, 1, dv * P:(dv + 1) * P], g_s[:, 1, 0:P], start=False,
                                       stop=True)
                    i_.then_inc(s["g_pv"], 1)
                    pe.wait_ge(s["g_sq"], h + 1)
                    for dv in range(4):
                        i_ = pe.matmul(bank[5][:, 0:T], ones[:, 0:P], g_q2[:, dv, :], start=dv == 0, stop=dv == 3)
                    i_.then_inc(s["g_ss"], 1)
                pe.wait_ge(s["g_ol"], G_HEADS)

            pe.sem_inc(s_unit, SPLIT_SLOTS)
            pe.wait_ge(s_ones, 1)
            pe.wait_ge(s_in["ident"], 16)
            reduce_section(0)
            reduce_section(1)

            for ph in PHASES:
                first = ph.kind == "gates" or (ph.kind == "ff_up" and ph.group == 0)
                if first:
                    sum_squares(sq_y)
                if ph.kind == "mixed":
                    (even_mixer if ph.layer == 0 else odd_mixer)()
                if ph.kind == "ff_down":
                    pe.wait_ge(s_mid, ph.pairs)
                if first:
                    pe.wait_ge(s_act, actn.step(DK))

                def body(i, ph=ph):
                    for j in range(ph.units):
                        n = unit(ph, i, j)
                        slot = (ph.n0 + j) % SPLIT_SLOTS
                        pe.wait_ge(s_lo, RAW_SLOTS + n + 1)
                        if ph.kind == "values":
                            tile_no = ph.t0 + j // 4
                            if j % 4 == 0:
                                pe.wait_ge(s_evac, ph.t0 + i * ph.tiles + j // 4 + 1)
                            for q in range(4):
                                kt = 4 * (j % 4) + q
                                w_hi, w_lo = hi[:, slot, q * 512:(q + 1) * 512], lo[:, slot, q * 512:(q + 1) * 512]
                                for tb in range(TB):
                                    dst = bank[2 * (tile_no % 2) + tb][:, :]
                                    x_hi = act[:, kt, tb * P:(tb + 1) * P]
                                    x_lo = act[:, kt, T + tb * P:T + (tb + 1) * P]
                                    pe.matmul(dst, x_hi, w_hi, start=kt == 0, stop=False)
                                    pe.matmul(dst, x_hi, w_lo, start=False, stop=False)
                                    i_ = pe.matmul(dst, x_lo, w_hi, start=False, stop=kt == DK - 1)
                            i_.then_inc(s_unit, 1)
                            continue
                        pe.wait_ge(s_evac, ph.t0 + i * ph.tiles + j + 1)
                        dst = bank[2 * ((ph.t0 + j) % 2)][:, 0:T]
                        src = mid if ph.kind == "ff_down" else act
                        kts = FF_GROUPS[ph.group] if ph.kind == "ff_down" else DK
                        for kt in range(kts):
                            w_hi, w_lo = hi[:, slot, kt * P:(kt + 1) * P], lo[:, slot, kt * P:(kt + 1) * P]
                            pe.matmul(dst, w_hi, src[:, kt, 0:T], start=kt == 0, stop=False)
                            pe.matmul(dst, w_hi, src[:, kt, T:2 * T], start=False, stop=False)
                            i_ = pe.matmul(dst, w_lo, src[:, kt, 0:T], start=False, stop=kt == kts - 1)
                        i_.then_inc(s_unit, 1)

                repeat(pe, ph, body)
                if ph.closes:
                    reduce_section(ph.section)
                if ph.kind == "mixed" or (ph.kind == "ff_down" and ph.group == len(FF_GROUPS) - 1):
                    sum_squares(sq_r)



def columns_unit(w, cols):
    return w[:, cols].reshape(-1, P, P).transpose(1, 0, 2).reshape(P, -1)


def values_units(w):
    return w.reshape(4, 4, P, 4, 512).transpose(3, 0, 2, 1, 4).reshape(16, P, UNIT)


def per_channel(v):
    return v.reshape(-1, P).T


def kernel(x, c, ada_w, ada_b, norm_w, even_in_w, m_gate_b, m_norm_w, fox_f_b, even_out_w, odd_in_w, gla_a_w2,
           gla_a_b, gla_norm_w, odd_out_w, ffn_in_w, ffn_conv_w, ffn_conv_b, ffn_out_w):
    from concourse import bacc
    from concourse.bass_utils import run_bass_kernel_spmd

    (x, c, ada_w, ada_b, norm_w, even_in_w, m_gate_b, m_norm_w, fox_f_b, even_out_w, odd_in_w, gla_a_w2, gla_a_b,
     gla_norm_w, odd_out_w, ffn_in_w, ffn_conv_w, ffn_conv_b, ffn_out_w) = (
        np.asarray(v) for v in (x, c, ada_w, ada_b, norm_w, even_in_w, m_gate_b, m_norm_w, fox_f_b, even_out_w,
                                odd_in_w, gla_a_w2, gla_a_b, gla_norm_w, odd_out_w, ffn_in_w, ffn_conv_w,
                                ffn_conv_b, ffn_out_w))
    mv, fv = slice(1024, 2048), slice(5128, 6152)
    even_cols = [0, 512, 2048, 3080, 4104]
    even_width = [512, 512, 1024, 1024, 1024]
    odd_cols, odd_width = [0, 1024, 4096], [1024, 1024, 2048]
    even, odd = even_in_w[0], odd_in_w[0]
    units = np.zeros((UNITS, P, UNIT), np.float32)
    n = 0
    for layer in range(LAYERS):
        w = (even, odd)[layer]
        if layer == 0:
            gate_cols = [w[:, 3072:3080], w[:, 6152:6160]]
            cols, widths, val = even_cols, even_width, np.concatenate([w[:, mv], w[:, fv]], axis=1)
        else:
            gate_cols = [w[:, 6144:6160]]
            cols, widths, val = odd_cols, odd_width, w[:, 2048:4096]
        units[n].reshape(P, DK, P)[:, :, 0:GATES] = \
            np.concatenate(gate_cols, axis=1).reshape(DK, P, GATES).transpose(1, 0, 2)
        n += 1
        for first, width in zip(cols, widths):
            for k in range(first, first + width, P):
                units[n] = columns_unit(w, slice(k, k + P))
                n += 1
        units[n:n + 16] = values_units(np.ascontiguousarray(val))
        n += 16
        w = (even_out_w, odd_out_w)[layer][0]
        for m in range(DK):
            units[n] = columns_unit(w, slice(m * P, (m + 1) * P))
            n += 1
        first = 0
        for tiles in FF_GROUPS:
            for k in range(first, first + tiles):
                for part in range(2):
                    at = part * D_FF + k * P
                    units[n] = columns_unit(ffn_in_w[layer], slice(at, at + P))
                    n += 1
            rows = ffn_out_w[layer][first * P:(first + tiles) * P]
            for m in range(DK):
                units[n][:, 0:tiles * P] = columns_unit(rows, slice(m * P, (m + 1) * P))
                n += 1
            first += tiles
    assert n == UNITS

    ada = ada_w.reshape(LAYERS, DK, P, 6, 2, PIECE).transpose(0, 3, 1, 4, 2, 5).reshape(-1, P, PIECE)
    conv = np.concatenate([ffn_conv_w.reshape(LAYERS, CONV_W, 2, D_FF // P, P),
                           ffn_conv_b.reshape(LAYERS, 1, 2, D_FF // P, P)], axis=1)
    conv = conv.transpose(4, 0, 3, 2, 1).reshape(P, -1)
    vec = np.zeros((P, V_END), np.float32)
    vec[:, V_C:V_ADAB] = per_channel(c)
    vec[:, V_ADAB:V_NORM] = per_channel(ada_b)
    vec[:, V_NORM:V_MNORM] = per_channel(norm_w)
    vec[:, V_MNORM:V_GNORM] = per_channel(m_norm_w)
    vec[:, V_GNORM:V_AB] = per_channel(gla_norm_w)
    vec[:, V_AB:V_GATEB] = per_channel(gla_a_b)
    vec[0:GATES, V_GATEB] = np.concatenate([m_gate_b[0], fox_f_b[0]])
    for h in range(M_HEADS):
        vec[h, V_COEF + h] = 1.0
        vec[M_HEADS + h, V_COEF + h] = -1.0
    for h in range(F_HEADS):
        vec[2 * M_HEADS + h, V_COEF + M_HEADS + h] = -1.0
    vec[:, V_CONV:V_END] = conv

    tok = np.arange(T)
    causal = np.zeros((P, TB, T), np.float32)
    for tb in range(TB):
        causal[:, tb][tok[None, :] > (tok[tb * P:(tb + 1) * P])[:, None]] = NEG
    blocks = np.zeros((P, LEVELS, P), np.float32)
    a, b = np.arange(P)[:, None], np.arange(P)[None, :]
    blocks[:, 0][a == b] = float(G_DK) ** -0.5
    for lv in range(1, LEVELS):
        size = 1 << (lv - 1)
        blocks[:, lv][(a // size % 2 == 0) & (b // size == a // size + 1)] = float(G_DK) ** -0.5
    w2 = gla_a_w2[0].reshape(G_RANK, G_HEADS, G_DK).transpose(1, 0, 2)

    arrays = {
        "w_units": units,
        "ada_pieces": np.ascontiguousarray(ada),
        "vectors": vec,
        "x_in": np.ascontiguousarray(x[0].T.reshape(DK, P, T).transpose(1, 0, 2)),
        "identity": np.eye(P, dtype=np.float32),
        "causal": causal.reshape(P, -1),
        "blocks": blocks.reshape(P, -1),
        "a_w2": np.ascontiguousarray(w2),
    }
    nc = bacc.Bacc("TRN2", target_bir_lowering=False, num_devices=1)
    aps = [nc.dram_tensor(k, v.shape, F32, kind="ExternalInput").ap() for k, v in arrays.items()]
    out = nc.dram_tensor("x_out", (P, DK, T), F32, kind="ExternalOutput").ap()
    program(nc, *aps, out)
    got = run_bass_kernel_spmd(nc, [arrays], core_ids=[0]).results[0]["x_out"]
    return np.ascontiguousarray(got.transpose(1, 0, 2).reshape(1, D, T).transpose(0, 2, 1))
```

```python
from contextlib import ExitStack

import numpy as np

import concourse.bass as bass
from concourse import mybir

F32 = mybir.dt.float32
F32R = mybir.dt.float32r
U8 = mybir.dt.uint8
ALU = mybir.AluOpType
ACT = mybir.ActivationFunctionType
AX_X = mybir.AxisListType.X

P = 128
T = 256
TB = T // P
D = 2048
DK = D // P
EPS = 1e-6
LAYERS = 2

M_HEADS, M_DQK, M_DV = 4, 128, 256
F_HEADS, F_DH = 8, 128
G_HEADS, G_DK, G_DV, G_RANK, G_TAU = 4, 256, 512, 16, 16.0
D_FF = 5632
CONV_W = 3
GATES = 16

UNIT = DK * P
RAW_SLOTS, SPLIT_SLOTS = 4, 2
PIECE = 1024
PIECES = D // P * (D // PIECE)
SECTIONS = 6 * LAYERS
ADA_SLOTS = 2
HEAD_SLOTS = 8
FF_GROUPS = (16, 16, 12)

LEVELS = 8
NEG = -1e30


class Phase:

    def __init__(self, kind, layer, bodies, units, ada, group=0, dest=0, side=None, side0=0):
        self.kind, self.layer, self.bodies, self.units, self.ada = kind, layer, bodies, units, ada
        self.group, self.dest, self.side, self.side0 = group, dest, side, side0
        self.per_body = sum(ada)
        self.tiles = units // 4 if kind == "values" else units
        self.sums = kind == "mixed" or (kind == "ff_down" and group == len(FF_GROUPS) - 1)
        self.norms = kind == "gates" or (kind == "ff_up" and group == 0)
        self.peel = self.head = 0

    def place(self, n, t, a, pairs):
        self.n0, self.t0, self.a0, self.pairs = n, t, a, pairs
        self.end = n + self.bodies * self.units
        self.a_end = a + self.bodies * self.per_body
        self.closes = self.per_body > 0 and self.a_end % PIECES == 0
        return self.end, t + self.bodies * self.tiles, self.a_end, pairs + (2 * self.bodies if self.kind == "ff_up" else 0)


    def straight(self, i):
        first = self.a0 + i * self.per_body
        return (i < self.head or i >= self.bodies - self.peel
                or any(a % PIECES in (0, PIECES - 1) for a in range(first, first + self.per_body)))


MQ, MK, MO, FQ, FK = 0, 4, 8, 16, 24
GQ, GK, GR = 0, 8, 16


def plan():
    no = (0,) * 4
    phases = [Phase("gates", 0, 1, 1, (0,)),
              Phase("columns", 0, 4, 4, (2, 1, 2, 1), dest=FQ),
              Phase("values", 0, 1, 8, (1,) * 8, dest=M_HEADS * M_DV),
              Phase("columns", 0, 2, 4, (2, 1, 2, 1), dest=MQ, side="fox"),
              Phase("values", 0, 1, 8, (2, 1) * 4, side="fox", side0=2),
              Phase("columns", 0, 2, 4, (1,) * 4, dest=MO, side="mlstm"),
              Phase("mixed", 0, 4, 4, (2,) * 4),
              Phase("ff_up", 0, 8, 4, (1,) * 4, 0), Phase("ff_down", 0, 4, 4, (2, 1, 2, 1), 0),
              Phase("ff_up", 0, 8, 4, (1,) * 4, 1), Phase("ff_down", 0, 4, 4, (2, 1, 2, 1), 1),
              Phase("ff_up", 0, 6, 4, (1,) * 4, 2), Phase("ff_down", 0, 4, 4, (1, 0, 1, 0), 2),
              Phase("gates", 1, 1, 1, (0,)),
              Phase("columns", 1, 4, 4, (2, 1, 2, 1), dest=GQ, side="decay"),
              Phase("values", 1, 2, 8, (0,) * 8, side="gla"),
              Phase("columns", 1, 2, 8, (0,) * 8, dest=GR, side="gla", side0=2),
              Phase("mixed", 1, 4, 4, (2, 1, 2, 1)),
              Phase("ff_up", 1, 8, 4, (1,) * 4, 0), Phase("ff_down", 1, 4, 4, no, 0),
              Phase("ff_up", 1, 8, 4, no, 1), Phase("ff_down", 1, 4, 4, no, 1),
              Phase("ff_up", 1, 6, 4, no, 2), Phase("ff_down", 1, 4, 4, no, 2)]
    state = (0, 0, 2 * PIECES, 0)
    for ph in phases:
        state = ph.place(*state)
        ph.head = 1 if (ph.side == "gla" and ph.side0 == 0) or ph.sums or ph.norms or ph.kind == "ff_up" else 0
    assert state[2] == SECTIONS * PIECES
    phases[-1].peel = 2
    return phases, state[0]


PHASES, UNITS = plan()
MIXED = [ph for ph in PHASES if ph.kind == "mixed"]
PAUSE = next(ph for ph in PHASES if ph.side == "gla").a0

V_C, V_ADAB = 0, DK
V_NORM = V_ADAB + SECTIONS * DK
V_MNORM = V_NORM + LAYERS * 4 * DK
V_GNORM = V_MNORM + M_HEADS * M_DV // P
V_AB = V_GNORM + G_HEADS * G_DV // P
V_GATEB = V_AB + G_HEADS * G_DK // P
V_COEF = V_GATEB + 1
V_CONV = V_COEF + M_HEADS + F_HEADS
FF_TILES = 2 * D_FF // P
V_END = V_CONV + LAYERS * FF_TILES * (CONV_W + 1)

V_AT = 32 * T
REGION = V_AT + TB * D
OWN = {("ff_up", None): 8, ("columns", "fox"): 6, ("values", "fox"): 12, ("columns", "mlstm"): 14,
       ("values", "gla"): 8, ("columns", "gla"): 8}


class Tally:

    def __init__(self, sem, start=0):
        self.sem, self.base, self.at, self.extra = sem, start, start, 0

    def tick(self, k=1):
        self.at = self.at + k
        self.extra += k
        return k

    def step(self, k=1):
        self.tick(k)
        return self.at

    def enter(self, i, per):
        self.base, self.per, self.extra = self.at, per, 0
        self.at = self.at + i * per

    def leave(self, trips):
        assert self.extra == self.per, (self.extra, self.per)
        self.at = self.base + trips * self.per


def repeat(eng, ph, body):
    at = 0
    while at < ph.bodies:
        stop = at
        while stop < ph.bodies and not ph.straight(stop):
            stop += 1
        ph.now = at
        if stop - at > 1:
            with eng.Fori(at, stop) as i:
                body(i)
            at = stop
        else:
            body(at)
            at += 1


def first_body(i):
    return isinstance(i, int) and i == 0


def program(nc, w_dram, ada_dram, vec_dram, x_dram, ident_dram, causal_dram, blocks_dram, w2_dram, out_dram):
    with ExitStack() as ctx:
        def sb(name, shape, dt=F32):
            return ctx.enter_context(nc.sbuf_tensor(name, shape, dt))

        def sem(name):
            return ctx.enter_context(nc.semaphore(name))

        def flat(ap):
            return ap.rearrange("p a t -> p (a t)")

        def split2(ap, b=TB):
            return ap.rearrange("p (b c) -> p b c", b=b)

        region_at = -(-nc.sbuf_base // 32) * 32
        region = sb("region", [P, REGION])
        mid = nc.alloc_sbuf_tensor_at("mid", [P, 16, 2 * T], F32R, offset=region_at)
        x = sb("x", [P, DK, T])
        y = sb("y", [P, DK, T])
        act = sb("act", [P, DK, 2 * T], F32R)
        raw = sb("raw", [P, RAW_SLOTS, UNIT])
        hi = sb("hi", [P, SPLIT_SLOTS, UNIT], F32R)
        lo = sb("lo", [P, SPLIT_SLOTS, UNIT], F32R)
        piece = sb("piece", [P, ADA_SLOTS, PIECE])
        acc = sb("acc", [P, D])
        vec = sb("vec", [P, V_END])
        mod = sb("mod", [P, SECTIONS, DK])
        cond = sb("cond", [P, DK])
        alpha = sb("alpha", [P, DK])
        gamma = sb("gamma", [P, DK])
        ident = sb("ident", [P, P])
        ones = sb("ones", [P, T])
        causal = sb("causal", [P, TB, T])
        blocks = sb("blocks", [P, LEVELS, P], U8)
        gates = sb("gates", [GATES, T])
        extra = sb("extra", [P, 4 * T])
        stat = sb("stat", [P, 64])

        yf = flat(y[:, :, :])
        values = split2(region[:, V_AT:REGION])
        conv_a, conv_g, gelu_g, ff_m = (split2(region[:, V_AT + k * 2 * T:V_AT + (k + 1) * 2 * T], 2)
                                        for k in range(4))
        y_sq = split2(region[:, V_AT:V_AT + 2 * T], 2)
        y_rstd = region[:, V_AT + 2 * T:V_AT + 3 * T]
        x_rstd = region[:, V_AT + 3 * T:V_AT + 4 * T]
        x_sq = region[:, V_AT + 4 * T:V_AT + 12 * T].rearrange("p (b a t) -> p b a t", b=2, a=4)

        gate_t1 = region[0:GATES, MO * T:(MO + 1) * T]
        gate_t2 = region[0:GATES, (MO + 1) * T:(MO + 2) * T]
        gate_rows = extra[0:GATES, 0:T]

        def row(k):
            return extra[0:GATES, (1 + k) * T:(2 + k) * T]

        def fox_part(k, a, b):
            return region[:, (MO + 4 * k + a) * T:(MO + 4 * k + b) * T]

        def fox_q(k):
            return fox_part(k, 0, 1)

        def fox_v(k):
            return split2(fox_part(k, 1, 2))

        def fox_l(k):
            return split2(fox_part(k, 2, 4))

        def m_part(k, a, b):
            return region[:, (FQ + 5 * k + a) * T:(FQ + 5 * k + b) * T]

        def m_q(k):
            return m_part(k, 0, 1)

        def m_v(k):
            return split2(m_part(k, 1, 3))

        def m_l(k):
            return split2(m_part(k, 3, 5))

        pf = flat(piece[:, :, :])
        g_q, g_k, g_a, g_r = (pf[:, k * 2 * T:(k + 1) * 2 * T] for k in range(4))
        g_e = extra[:, 0:2 * T]
        g_s = split2(extra[:, 2 * T:4 * T])
        g_w2 = extra[0:G_RANK, :]
        g_abs = yf[:, 0:2 * T]
        g_rstd = causal[:, 0, :]
        g_v = split2(yf[:, 12 * T:16 * T])
        g_sq = yf[:, 12 * T:16 * T].rearrange("p (a t) -> p a t", a=4)

        def g_decay(h):
            return region[:, bass.ds((GR + 8 + 2 * h) * T, 2 * T)]

        def halves(ap, b, right):
            return ap.rearrange("p (n two c) -> p n two c", two=2, c=b)[:, :, right, :]

        bank = [ctx.enter_context(nc.psum_tensor(f"bank{k}", [P, 512], F32)) for k in range(8)]

        s_raw = [sem(f"raw_ready{j}") for j in range(RAW_SLOTS)]
        s_hi = sem("hi_ready")
        s_lo = sem("lo_ready")
        s_unit = sem("unit_done")
        s_evac = sem("tile_evacuated")
        s_piece = [sem(f"piece_ready{j}") for j in range(ADA_SLOTS)]
        s_head = [sem(f"head_piece_ready{j}") for j in range(HEAD_SLOTS)]
        s_mac = sem("piece_summed")
        s_red = sem("section_reduced")
        s_mod = sem("section_stored")
        s_in = {k: sem(f"loaded_{k}") for k in ("vec", "x", "ident", "causal", "blocks")}
        s_cond = sem("cond_ready")
        s_ones = sem("ones_ready")
        s_v = sem("vector_step")
        s_mean = sem("mean_square_ready")
        s_root = sem("root_ready")
        s_sq = sem("x_squares_ready")
        s_sqp = sem("x_squares_summed")
        s_ysq = sem("y_squares_ready")
        s_ysqp = sem("y_squares_summed")
        s_h = sem("normed_ready")
        s_hh = sem("act_hi_ready")
        s_act = [sem("act_ready"), sem("act_ready_pool")]
        s_gamma = sem("gamma_ready")
        s_alpha = sem("alpha_ready")
        s_ys = sem("y_scaled")
        s_xs = sem("x_scaled")
        s_x = sem("x_updated")
        s_gelu = sem("gelu_ready")
        s_mul = sem("ff_product_ready")
        s_mh = sem("mid_hi_ready")
        s_mid = sem("mid_ready")
        s_store = sem("stored")
        names = ("masks", "pool_h", "gate_abs", "gate_ln", "gate_cum", "gate_t", "gate_col",
                 "qst", "vst", "row", "score", "lmax", "prob", "pn", "pt", "pc", "pv", "fy",
                 "m_qst", "m_vst", "m_row", "m_score", "m_max", "m_prob", "m_pn", "m_pt", "m_pc", "m_pv",
                 "m_sq", "m_ss", "m_y",
                 "w2", "g_vst", "z", "g_ln", "decays", "copies", "decay", "expd", "scaled", "prod", "used",
                 "g_pv", "g_sq", "g_ss", "g_mean", "g_root", "g_rstd", "g_y", "t_gate", "t_mul", "t_hi", "t_lo")
        s = {k: sem(k) for k in names}

        block = ctx.enter_context(nc.Block())

        def unit(ph, i, j):
            return ph.n0 + i * ph.units + j

        def evacuated(ph, i, j):
            return 2 + ph.t0 + i * ph.tiles + j + 1

        def fox_pair(ph, i, j):
            return ph.side0 + (i if ph.units == 4 else j // 4), j % 4

        def tail(ph):
            return ((2, 3, 0, 1), (0, 1), MO, ACT.Sigmoid) if ph.layer == 0 else \
                ((0, 1, 2, 3), (0, 1, 2, 3), GR, ACT.Silu)

        @block.sync
        def _(sp):
            sp.dma_start(vec[:, :], vec_dram).then_inc(s_in["vec"], 16)

            def head_load(i, j):
                src = ada_dram[bass.ds(i * HEAD_SLOTS + j, 1)].rearrange("a p n -> p (a n)")
                sp.dma_start(region[:, j * PIECE:(j + 1) * PIECE], src).then_inc(s_head[j], 16)

            for j in range(HEAD_SLOTS):
                head_load(0, j)
            sp.dma_start(x[:, :, :], x_dram).then_inc(s_in["x"], 16)
            sp.dma_start(ident[:, :], ident_dram).then_inc(s_in["ident"], 16)
            with sp.Fori(1, 2 * PIECES // HEAD_SLOTS) as i:
                for j in range(HEAD_SLOTS):
                    sp.wait_ge(s_mac, (i - 1) * HEAD_SLOTS + j + 1)
                    head_load(i, j)

            def load_unit(n, slot):
                src = w_dram[bass.ds(n, 1)].rearrange("a p n -> p (a n)")
                sp.dma_start(raw[:, slot, :], src).then_inc(s_raw[slot], 16)

            def load_piece(a, slot):
                src = ada_dram[bass.ds(a, 1)].rearrange("a p n -> p (a n)")
                sp.dma_start(piece[:, slot, :], src).then_inc(s_piece[slot], 16)

            for n in range(RAW_SLOTS):
                load_unit(n, n)
            for a in range(ADA_SLOTS):
                load_piece(2 * PIECES + a, a)
            sp.dma_start(causal[:, :, :], causal_dram).then_inc(s_in["causal"], 16)
            sp.dma_start(extra[:, :], blocks_dram).then_inc(s_in["blocks"], 16)
            sp.wait_ge(s_lo, RAW_SLOTS + 1)
            load_unit(RAW_SLOTS, 0)

            for ph in PHASES:
                def body(i, ph=ph):
                    k = 0
                    for j in range(ph.units):
                        n = unit(ph, i, j)
                        if not isinstance(n, int) or n + RAW_SLOTS + 1 < UNITS:
                            sp.wait_ge(s_lo, RAW_SLOTS + n + 2)
                            load_unit(n + RAW_SLOTS + 1, (ph.n0 + j + 1) % RAW_SLOTS)
                        for _ in range(ph.ada[j]):
                            a = ph.a0 + i * ph.per_body + k
                            if not isinstance(a, int) or not (a + ADA_SLOTS >= SECTIONS * PIECES
                                                              or PAUSE <= a + ADA_SLOTS < PAUSE + ADA_SLOTS):
                                sp.wait_ge(s_mac, a + 1)
                                load_piece(a + ADA_SLOTS, k % ADA_SLOTS)
                            k += 1

                if ph.kind == "gates" and ph.layer == 1:
                    sp.wait_ge(s["m_y"], 2 + M_HEADS)
                    sp.dma_start(g_w2, w2_dram).then_inc(s["w2"], 16)
                if ph.a0 == PAUSE and ph.kind == "mixed":
                    sp.wait_ge(s["g_y"], G_HEADS)
                    for k in range(ADA_SLOTS):
                        load_piece(PAUSE + k, k)
                straight = ph.per_body > 0 and ph.a_end in (PAUSE, SECTIONS * PIECES)
                kept, ph.peel = ph.peel, max(ph.peel, int(straight))
                repeat(sp, ph, body)
                ph.peel = kept

            for c in range(4):
                sp.wait_ge(s_x, 8 * LAYERS - 3 + c)
                sp.dma_start(out_dram[:, 4 * c:4 * c + 4, :], x[:, 4 * c:4 * c + 4, :]).then_inc(s_store, 16)
            sp.wait_ge(s_store, 4 * 16)

        @block.scalar
        def _(sc):
            def split(n, slot, raw_slot, uses):
                sc.wait_ge(s_raw[raw_slot], 16 * uses)
                sc.wait_ge(s_unit, n + 1)
                sc.activation(hi[:, slot, :], raw[:, raw_slot, :], ACT.Copy).then_inc(s_hi, 1)

            def split_next(ph, i, j):
                m = ph.n0 + j + 1
                if isinstance(i, int) and unit(ph, i, j) + 1 >= UNITS:
                    return
                split(unit(ph, i, j) + 1, m % SPLIT_SLOTS, m % RAW_SLOTS,
                      m // RAW_SLOTS + i * (ph.units // RAW_SLOTS) + 1)

            sqp = Tally(s_sqp)
            ysq = Tally(s_ysq)
            xup = Tally(s_x)
            means = Tally(s_mean)

            def root(at_, scale=1.0):
                sc.wait_ge(s_mean, means.step())
                sc.activation(at_, at_, ACT.Sqrt, scale=scale).then_inc(s_root, 1)

            def by_weight(c):
                for k in range(4 * c, 4 * c + 4):
                    i_ = sc.activation(y[:, k, :], x[:, k, :], ACT.Copy, scale=alpha[:, k:k + 1])
                i_.then_inc(s_xs, 1)

            def pre_norm(layer, part):
                for b in range(4):
                    if xup.at == 0:
                        sc.wait_ge(s_in["x"], 16)
                    else:
                        sc.wait_ge(s_x, xup.at - 4 + b + 1)
                    if sqp.at + b >= 2:
                        sc.wait_ge(s_sqp, sqp.at + b - 1)
                    sc.activation(x_sq[:, b % 2], x[:, 4 * b:4 * b + 4, :], ACT.Square).then_inc(s_sq, 1)
                    if b == 0:
                        sc.wait_ge(s_alpha, sqp.at // 4 + 1)
                    if b < 2:
                        by_weight(b)
                by_weight(2)
                root(x_rstd)
                by_weight(3)
                sh = 6 * layer + 3 * part
                for c in range(4):
                    sc.wait_ge(s_h, sqp.at + c + 1)
                    for k in range(4 * c, 4 * c + 4):
                        sc.activation(act[:, k, 0:T], y[:, k, :], ACT.Identity, bias=mod[:, sh, k:k + 1])\
                          .then_inc(s_hh, 1)
                sqp.tick(4)

            def square_tile(ph, q, slot):
                sc.wait_ge(s_evac, 2 + ph.t0 + q + 1)
                if not isinstance(q, int) or ysq.at + q >= 2:
                    sc.wait_ge(s_ysqp, ysq.at + q - 1)
                tile_ = flat(y[:, bass.ds(q, 1), :])
                sc.activation(y_sq[:, slot, :], tile_, ACT.Square).then_inc(s_ysq, 1)
                sc.activation(tile_, tile_, ACT.Copy, scale=gamma[:, bass.ds(q, 1)]).then_inc(s_ys, 1)

            def gate_ln():
                sc.wait_ge(s_evac, 2 + 1)
                sc.activation(gate_t1, gates[:, :], ACT.Abs).then_inc(s["gate_abs"], 1)
                sc.wait_ge(s["gate_abs"], 1)
                sc.activation(gate_t1, gate_t1, ACT.Exp, scale=-1.0).then_inc(s["gate_abs"], 1)
                sc.wait_ge(s["gate_abs"], 2)
                sc.activation(gate_t1, gate_t1, ACT.Ln, bias=1.0).then_inc(s["gate_ln"], 1)

            def u_tile(k):
                return region[:, bass.ds(k * T, T)]

            def column(c):
                return stat[:, c:c + 1]

            def before_split(ph, i, j):
                if ph.side == "fox":
                    pair, r = fox_pair(ph, i, j)
                    if r == 0:
                        sc.wait_ge(s["gate_col"], 1)
                        for k in range(2):
                            sc.activation(fox_q(k), u_tile(FQ + 2 * pair + k), ACT.Copy,
                                          scale=float(F_DH) ** -0.5).then_inc(s["qst"], 1)
                if ph.side == "mlstm" and j == 0:
                    sc.wait_ge(s["fy"], 2 + F_HEADS)
                    sc.wait_ge(s["m_y"], 2 * (i + 1))
                    for k in range(2):
                        sc.activation(m_q(k), u_tile(MQ + 2 * i + k), ACT.Copy,
                                      scale=float(M_DQK) ** -0.5).then_inc(s["m_qst"], 1)
                if ph.side == "gla" and j == 0:
                    h = ph.side0 + i
                    if first_body(h):
                        sc.wait_ge(s_mac, PAUSE)
                    else:
                        sc.wait_ge(s["prod"], h * (LEVELS + 1))
                        sc.wait_ge(s["expd"], h * LEVELS)
                    sc.activation(g_q, region[:, bass.ds(GQ * T + h * 2 * T, 2 * T)], ACT.Copy)
                    sc.activation(g_k, region[:, bass.ds(GK * T + h * 2 * T, 2 * T)], ACT.Copy)
                    sc.wait_ge(s["decays"], G_HEADS)
                    sc.activation(g_a, g_decay(h), ACT.Copy).then_inc(s["copies"], 1)

            def exps(h, lv):
                sc.wait_ge(s["decay"], h * LEVELS + lv)
                if lv == 1:
                    sc.wait_ge(s["copies"], h + 1)
                if lv > 1 or not first_body(h):
                    sc.wait_ge(s["scaled"], h * LEVELS + lv - 1)
                b = 1 << (lv - 1)
                sc.activation(g_e[:, 0:T].rearrange("p (n c) -> p n c", c=b), halves(g_a, b, 1), ACT.Exp,
                              scale=1.0 / G_TAU)
                sc.activation(g_e[:, T:2 * T].rearrange("p (n c) -> p n c", c=b), halves(g_r, b, 0), ACT.Exp,
                              scale=1.0 / G_TAU).then_inc(s["expd"], 1)

            def after_split(ph, i, j):
                if ph.side == "fox":
                    pair, r = fox_pair(ph, i, j)
                    for k in range(2):
                        done = 2 * pair + k + 1
                        if r == 1:
                            sc.wait_ge(s["lmax"], done)
                            for tb in range(TB):
                                i_ = sc.activation(fox_l(k)[:, tb, :], fox_l(k)[:, tb, :], ACT.Exp,
                                                   bias=column(4 * k + tb), accum_out=column(4 * k + 2 + tb))
                            i_.then_inc(s["prob"], 1)
                        if r == 3:
                            sc.wait_ge(s["pt"], done)
                            sc.activation(fox_l(k)[:, 0, :], bank[4 + k][:, 0:T], ACT.Copy)
                            sc.activation(fox_l(k)[:, 1, P:T], bank[4 + k][:, T + P:2 * T], ACT.Copy)\
                              .then_inc(s["pc"], 1)
                if ph.side == "mlstm":
                    for k in range(2):
                        done = 2 * i + k + 1
                        if j == 1:
                            sc.wait_ge(s["m_max"], done)
                            for tb in range(TB):
                                sc.activation(column(8 * k + 4 + tb),
                                              stat[:, bass.ds(32 + tb * GATES + M_HEADS + 2 * i + k, 1)], ACT.Exp,
                                              bias=column(8 * k + tb), scale=-1.0)
                            for tb in range(TB):
                                i_ = sc.activation(m_l(k)[:, tb, :], m_l(k)[:, tb, :], ACT.Exp,
                                                   bias=column(8 * k + tb))
                            i_.then_inc(s["m_prob"], 1)
                        if j == 2:
                            sc.wait_ge(s["m_pt"], done)
                            sc.activation(m_l(k)[:, 0, :], bank[4 + 2 * k][:, 0:T], ACT.Copy)
                            sc.activation(m_l(k)[:, 1, P:T], bank[4 + 2 * k][:, T + P:2 * T], ACT.Copy)\
                              .then_inc(s["m_pc"], 1)
                        if j == 3:
                            sc.wait_ge(s["m_pv"], done)
                            sc.activation(m_v(k), split2(bank[5 + 2 * k][:, :]), ACT.Square).then_inc(s["m_sq"], 1)
                    if j == 3:
                        means.enter(i, 2)
                        for k in range(2):
                            root(m_q(k))
                        means.leave(0)
                if ph.side == "decay":
                    if j == 1:
                        if not first_body(i):
                            sc.wait_ge(s["decays"], i)
                        sc.wait_ge(s["z"], i + 1)
                        for dh in range(2):
                            z_ps, bias = bank[4][:, dh * T:(dh + 1) * T], vec[:, bass.ds(V_AB + 2 * i + dh, 1)]
                            sc.activation(region[:, bass.ds((GR + 8 + 2 * i + dh) * T, T)], z_ps, ACT.Identity,
                                          bias=bias)
                            i_ = sc.activation(g_abs[:, dh * T:(dh + 1) * T], z_ps, ACT.Abs, bias=bias)
                        i_.then_inc(s["g_ln"], 1)
                    if j == 2:
                        sc.wait_ge(s["g_ln"], 3 * i + 1)
                        sc.activation(g_abs, g_abs, ACT.Exp, scale=-1.0).then_inc(s["g_ln"], 1)
                    if j == 3:
                        sc.wait_ge(s["g_ln"], 3 * i + 2)
                        sc.activation(g_abs, g_abs, ACT.Ln, bias=1.0).then_inc(s["g_ln"], 1)
                if ph.side == "gla":
                    h = ph.side0 + i
                    if j == 0:
                        exps(h, 1)
                    if j < 7:
                        exps(h, j + 2)
                    if j == 0 and not first_body(h):
                        gla_squares(h)
                    if j == 1 and not first_body(h):
                        gla_root(h)

            def gla_squares(heads):
                sc.wait_ge(s["g_pv"], heads)
                for half in range(2):
                    i_ = sc.activation(g_sq[:, 2 * half:2 * half + 2, :], split2(bank[6 + half][:, :]), ACT.Square)
                i_.then_inc(s["g_sq"], 1)

            def gla_root(heads):
                sc.wait_ge(s["g_mean"], heads)
                sc.activation(g_rstd, g_rstd, ACT.Sqrt, scale=float(G_DK)).then_inc(s["g_root"], 1)

            def gate_tail(ph):
                order, gated, gate0, func = tail(ph)
                sc.wait_ge(s_evac, 2 + ph.t0)
                base = 4 * ph.layer

                def to_act(at_, c):
                    sc.activation(act[:, 4 * c:4 * c + 4, 0:T], y[:, 4 * c:4 * c + 4, :], ACT.Copy)\
                      .then_inc(s["t_hi"], 1)

                gates0 = 2 * ph.layer
                if ph.layer == 0:
                    sc.wait_ge(s["fy"], 2 + F_HEADS)
                    to_act(0, 2)
                    to_act(1, 3)
                else:
                    sc.wait_ge(s["g_y"], G_HEADS)
                for c in gated:
                    at_ = region[:, (gate0 + 4 * c) * T:(gate0 + 4 * c + 4) * T]
                    sc.activation(at_, at_, func).then_inc(s["t_gate"], 1)
                for k, c in enumerate(gated):
                    sc.wait_ge(s["t_mul"], gates0 + k + 1)
                    to_act(0, c)

            sc.wait_ge(s_in["vec"], 16)
            sc.activation(cond[:, :], vec[:, V_C:V_C + DK], ACT.Silu).then_inc(s_cond, 1)
            split(0, 0, 0, 1)

            def gelu(ph, q, slot):
                sc.wait_ge(s_evac, 2 + ph.t0 + 2 * q + 2)
                sc.wait_ge(s_mul, ph.pairs + q + 1)
                sc.activation(gelu_g[:, slot, :], conv_g[:, slot, :], ACT.Gelu_apprx_tanh).then_inc(s_gelu, 1)

            def to_mid(ph, q, slot):
                sc.wait_ge(s_mul, ph.pairs + q + 3)
                sc.activation(flat(mid[:, bass.ds(q, 1), 0:T]), ff_m[:, slot, :], ACT.Copy).then_inc(s_mh, 1)

            for ph in PHASES:
                if ph.norms:
                    split_next(ph, 0, 0)
                    pre_norm(ph.layer, int(ph.kind == "ff_up"))
                if ph.kind == "values" and ph.layer == 0 and ph.side is None:
                    gate_ln()
                if ph.kind == "mixed" and ph.layer == 1:
                    gla_squares(G_HEADS)
                    gla_root(G_HEADS)
                if ph.kind == "mixed":
                    gate_tail(ph)

                def body(i, ph=ph):
                    for j in range(ph.units):
                        before_split(ph, i, j)
                        if not (ph.norms and first_body(i) and j == 0):
                            split_next(ph, i, j)
                        after_split(ph, i, j)
                        if ph.kind == "ff_up" and not (first_body(i) and j < 2):
                            q = 2 * i + (j // 2 - 1)
                            (gelu if j % 2 == 0 else to_mid)(ph, q, (j // 2 + 1) % 2)
                        if ph.sums and not (first_body(i) and j == 0):
                            square_tile(ph, ph.units * i + j - 1, (j + 1) % 2)

                if ph.sums:
                    sc.wait_ge(s_gamma, ysq.at // DK + 1)
                if ph.kind == "ff_up" and ph.group > 0:
                    sc.wait_ge(s_unit, SPLIT_SLOTS + ph.n0)
                repeat(sc, ph, body)
                if ph.side == "mlstm":
                    means.tick(M_HEADS)
                if ph.kind == "ff_up":
                    gelu(ph, 2 * ph.bodies - 1, 1)
                    to_mid(ph, 2 * ph.bodies - 1, 1)
                if ph.sums:
                    square_tile(ph, DK - 1, 1)
                    ysq.tick(DK)
                    root(y_rstd)
                    xup.tick(4)

        @block.gpsimd
        def _(gp):
            gp.memset(ones[:, :], 1.0).then_inc(s_ones, 1)
            gp.sem_inc(s_mul, 2)
            hh = Tally(s_hh)

            gp.wait_ge(s_in["blocks"], 16)
            gp.tensor_copy(blocks[:, :, :].rearrange("p l t -> p (l t)"), extra[:, :]).then_inc(s["masks"], 1)

            for ph in PHASES:
                if ph.norms:
                    sh = 6 * ph.layer + (3 if ph.kind == "ff_up" else 0)
                    for c in range(4):
                        k, h = 4 * c + 3, x_sq[:, 0, c, :]
                        gp.wait_ge(s_h, hh.at // 4 + c + 1)
                        gp.tensor_scalar(h, y[:, k, :], mod[:, sh, k:k + 1], None, ALU.add).then_inc(s["pool_h"], 1)
                        gp.wait_ge(s["pool_h"], hh.at // 4 + c + 1)
                        gp.wait_ge(s_hh, hh.at + k + 1)
                        gp.tensor_tensor(act[:, k, T:2 * T], h, act[:, k, 0:T].bitcast(F32), ALU.subtract)\
                          .then_inc(s_act[1], 1)
                    hh.tick(DK)
                if ph.kind == "values" and ph.layer == 0 and ph.side is None:
                    gp.wait_ge(s_evac, 2 + ph.t0 + ph.tiles)
                    gp.wait_ge(s["gate_col"], 1)
                    with gp.Fori(0, F_HEADS // 2) as i:
                        gp.wait_ge(s["pv"], 2 * (i + 1))
                        for k in range(2):
                            gp.tensor_copy(fox_v(k), values[:, :, bass.ds(M_HEADS * M_DV + 2 * P * i + P * k, P)])\
                              .then_inc(s["vst"], 1)
                if ph.side == "mlstm":
                    gp.wait_ge(s_evac, 2 + ph.t0)
                    gp.wait_ge(s["fy"], 2 + F_HEADS)
                    with gp.Fori(0, M_HEADS // 2) as i:
                        gp.wait_ge(s["m_ss"], 2 * (i + 1))
                        for k in range(2):
                            gp.tensor_copy(m_v(k), values[:, :, bass.ds(512 * i + 256 * k, 256)])\
                              .then_inc(s["m_vst"], 1)
                if ph.side == "gla" and ph.side0 == 0:
                    def stage_values(h, ph=ph):
                        gp.wait_ge(s_evac, 2 + ph.t0 + h + 1)
                        if not first_body(h):
                            gp.wait_ge(s["g_ss"], h)
                        gp.tensor_copy(g_v, values[:, :, bass.ds(h * G_DV, G_DV)]).then_inc(s["g_vst"], 1)

                    stage_values(0)
                    with gp.Fori(1, G_HEADS) as h:
                        stage_values(h)
                if ph.kind == "ff_up":
                    def body(i, ph=ph):
                        for slot in range(2):
                            p = ph.pairs + 2 * i + slot + 1
                            at_ = bass.ds(2 * i + slot, 1)
                            gp.wait_ge(s_gelu, p)
                            gp.tensor_tensor(ff_m[:, slot, :], conv_a[:, slot, :], gelu_g[:, slot, :],
                                             ALU.mult).then_inc(s_mul, 1)
                            gp.wait_ge(s_mh, p)
                            gp.tensor_tensor(flat(mid[:, at_, T:2 * T]), ff_m[:, slot, :],
                                             flat(mid[:, at_, 0:T].bitcast(F32)), ALU.subtract).then_inc(s_mid, 1)
                    repeat(gp, ph, body)

        @block.vector
        def _(ve):
            own = Tally(s_v)
            roots = Tally(s_root)

            def mine():
                ve.wait_ge(s_v, own.at)

            def split(n, slot, raw_slot):
                ve.wait_ge(s_hi, n + 1)
                ve.tensor_tensor(lo[:, slot, :], raw[:, raw_slot, :], hi[:, slot, :].bitcast(F32),
                                 ALU.subtract).then_inc(s_lo, 1)

            def split_next(ph, i, j):
                m = ph.n0 + j + 1
                if isinstance(i, int) and unit(ph, i, j) + 1 >= UNITS:
                    return
                split(unit(ph, i, j) + 1, m % SPLIT_SLOTS, m % RAW_SLOTS)

            def summed(src, half, kt, first):
                at_, weight = acc[:, half * PIECE:(half + 1) * PIECE], cond[:, bass.ds(kt, 1)]
                if first:
                    return ve.tensor_scalar(at_, src, weight, None, ALU.mult)
                return ve.scalar_tensor_tensor(out=at_, in0=src, scalar=weight, in1=at_, op0=ALU.mult, op1=ALU.add)

            def close_section(sec):
                ve.wait_ge(s_red, sec + 1)
                ve.tensor_tensor(mod[:, sec, :], bank[7][:, 0:DK], vec[:, V_ADAB + sec * DK:V_ADAB + (sec + 1) * DK],
                                 ALU.add).then_inc(s_mod, 1)

            sq_n = Tally(s_sqp)
            ysq_n = Tally(s_ysqp)
            hh = Tally(s_hh)

            def rstd(dst, src, width):
                ve.tensor_scalar(dst, src, 1.0 / width, EPS, ALU.mult, ALU.add).then_inc(s_mean, 1)
                ve.wait_ge(s_root, roots.step())
                ve.reciprocal(dst, dst).then_inc(s_v, own.tick())
                mine()

            def norm_weight(layer, part):
                scl = 6 * layer + 3 * part + 1
                w = V_NORM + (4 * layer + 2 * part) * DK
                ve.wait_ge(s_mod, scl + 1)
                ve.scalar_tensor_tensor(out=alpha[:, :], in0=mod[:, scl, :], scalar=1.0, in1=vec[:, w:w + DK],
                                        op0=ALU.add, op1=ALU.mult).then_inc(s_alpha, 1)

            def pre_norm(layer, part):
                sh = 6 * layer + 3 * part
                ve.wait_ge(s_sqp, sq_n.step(4))
                rstd(x_rstd, bank[4][:, 0:T], D)

                def scaled(c):
                    four = y[:, 4 * c:4 * c + 4, :]
                    ve.wait_ge(s_xs, sq_n.at - 3 + c)
                    ve.tensor_tensor(four, four, x_rstd.unsqueeze(1).broadcast_to([P, 4, T]), ALU.mult)\
                      .then_inc(s_h, 1)

                scaled(0)
                for c in range(4):
                    if c < 3:
                        scaled(c + 1)
                    for k in range(4 * c, 4 * c + 3):
                        ve.wait_ge(s_hh, hh.at + k + 1)
                        ve.scalar_tensor_tensor(out=act[:, k, T:2 * T], in0=y[:, k, :], scalar=mod[:, sh, k:k + 1],
                                                in1=act[:, k, 0:T].bitcast(F32), op0=ALU.add, op1=ALU.subtract)\
                          .then_inc(s_act[0], 1)
                hh.tick(DK)

            def gate_weight(layer, part):
                w = V_NORM + (4 * layer + 2 * part + 1) * DK
                ve.wait_ge(s_mod, 6 * layer + 3 * part + 3)
                ve.tensor_tensor(gamma[:, :], mod[:, 6 * layer + 3 * part + 2, :], vec[:, w:w + DK],
                                 ALU.mult).then_inc(s_gamma, 1)

            def post_norm(between):
                ve.wait_ge(s_ysqp, ysq_n.step(DK))
                rstd(y_rstd, bank[4][:, 0:T], D)
                ve.wait_ge(s_ys, ysq_n.at)
                for c in range(4):
                    four, x_four = y[:, 4 * c:4 * c + 4, :], x[:, 4 * c:4 * c + 4, :]
                    ve.tensor_tensor(four, four, y_rstd.unsqueeze(1).broadcast_to([P, 4, T]), ALU.mult)\
                      .then_inc(s_v, own.tick())
                    mine()
                    ve.tensor_tensor(x_four, x_four, four, ALU.add).then_inc(s_x, 1)
                    if c == 0:
                        between()

            def gate_rows_ready():
                ve.wait_ge(s["gate_ln"], 1)
                ve.scalar_tensor_tensor(out=gate_t2, in0=gates[:, :], scalar=0.0, in1=gate_t1, op0=ALU.min,
                                        op1=ALU.subtract).then_inc(s_v, own.tick())
                mine()
                ve.wait_ge(s["masks"], 1)
                ve.tensor_tensor_scan(gate_rows, ones[0:GATES, :], gate_t2, 0.0, ALU.mult, ALU.add)\
                  .then_inc(s_v, own.tick())
                mine()
                ve.tensor_copy(gate_rows[0:M_HEADS, :], gates[0:M_HEADS, :]).then_inc(s["gate_cum"], 1)

            def row_of(k, head):
                ve.wait_ge(s["gate_cum"], 1)
                return ve.tensor_scalar(row(k), gate_rows, vec[0:GATES, bass.ds(V_COEF + head, 1)], None, ALU.mult)

            def before_split(ph, i, j):
                if ph.side == "fox":
                    pair, r = fox_pair(ph, i, j)
                    if r == 0:
                        for k in range(2):
                            row_of(k, M_HEADS + 2 * pair + k).then_inc(s["row"], 1)
                if ph.side == "mlstm" and j == 0:
                    for k in range(2):
                        row_of(k, 2 * i + k).then_inc(s["m_row"], 1)
                if ph.side == "gla":
                    h = ph.side0 + i
                    if j == 0:
                        if first_body(h):
                            ve.wait_ge(s_mac, PAUSE)
                        else:
                            ve.wait_ge(s["expd"], h * LEVELS)
                        ve.memset(g_r, 0.0).then_inc(s["decay"], 1)
                    if j >= 1:
                        scale(h, j + 1)
                        use(h, j)
                    if 1 <= j < 7:
                        grow(h, j + 2)

            def normed(l_, at_):
                ve.reciprocal(stat[:, at_:at_ + 2], stat[:, at_:at_ + 2]).then_inc(s_v, own.tick())
                mine()
                for tb in range(TB):
                    i_ = ve.tensor_scalar(l_[:, tb, :], l_[:, tb, :], stat[:, at_ + tb:at_ + tb + 1], None, ALU.mult)
                return i_

            def masked_max(l_, bank_, at_):
                ve.tensor_tensor(l_, split2(bank_[:, :]), causal[:, :, :], ALU.add).then_inc(s_v, own.tick())
                mine()
                ve.tensor_reduce(stat[:, at_:at_ + 2], l_, AX_X, ALU.max).then_inc(s_v, own.tick())
                mine()

            def grow(h, lv):
                c = 1 << (lv - 2)
                of = [P, T // c, c]
                ve.wait_ge(s["decay"], h * LEVELS + lv - 1)
                ve.tensor_tensor(halves(g_r, c, 0), halves(g_r, c, 0),
                                 halves(g_a, c, 1)[:, :, c - 1:c].broadcast_to(of), ALU.add)\
                  .then_inc(s_v, own.tick())
                mine()
                ve.tensor_tensor(halves(g_a, c, 1), halves(g_a, c, 1),
                                 halves(g_a, c, 0)[:, :, c - 1:c].broadcast_to(of), ALU.add).then_inc(s["decay"], 1)

            def scale(h, lv):
                b = 1 << (lv - 1)
                ve.wait_ge(s["expd"], h * LEVELS + lv)
                ve.wait_ge(s["prod"], h * (LEVELS + 1) + lv)
                ve.tensor_tensor(halves(g_q, b, 1), halves(region[:, bass.ds(GQ * T + h * 2 * T, 2 * T)], b, 1),
                                 g_e[:, 0:T].rearrange("p (n c) -> p n c", c=b), ALU.mult)
                ve.tensor_tensor(halves(g_k, b, 0), halves(region[:, bass.ds(GK * T + h * 2 * T, 2 * T)], b, 0),
                                 g_e[:, T:2 * T].rearrange("p (n c) -> p n c", c=b), ALU.mult)\
                  .then_inc(s["scaled"], 1)

            def use(h, lv):
                prod = split2(bank[5 - lv % 2][:, 0:TB * P])
                if lv == LEVELS:
                    ve.wait_ge(s["prod"], (h + 1) * (LEVELS + 1))
                    ve.tensor_copy(g_s[:, 0, P:T], prod[:, 0, :]).then_inc(s["used"], 1)
                else:
                    ve.copy_predicated(g_s[:, :, 0:P], blocks[:, lv, :].unsqueeze(1).broadcast_to([P, TB, P]), prod)\
                      .then_inc(s["used"], 1)

            def after_split(ph, i, j):
                if ph.side == "fox":
                    pair, r = fox_pair(ph, i, j)
                    for k in range(2):
                        done = 2 * pair + k + 1
                        if r == 1:
                            ve.wait_ge(s_in["causal"], 16)
                            ve.wait_ge(s["score"], done)
                            masked_max(fox_l(k), bank[4 + k], 4 * k)
                            ve.tensor_scalar(stat[:, 4 * k:4 * k + 2], stat[:, 4 * k:4 * k + 2], -1.0, None, ALU.mult)\
                              .then_inc(s["lmax"], 1)
                        if r == 2:
                            ve.wait_ge(s["prob"], done)
                            normed(fox_l(k), 4 * k + 2).then_inc(s["pn"], 1)
                if ph.side == "mlstm" and j == 1:
                    for k in range(2):
                        ve.wait_ge(s["m_score"], 2 * i + k + 1)
                        masked_max(m_l(k), bank[4 + 2 * k], 8 * k)
                        ve.tensor_scalar(stat[:, 8 * k:8 * k + 2], stat[:, 8 * k:8 * k + 2], -1.0, 0.0, ALU.mult,
                                         ALU.min).then_inc(s["m_max"], 1)
                    for k in range(2):
                        ve.wait_ge(s["m_prob"], 2 * i + k + 1)
                        for tb in range(TB):
                            i_ = ve.tensor_tensor_reduce(m_l(k)[:, tb, :], m_l(k)[:, tb, :],
                                                         bank[5 + 2 * k][:, tb * T:(tb + 1) * T], 1.0, 0.0, ALU.mult,
                                                         ALU.add, stat[:, 8 * k + 2 + tb:8 * k + 3 + tb])
                        i_.then_inc(s_v, own.tick())
                        mine()
                        den = stat[:, 8 * k + 2:8 * k + 4]
                        ve.scalar_tensor_tensor(out=den, in0=den, scalar=-1.0, in1=den, op0=ALU.mult, op1=ALU.max)\
                          .then_inc(s_v, own.tick())
                        mine()
                        ve.tensor_tensor(den, den, stat[:, 8 * k + 4:8 * k + 6], ALU.max).then_inc(s_v, own.tick())
                        mine()
                        normed(m_l(k), 8 * k + 2).then_inc(s["m_pn"], 1)
                if ph.side == "gla":
                    h = ph.side0 + i
                    if j == 0:
                        if not first_body(h):
                            ve.wait_ge(s["g_pv"], h)
                        ve.memset(g_s[:, :, :], 0.0).then_inc(s_v, own.tick())
                        mine()
                        scale(h, 1)
                        use(h, 0)
                        grow(h, 2)
                    if j == 1 and not first_body(h):
                        gla_store(h)
                    if j == 7:
                        use(h, 8)

            def gla_store(heads):
                ve.wait_ge(s["g_ss"], heads)
                ve.tensor_scalar(g_rstd, bank[5][:, T:2 * T], 1.0 / (G_DV * G_DK), EPS, ALU.mult, ALU.add)\
                  .then_inc(s["g_mean"], 1)
                ve.wait_ge(s["g_root"], heads)
                ve.reciprocal(g_rstd, g_rstd).then_inc(s["g_rstd"], 1)
                ve.wait_ge(s["g_rstd"], heads)
                for dv in range(4):
                    t = 4 * (heads - 1) + dv
                    i_ = ve.scalar_tensor_tensor(out=flat(y[:, bass.ds(t, 1), :]),
                                                 in0=bank[6 + dv // 2][:, (dv % 2) * T:(dv % 2 + 1) * T],
                                                 scalar=vec[:, bass.ds(V_GNORM + t, 1)], in1=g_rstd,
                                                 op0=ALU.mult, op1=ALU.mult)
                i_.then_inc(s["g_y"], 1)

            def after_evac(ph, i, j):
                if ph.side == "fox":
                    pair, r = fox_pair(ph, i, j)
                    if r == 3:
                        for k in range(2):
                            ve.wait_ge(s["pv"], 2 + 2 * pair + k + 1)
                            ve.tensor_copy(flat(y[:, bass.ds(8 + 2 * pair + k, 1), :]), bank[4 + k][:, 0:T])\
                              .then_inc(s["fy"], 1)
                if ph.side == "mlstm" and j == 3:
                    for k in range(2):
                        ve.wait_ge(s["m_ss"], 2 + 2 * i + k + 1)
                        rstd(m_q(k), bank[4 + 2 * k][:, 0:T], M_DV)
                        for dv in range(2):
                            t = 4 * i + 2 * k + dv
                            i_ = ve.scalar_tensor_tensor(out=flat(y[:, bass.ds(t, 1), :]),
                                                         in0=bank[5 + 2 * k][:, dv * T:(dv + 1) * T],
                                                         scalar=vec[:, bass.ds(V_MNORM + t, 1)], in1=m_q(k),
                                                         op0=ALU.mult, op1=ALU.mult)
                        i_.then_inc(s["m_y"], 1)
                if ph.side == "decay" and j == 3:
                    ve.wait_ge(s["g_ln"], 3 * i + 3)
                    ve.scalar_tensor_tensor(out=g_decay(i), in0=g_decay(i), scalar=0.0, in1=g_abs, op0=ALU.min,
                                            op1=ALU.subtract).then_inc(s["decays"], 1)

            def gate_tail(ph):
                order, gated, gate0, _ = tail(ph)
                for k, c in enumerate(gated):
                    ve.wait_ge(s["t_gate"], 2 * ph.layer + k + 1)
                    four = y[:, 4 * c:4 * c + 4, :]
                    if ph.layer == 0:
                        ve.wait_ge(s["m_y"], 2 + M_HEADS)
                    else:
                        ve.wait_ge(s["g_y"], G_HEADS)
                    ve.tensor_tensor(four, four, split2(region[:, (gate0 + 4 * c) * T:(gate0 + 4 * c + 4) * T], 4),
                                     ALU.mult).then_inc(s["t_mul"], 1)
                for k, c in enumerate(order):
                    ve.wait_ge(s["t_hi"], 4 * ph.layer + k + 1)
                    ve.tensor_tensor(act[:, 4 * c:4 * c + 4, T:2 * T], y[:, 4 * c:4 * c + 4, :],
                                     act[:, 4 * c:4 * c + 4, 0:T].bitcast(F32), ALU.subtract).then_inc(s["t_lo"], 1)

            ve.sem_inc(s_lo, RAW_SLOTS)
            ve.sem_inc(s_evac, 2)
            ve.sem_inc(s["fy"], 2)
            ve.sem_inc(s["m_y"], 2)
            ve.wait_ge(s_cond, 1)
            for sec in range(2):
                if sec > 0:
                    close_section(0)
                trips = PIECES // HEAD_SLOTS

                def eight_pieces(i, sec=sec, trips=trips):
                    for j in range(HEAD_SLOTS):
                        ve.wait_ge(s_head[j], 16 * (i + sec * trips + 1))
                        if j >= 2 or not (sec == 0 and first_body(i)):
                            ve.wait_ge(s_mac, sec * PIECES + i * HEAD_SLOTS + j - 1)
                        summed(region[:, j * PIECE:(j + 1) * PIECE], j % 2, i * (HEAD_SLOTS // 2) + j // 2,
                               first_body(i) and j < 2).then_inc(s_mac, 1)

                eight_pieces(0)
                with ve.Fori(1, trips) as i:
                    eight_pieces(i)
            close_section(1)
            split(0, 0, 0)

            for ph in PHASES:
                if ph.sums:
                    gate_weight(ph.layer, int(ph.kind == "ff_down"))
                if ph.norms:
                    if ph is PHASES[0]:
                        norm_weight(0, 0)
                    split_next(ph, 0, 0)
                    pre_norm(ph.layer, int(ph.kind == "ff_up"))
                if ph.kind == "values" and ph.layer == 0 and ph.side is None:
                    gate_rows_ready()
                if ph.side == "fox" and ph.side0 == 0:
                    ve.wait_ge(s["gate_t"], 1)
                    ve.tensor_copy(stat[:, 32:32 + TB * GATES], bank[7][:, 0:TB * GATES]).then_inc(s["gate_col"], 1)
                if ph.kind == "mixed" and ph.layer == 1:
                    gla_store(G_HEADS)
                if ph.kind == "mixed":
                    gate_tail(ph)

                def body(i, ph=ph):
                    k = 0

                    def sum_piece(k):
                        a = ph.a0 + i * ph.per_body + k
                        done = (ph.a0 + ph.now * ph.per_body + k) % PIECES - ph.now * ph.per_body
                        first = isinstance(a, int) and a % PIECES < 2
                        if first and k > 0 and a % PIECES == 0:
                            close_section(a // PIECES - 1)
                        elif first and a % PIECES == 0 and not first_body(i):
                            close_section(a // PIECES - 1)
                        ve.wait_ge(s_piece[k % ADA_SLOTS],
                                   16 * ((ph.a0 - 2 * PIECES + k) // ADA_SLOTS + i * (ph.per_body // ADA_SLOTS) + 1))
                        ve.wait_ge(s_mac, a - 1)
                        kt = a % PIECES // 2 if isinstance(a, int) else (done - k % 2) // 2 + i * (ph.per_body // 2)
                        summed(piece[:, k % ADA_SLOTS, :], k % 2, kt, first).then_inc(s_mac, 1)

                    for j in range(ph.units):
                        before_split(ph, i, j)
                        if not (ph.norms and first_body(i) and j == 0):
                            split_next(ph, i, j)
                        after_split(ph, i, j)
                        if ph.ada[j] > 0:
                            sum_piece(k)
                        n = unit(ph, i, j)
                        tile_no = ph.t0 + (j // 4 if ph.kind == "values" else j)
                        tile_ps = bank[2 * (tile_no % 2)][:, 0:T]
                        if ph.kind != "values" or j % 4 == 3:
                            ve.wait_ge(s_unit, SPLIT_SLOTS + n + 1)
                        if ph.kind == "values" and j % 4 == 3:
                            at_ = bass.ds(ph.dest + i * ph.units * P + (j // 4) * 512, 512)
                            for tb in range(TB):
                                i_ = ve.tensor_copy(values[:, tb, at_], bank[2 * (tile_no % 2) + tb][:, :])
                            i_.then_inc(s_evac, 1)
                        elif ph.kind == "gates":
                            bias = vec[0:GATES, V_GATEB:V_GATEB + 1] if ph.layer == 0 else 0.0
                            ve.tensor_scalar(gates[:, :], tile_ps[0:GATES], bias, None, ALU.add).then_inc(s_evac, 1)
                        elif ph.kind == "columns":
                            ve.tensor_copy(region[:, bass.ds((ph.dest + ph.units * i + j) * T, T)], tile_ps)\
                              .then_inc(s_evac, 1)
                        elif ph.kind == "mixed" or (ph.kind == "ff_down" and ph.group == 0):
                            ve.tensor_copy(flat(y[:, bass.ds(4 * i + j, 1), :]), tile_ps).then_inc(s_evac, 1)
                        elif ph.kind == "ff_down":
                            at_ = flat(y[:, bass.ds(4 * i + j, 1), :])
                            ve.tensor_tensor(at_, at_, tile_ps, ALU.add).then_inc(s_evac, 1)
                        elif ph.kind == "ff_up":
                            slot, is_g = j // 2, j % 2
                            out_ = (conv_g if is_g else conv_a)[:, slot, :]
                            ch = V_CONV + (ph.layer * FF_TILES + 2 * sum(FF_GROUPS[:ph.group]) + j) * (CONV_W + 1)
                            ch = ch + i * ph.units * (CONV_W + 1)
                            if not is_g:
                                ve.wait_ge(s_mul, (ph.pairs + slot + 1) + 2 * i)
                            ve.tensor_scalar(out_, tile_ps, vec[:, bass.ds(ch + 2, 1)], vec[:, bass.ds(ch + 3, 1)],
                                             ALU.mult, ALU.add).then_inc(s_v, own.tick())
                            mine()
                            ve.scalar_tensor_tensor(out=out_[:, 1:T], in0=tile_ps[:, 0:T - 1],
                                                    scalar=vec[:, bass.ds(ch + 1, 1)], in1=out_[:, 1:T],
                                                    op0=ALU.mult, op1=ALU.add).then_inc(s_v, own.tick())
                            mine()
                            ve.scalar_tensor_tensor(out=out_[:, 2:T], in0=tile_ps[:, 0:T - 2],
                                                    scalar=vec[:, bass.ds(ch, 1)], in1=out_[:, 2:T],
                                                    op0=ALU.mult, op1=ALU.add).then_inc(s_evac, 1)
                        after_evac(ph, i, j)
                        for more in range(1, ph.ada[j]):
                            sum_piece(k + more)
                        k += ph.ada[j]

                per = OWN.get((ph.kind, ph.side), 0)
                roots_per = 2 if ph.side == "mlstm" else 0
                base, roots_base = own.at, roots.at

                def counted(i, base=base, roots_base=roots_base, per=per, roots_per=roots_per):
                    own.at, own.extra, roots.at = base + i * per, 0, roots_base + i * roots_per
                    body(i)
                    assert own.extra == per, (ph.kind, ph.side, own.extra)
                repeat(ve, ph, counted)
                own.at, roots.at = base + per * ph.bodies, roots_base + roots_per * ph.bodies

                def between(ph=ph):
                    if ph.closes:
                        close_section(ph.a_end // PIECES - 1)
                    if ph.sums and ph is not PHASES[-1]:
                        norm_weight(*((ph.layer, 1) if ph.kind == "mixed" else (ph.layer + 1, 0)))

                if ph.sums:
                    post_norm(between)
                else:
                    between()

        @block.tensor
        def _(pe):
            sqn = Tally(s_sq)
            ysqn = Tally(s_ysq)
            actn = Tally(s_act[1])

            def sum_x_squares():
                for b in range(4):
                    pe.wait_ge(s_sq, sqn.step())
                    for k in range(4):
                        i_ = pe.matmul(bank[4][:, 0:T], ones[:, 0:P], x_sq[:, b % 2, k, :], start=(b == 0 and k == 0),
                                       stop=(b == 3 and k == 3))
                    i_.then_inc(s_sqp, 1)

            def sum_y_square(q, slot):
                pe.wait_ge(s_ysq, ysqn.at + q + 1)
                first, last = isinstance(q, int) and q == 0, isinstance(q, int) and q == DK - 1
                pe.matmul(bank[4][:, 0:T], ones[:, 0:P], y_sq[:, slot, :], start=first, stop=last).then_inc(s_ysqp, 1)

            def reduce_section(sec):
                if sec > 0:
                    pe.wait_ge(s_mod, sec)
                pe.wait_ge(s_mac, (sec + 1) * PIECES)
                for j in range(DK):
                    i_ = pe.matmul(bank[7][:, j:j + 1], acc[:, j * P:(j + 1) * P], ones[:, 0:1], start=True, stop=True)
                i_.then_inc(s_red, 1)

            def transposes(dst, src):
                for tb, sb_ in ((0, 0), (1, 0), (1, 1)):
                    i_ = pe.transpose(dst[:, sb_ * T + tb * P:sb_ * T + (tb + 1) * P],
                                      src[:, tb, sb_ * P:(sb_ + 1) * P], ident[:, :])
                return i_

            def fox_work(ph, i, j):
                pair, r = fox_pair(ph, i, j)
                for k in range(2):
                    done = 2 * pair + k + 1
                    if r == 0:
                        pe.wait_ge(s["fy"], 2 * (pair + 1))
                        pe.wait_ge(s["qst"], done)
                        pe.wait_ge(s["row"], done)
                        for tb in range(TB):
                            dst = bank[4 + k][:, tb * T:(tb + 1) * T]
                            pe.matmul(dst, fox_q(k)[:, tb * P:(tb + 1) * P],
                                      region[:, bass.ds((FK + k + 2 * pair) * T, T)], start=True, stop=False)
                            i_ = pe.matmul(dst, ones[0:GATES, 0:P], row(k), start=False, stop=True)
                        i_.then_inc(s["score"], 1)
                    if r == 2:
                        pe.wait_ge(s["pn"], done)
                        transposes(bank[4 + k], fox_l(k)).then_inc(s["pt"], 1)
                    if r == 3:
                        pe.wait_ge(s["vst"], done)
                        pe.wait_ge(s["pc"], done)
                        pe.matmul(bank[4 + k][:, 0:T], fox_v(k)[:, 0, :], fox_l(k)[:, 0, :], start=True, stop=False)
                        pe.matmul(bank[4 + k][:, P:T], fox_v(k)[:, 1, :], fox_l(k)[:, 1, P:T], start=False, stop=True)\
                          .then_inc(s["pv"], 1)

            def mlstm_work(ph, i, j):
                for k in range(2):
                    done = 2 * i + k + 1
                    if j == 0:
                        pe.wait_ge(s["m_y"], 2 * (i + 1))
                        if k == 1:
                            pe.wait_ge(s_mod, 3)
                        pe.wait_ge(s["m_qst"], done)
                        pe.wait_ge(s["m_row"], done)
                        for tb in range(TB):
                            pe.matmul(bank[4 + 2 * k][:, tb * T:(tb + 1) * T], ones[0:GATES, 0:P], row(k),
                                      start=True, stop=True)
                            i_ = pe.matmul(bank[5 + 2 * k][:, tb * T:(tb + 1) * T], m_q(k)[:, tb * P:(tb + 1) * P],
                                           region[:, bass.ds((MK + k) * T + i * 2 * T, T)], start=True, stop=True)
                        i_.then_inc(s["m_score"], 1)
                    if j == 1:
                        pe.wait_ge(s["m_pn"], done)
                        transposes(bank[4 + 2 * k], m_l(k)).then_inc(s["m_pt"], 1)
                    if j == 2:
                        pe.wait_ge(s["m_vst"], done)
                        pe.wait_ge(s["m_pc"], done)
                        for dv in range(2):
                            dst = bank[5 + 2 * k][:, dv * T:(dv + 1) * T]
                            pe.matmul(dst, m_v(k)[:, 0, dv * P:(dv + 1) * P], m_l(k)[:, 0, :], start=True, stop=False)
                            i_ = pe.matmul(dst[:, P:T], m_v(k)[:, 1, dv * P:(dv + 1) * P], m_l(k)[:, 1, P:T],
                                           start=False, stop=True)
                        i_.then_inc(s["m_pv"], 1)
                    if j == 3:
                        pe.wait_ge(s["m_sq"], done)
                        for dv in range(2):
                            i_ = pe.matmul(bank[4 + 2 * k][:, 0:T], ones[:, 0:P], m_v(k)[:, dv, :], start=dv == 0,
                                           stop=dv == 1)
                        i_.then_inc(s["m_ss"], 1)

            def product(h, lv):
                if lv > 0:
                    pe.wait_ge(s["scaled"], h * LEVELS + lv)
                if lv == 2 and not first_body(h):
                    pe.wait_ge(s["g_mean"], h)
                if lv > 1:
                    pe.wait_ge(s["used"], h * (LEVELS + 1) + lv - 1)
                dst = bank[5 - lv % 2]
                for tb in range(1 if lv == LEVELS else TB):
                    t0 = P if lv == LEVELS else tb * P
                    for dh in range(2):
                        i_ = pe.matmul(dst[:, tb * P:(tb + 1) * P], g_k[:, dh * T + tb * P:dh * T + (tb + 1) * P],
                                       g_q[:, dh * T + t0:dh * T + t0 + P], start=dh == 0, stop=dh == 1)
                i_.then_inc(s["prod"], 1)

            def decay_work(ph, i, j):
                if j == 0:
                    pe.wait_ge(s["w2"], 16)
                    pe.wait_ge(s_evac, 2 + ph.t0)
                    if not first_body(i):
                        pe.wait_ge(s["g_ln"], 3 * i)
                    for dh in range(2):
                        i_ = pe.matmul(bank[4][:, dh * T:(dh + 1) * T],
                                       g_w2[:, bass.ds((2 * i + dh) * P, P)], gates[:, :], start=True, stop=True)
                    i_.then_inc(s["z"], 1)

            def gla_midway(ph, i, j):
                h = ph.side0 + i
                if j == 0:
                    pe.wait_ge(s["copies"], h + 1)
                    product(h, 0)
                if j == 7:
                    product(h, 8)

            def gla_work(ph, i, j):
                h = ph.side0 + i
                if j == 0 and not first_body(h):
                    gla_sums(h)
                if j < 7:
                    product(h, j + 1)
                else:
                    pe.wait_ge(s["used"], (h + 1) * (LEVELS + 1))
                    pe.wait_ge(s["g_vst"], h + 1)
                    if not first_body(h):
                        pe.wait_ge(s["g_y"], h)
                    for dv in range(4):
                        dst = bank[6 + dv // 2][:, (dv % 2) * T:(dv % 2 + 1) * T]
                        pe.matmul(dst, g_v[:, 0, dv * P:(dv + 1) * P], g_s[:, 0, :], start=True, stop=False)
                        i_ = pe.matmul(dst[:, P:T], g_v[:, 1, dv * P:(dv + 1) * P], g_s[:, 1, 0:P], start=False,
                                       stop=True)
                    i_.then_inc(s["g_pv"], 1)

            def gla_sums(heads):
                pe.wait_ge(s["g_sq"], heads)
                if not (isinstance(heads, int) and heads == G_HEADS):
                    pe.wait_ge(s["used"], heads * (LEVELS + 1) + 1)
                for dv in range(4):
                    i_ = pe.matmul(bank[5][:, T:2 * T], ones[:, 0:P], g_sq[:, dv, :], start=dv == 0, stop=dv == 3)
                i_.then_inc(s["g_ss"], 1)

            pe.sem_inc(s_unit, SPLIT_SLOTS)
            pe.sem_inc(s["pv"], 2)
            pe.sem_inc(s["m_ss"], 2)
            pe.wait_ge(s_ones, 1)
            pe.wait_ge(s_in["ident"], 16)
            reduce_section(0)
            reduce_section(1)

            for ph in PHASES:
                if ph.norms:
                    sum_x_squares()
                if ph.side == "fox" and ph.side0 == 0:
                    pe.wait_ge(s["gate_cum"], 1)
                    pe.wait_ge(s_mod, 3)
                    for tb in range(TB):
                        i_ = pe.transpose(bank[7][:, tb * GATES:(tb + 1) * GATES], gate_rows[:, tb * P:(tb + 1) * P],
                                          ident[0:GATES, 0:GATES])
                    i_.then_inc(s["gate_t"], 1)
                if ph.kind == "mixed" and ph.layer == 1:
                    gla_sums(G_HEADS)
                if ph.kind == "ff_down":
                    pe.wait_ge(s_mid, ph.pairs)

                def columns(ph, i, j, slot):
                    pe.wait_ge(s_evac, ph.t0 + i * ph.tiles + j + 1)
                    dst = bank[2 * ((ph.t0 + j) % 2)][:, 0:T]
                    src = mid if ph.kind == "ff_down" else act
                    order = list(range(FF_GROUPS[ph.group] if ph.kind == "ff_down" else DK))
                    if ph.kind == "mixed" and first_body(i) and j == 0:
                        order = [4 * c + k for c in tail(ph)[0] for k in range(4)]
                    for at, kt in enumerate(order):
                        if first_body(i) and j == 0:
                            if ph.norms:
                                own, k = divmod(kt, 4)
                                if k < 3:
                                    pe.wait_ge(s_act[0], 3 * (actn.at + own) + k + 1)
                                else:
                                    pe.wait_ge(s_act[1], actn.at + own + 1)
                            if ph.kind == "mixed" and at % 4 == 0:
                                pe.wait_ge(s["t_lo"], 4 * ph.layer + at // 4 + 1)
                        if ph.side == "gla" and at == DK // 2:
                            gla_midway(ph, i, j)
                        w_hi, w_lo = hi[:, slot, kt * P:(kt + 1) * P], lo[:, slot, kt * P:(kt + 1) * P]
                        pe.matmul(dst, w_hi, src[:, kt, 0:T], start=at == 0, stop=False)
                        pe.matmul(dst, w_hi, src[:, kt, T:2 * T], start=False, stop=False)
                        i_ = pe.matmul(dst, w_lo, src[:, kt, 0:T], start=False, stop=at == len(order) - 1)
                    return i_

                def tokens(ph, i, j, slot):
                    tile_no = ph.t0 + j // 4
                    if j % 4 == 0:
                        pe.wait_ge(s_evac, ph.t0 + i * ph.tiles + j // 4 + 1)
                    for q in range(4):
                        kt = 4 * (j % 4) + q
                        if ph.side == "gla" and q == 2:
                            gla_midway(ph, i, j)
                        w_hi, w_lo = hi[:, slot, q * 512:(q + 1) * 512], lo[:, slot, q * 512:(q + 1) * 512]
                        for tb in range(TB):
                            dst = bank[2 * (tile_no % 2) + tb][:, :]
                            x_hi = act[:, kt, tb * P:(tb + 1) * P]
                            x_lo = act[:, kt, T + tb * P:T + (tb + 1) * P]
                            pe.matmul(dst, x_hi, w_hi, start=kt == 0, stop=False)
                            pe.matmul(dst, x_hi, w_lo, start=False, stop=False)
                            i_ = pe.matmul(dst, x_lo, w_hi, start=False, stop=kt == DK - 1)
                    return i_

                def body(i, ph=ph):
                    for j in range(ph.units):
                        slot = (ph.n0 + j) % SPLIT_SLOTS
                        pe.wait_ge(s_lo, RAW_SLOTS + unit(ph, i, j) + 1)
                        (tokens if ph.kind == "values" else columns)(ph, i, j, slot).then_inc(s_unit, 1)
                        if ph.side is not None:
                            {"fox": fox_work, "mlstm": mlstm_work, "decay": decay_work, "gla": gla_work}[ph.side](ph, i, j)
                        a = ph.a0 + i * ph.per_body + sum(ph.ada[:j])
                        if isinstance(a, int):
                            for last in range(a, min(a + ph.ada[j], ph.a_end - 1)):
                                if last % PIECES == PIECES - 1:
                                    reduce_section(last // PIECES)
                        if ph.sums and not (first_body(i) and j == 0):
                            sum_y_square(ph.units * i + j - 1, (j + 1) % 2)

                if ph.side == "decay":
                    ph.head = ph.bodies
                repeat(pe, ph, body)
                if ph.norms:
                    actn.tick(DK // 4)
                if ph.sums:
                    sum_y_square(DK - 1, 1)
                    ysqn.tick(DK)
                if ph.closes:
                    if ph.side == "mlstm":
                        pe.wait_ge(s["m_y"], 2 + M_HEADS)
                    reduce_section(ph.a_end // PIECES - 1)


def columns_unit(w, cols):
    return w[:, cols].reshape(-1, P, P).transpose(1, 0, 2).reshape(P, -1)


def values_units(w):
    return w.reshape(4, 4, P, -1, 512).transpose(3, 0, 2, 1, 4).reshape(-1, P, UNIT)


def per_channel(v):
    return v.reshape(-1, P).T


def kernel(x, c, ada_w, ada_b, norm_w, even_in_w, m_gate_b, m_norm_w, fox_f_b, even_out_w, odd_in_w, gla_a_w2,
           gla_a_b, gla_norm_w, odd_out_w, ffn_in_w, ffn_conv_w, ffn_conv_b, ffn_out_w):
    from concourse import bacc
    from concourse.bass_utils import run_bass_kernel_spmd

    (x, c, ada_w, ada_b, norm_w, even_in_w, m_gate_b, m_norm_w, fox_f_b, even_out_w, odd_in_w, gla_a_w2, gla_a_b,
     gla_norm_w, odd_out_w, ffn_in_w, ffn_conv_w, ffn_conv_b, ffn_out_w) = (
        np.asarray(v) for v in (x, c, ada_w, ada_b, norm_w, even_in_w, m_gate_b, m_norm_w, fox_f_b, even_out_w,
                                odd_in_w, gla_a_w2, gla_a_b, gla_norm_w, odd_out_w, ffn_in_w, ffn_conv_w,
                                ffn_conv_b, ffn_out_w))
    even, odd = even_in_w[0], odd_in_w[0]
    parts = [[("gates", (3072, 3080), (6152, 6160)), ("columns", (3080, 4104), (4104, 5128)), ("values", (5128, 6152)),
              ("columns", (0, 512), (512, 1024)), ("values", (1024, 2048)), ("columns", (2048, 3072))],
             [("gates", (6144, 6160)), ("columns", (0, 1024), (1024, 2048)), ("values", (2048, 4096)),
              ("columns", (4096, 6144))]]
    units = np.zeros((UNITS, P, UNIT), np.float32)
    n = 0
    for layer in range(LAYERS):
        w = (even, odd)[layer]
        for kind, *spans in parts[layer]:
            cols = np.concatenate([w[:, a:b] for a, b in spans], axis=1)
            if kind == "gates":
                units[n].reshape(P, DK, P)[:, :, 0:GATES] = cols.reshape(DK, P, GATES).transpose(1, 0, 2)
                n += 1
            elif kind == "columns":
                for k in range(0, cols.shape[1], P):
                    units[n] = columns_unit(cols, slice(k, k + P))
                    n += 1
            else:
                got = values_units(cols)
                units[n:n + len(got)] = got
                n += len(got)
        w = (even_out_w, odd_out_w)[layer][0]
        for m in range(DK):
            units[n] = columns_unit(w, slice(m * P, (m + 1) * P))
            n += 1
        first = 0
        for tiles in FF_GROUPS:
            for k in range(first, first + tiles):
                for part in range(2):
                    at = part * D_FF + k * P
                    units[n] = columns_unit(ffn_in_w[layer], slice(at, at + P))
                    n += 1
            rows = ffn_out_w[layer][first * P:(first + tiles) * P]
            for m in range(DK):
                units[n][:, 0:tiles * P] = columns_unit(rows, slice(m * P, (m + 1) * P))
                n += 1
            first += tiles
    assert n == UNITS

    ada = ada_w.reshape(LAYERS, DK, P, 6, 2, PIECE).transpose(0, 3, 1, 4, 2, 5).reshape(-1, P, PIECE)
    conv = np.concatenate([ffn_conv_w.reshape(LAYERS, CONV_W, 2, D_FF // P, P),
                           ffn_conv_b.reshape(LAYERS, 1, 2, D_FF // P, P)], axis=1)
    conv = conv.transpose(4, 0, 3, 2, 1).reshape(P, -1)
    vec = np.zeros((P, V_END), np.float32)
    vec[:, V_C:V_ADAB] = per_channel(c)
    vec[:, V_ADAB:V_NORM] = per_channel(ada_b)
    vec[:, V_NORM:V_MNORM] = per_channel(norm_w)
    vec[:, V_MNORM:V_GNORM] = per_channel(m_norm_w)
    vec[:, V_GNORM:V_AB] = per_channel(gla_norm_w)
    vec[:, V_AB:V_GATEB] = per_channel(gla_a_b)
    vec[0:GATES, V_GATEB] = np.concatenate([m_gate_b[0], fox_f_b[0]])
    for h in range(M_HEADS):
        vec[h, V_COEF + h] = 1.0
        vec[M_HEADS + h, V_COEF + h] = -1.0
    for h in range(F_HEADS):
        vec[2 * M_HEADS + h, V_COEF + M_HEADS + h] = -1.0
    vec[:, V_CONV:V_END] = conv

    tok = np.arange(T)
    causal = np.zeros((P, TB, T), np.float32)
    for tb in range(TB):
        causal[:, tb][tok[None, :] > (tok[tb * P:(tb + 1) * P])[:, None]] = NEG
    blocks = np.zeros((P, LEVELS, P), np.float32)
    a, b = np.arange(P)[:, None], np.arange(P)[None, :]
    blocks[:, 0][a == b] = 1
    for lv in range(1, LEVELS):
        size = 1 << (lv - 1)
        blocks[:, lv][(a // size % 2 == 0) & (b // size == a // size + 1)] = 1

    arrays = {
        "w_units": units,
        "ada_pieces": np.ascontiguousarray(ada),
        "vectors": vec,
        "x_in": np.ascontiguousarray(x[0].T.reshape(DK, P, T).transpose(1, 0, 2)),
        "identity": np.eye(P, dtype=np.float32),
        "causal_in": causal,
        "blocks_in": blocks.reshape(P, -1),
        "a_w2": np.ascontiguousarray(gla_a_w2[0]),
    }
    nc = bacc.Bacc("TRN2", target_bir_lowering=False, num_devices=1)
    aps = [nc.dram_tensor(k, v.shape, mybir.dt.from_np(v.dtype), kind="ExternalInput").ap()
           for k, v in arrays.items()]
    out = nc.dram_tensor("x_out", (P, DK, T), F32, kind="ExternalOutput").ap()
    program(nc, *aps, out)
    got = run_bass_kernel_spmd(nc, [arrays], core_ids=[0]).results[0]["x_out"]
    return np.ascontiguousarray(got.transpose(1, 0, 2).reshape(1, D, T).transpose(0, 2, 1))
```

```python
from contextlib import ExitStack

import numpy as np

import concourse.bass as bass
from concourse import mybir

F32 = mybir.dt.float32
F32R = mybir.dt.float32r
U8 = mybir.dt.uint8
ALU = mybir.AluOpType
ACT = mybir.ActivationFunctionType
AX_X = mybir.AxisListType.X

P = 128
T = 256
TB = T // P
D = 2048
DK = D // P
EPS = 1e-6
LAYERS = 2

M_HEADS, M_DQK, M_DV = 4, 128, 256
F_HEADS, F_DH = 8, 128
G_HEADS, G_DK, G_DV, G_RANK, G_TAU = 4, 256, 512, 16, 16.0
D_FF = 5632
CONV_W = 3
GATES = 16

UNIT = DK * P
RAW_SLOTS, SPLIT_SLOTS = 4, 2
PIECE = 1024
PIECES = D // P * (D // PIECE)
SECTIONS = 6 * LAYERS
ADA_SLOTS = 2
HEAD_SLOTS = 8
FF_GROUPS = (16, 16, 12)

LEVELS = 8
NEG = -1e30


class Phase:

    def __init__(self, kind, layer, bodies, units, ada, group=0, dest=0, side=None, side0=0):
        self.kind, self.layer, self.bodies, self.units, self.ada = kind, layer, bodies, units, ada
        self.group, self.dest, self.side, self.side0 = group, dest, side, side0
        self.per_body = sum(ada)
        self.tiles = units // 4 if kind == "values" else units
        self.sums = kind == "mixed" or (kind == "ff_down" and group == len(FF_GROUPS) - 1)
        self.norms = kind == "gates" or (kind == "ff_up" and group == 0)
        self.peel = self.head = 0

    def place(self, n, t, a, pairs):
        self.n0, self.t0, self.a0, self.pairs = n, t, a, pairs
        self.end = n + self.bodies * self.units
        self.a_end = a + self.bodies * self.per_body
        self.closes = self.per_body > 0 and self.a_end % PIECES == 0
        pairs += 2 * self.bodies if self.kind == "ff_up" else 0
        return self.end, t + self.bodies * self.tiles, self.a_end, pairs

    def straight(self, i):
        first = self.a0 + i * self.per_body
        return (i < self.head or i >= self.bodies - self.peel
                or any(a % PIECES in (0, PIECES - 1) for a in range(first, first + self.per_body)))


MQ, MK, MO, FQ, FK = 0, 4, 8, 16, 24
GQ, GK, GR = 0, 8, 16


def plan():
    no = (0,) * 4
    phases = [Phase("gates", 0, 1, 1, (0,)),
              Phase("columns", 0, 4, 4, (2, 1, 2, 1), dest=FQ),
              Phase("values", 0, 1, 8, (1,) * 8, dest=M_HEADS * M_DV),
              Phase("columns", 0, 2, 4, (2,) * 4, dest=MQ, side="fox"),
              Phase("values", 0, 1, 8, (2,) * 8, side="fox", side0=2),
              Phase("columns", 0, 2, 4, (1,) * 4, dest=MO, side="mlstm"),
              Phase("mixed", 0, 4, 4, (2, 1, 2, 1)),
              Phase("ff_up", 0, 8, 4, (1,) * 4, 0), Phase("ff_down", 0, 4, 4, (2, 1, 2, 1), 0),
              Phase("ff_up", 0, 8, 4, (1,) * 4, 1), Phase("ff_down", 0, 4, 4, (2, 1, 2, 1), 1),
              Phase("ff_up", 0, 6, 4, (1,) * 4, 2), Phase("ff_down", 0, 4, 4, (1, 0, 1, 0), 2),
              Phase("gates", 1, 1, 1, (0,)),
              Phase("columns", 1, 4, 4, (2, 1, 2, 1), dest=GQ, side="decay"),
              Phase("values", 1, 2, 8, (0,) * 8, side="gla"),
              Phase("columns", 1, 2, 8, (0,) * 8, dest=GR, side="gla", side0=2),
              Phase("mixed", 1, 4, 4, (2, 1, 2, 1)),
              Phase("ff_up", 1, 8, 4, (1,) * 4, 0), Phase("ff_down", 1, 4, 4, no, 0),
              Phase("ff_up", 1, 8, 4, no, 1), Phase("ff_down", 1, 4, 4, no, 1),
              Phase("ff_up", 1, 6, 4, no, 2), Phase("ff_down", 1, 4, 4, no, 2)]
    state = (0, 0, 2 * PIECES, 0)
    for ph in phases:
        state = ph.place(*state)
        starts_gla = ph.side == "gla" and ph.side0 == 0
        ph.head = int(starts_gla or ph.sums or ph.norms or ph.kind in ("ff_up", "ff_down"))
    assert state[2] == SECTIONS * PIECES
    phases[-1].peel = 2
    return phases, state[0]


PHASES, UNITS = plan()
PAUSE = next(ph for ph in PHASES if ph.side == "gla").a0

V_C, V_ADAB = 0, DK
V_NORM = V_ADAB + SECTIONS * DK
V_MNORM = V_NORM + LAYERS * 4 * DK
V_GNORM = V_MNORM + M_HEADS * M_DV // P
V_AB = V_GNORM + G_HEADS * G_DV // P
V_GATEB = V_AB + G_HEADS * G_DK // P
V_COEF = V_GATEB + 1
V_CONV = V_COEF + M_HEADS + F_HEADS
FF_TILES = 2 * D_FF // P
V_END = V_CONV + LAYERS * FF_TILES * (CONV_W + 1)

V_AT = 32 * T
REGION = V_AT + TB * D
OWN = {("ff_up", None): 8, ("columns", "fox"): 6, ("values", "fox"): 12, ("columns", "mlstm"): 14,
       ("values", "gla"): 8, ("columns", "gla"): 8}


class Tally:

    def __init__(self, sem, start=0):
        self.sem, self.base, self.at, self.extra = sem, start, start, 0

    def tick(self, k=1):
        self.at = self.at + k
        self.extra += k
        return k

    def step(self, k=1):
        self.tick(k)
        return self.at

    def enter(self, i, per):
        self.base, self.per, self.extra = self.at, per, 0
        self.at = self.at + i * per

    def leave(self, trips):
        assert self.extra == self.per, (self.extra, self.per)
        self.at = self.base + trips * self.per


def repeat(eng, ph, body):
    at = 0
    while at < ph.bodies:
        stop = at
        while stop < ph.bodies and not ph.straight(stop):
            stop += 1
        ph.now = at
        if stop - at > 1:
            with eng.Fori(at, stop) as i:
                body(i)
            at = stop
        else:
            body(at)
            at += 1


def first_body(i):
    return isinstance(i, int) and i == 0


def program(nc, w_dram, ada_dram, vec_dram, x_dram, ident_dram, causal_dram, blocks_dram, w2_dram, out_dram):
    with ExitStack() as ctx:
        def sb(name, shape, dt=F32):
            return ctx.enter_context(nc.sbuf_tensor(name, shape, dt))

        def sem(name):
            return ctx.enter_context(nc.semaphore(name))

        def flat(ap):
            return ap.rearrange("p a t -> p (a t)")

        def split2(ap, b=TB):
            return ap.rearrange("p (b c) -> p b c", b=b)

        region_at = -(-nc.sbuf_base // 32) * 32
        region = sb("region", [P, REGION])
        mid = nc.alloc_sbuf_tensor_at("mid", [P, 16, 2 * T], F32R, offset=region_at)
        x = sb("x", [P, DK, T])
        y = sb("y", [P, DK, T])
        act = sb("act", [P, DK, 2 * T], F32R)
        raw = sb("raw", [P, RAW_SLOTS, UNIT])
        hi = sb("hi", [P, SPLIT_SLOTS, UNIT], F32R)
        lo = sb("lo", [P, SPLIT_SLOTS, UNIT], F32R)
        piece = sb("piece", [P, ADA_SLOTS, PIECE])
        acc = sb("acc", [P, D])
        vec = sb("vec", [P, V_END])
        mod = sb("mod", [P, SECTIONS, DK])
        cond = sb("cond", [P, DK])
        alpha = sb("alpha", [P, DK])
        gamma = sb("gamma", [P, DK])
        ident = sb("ident", [P, P])
        ones = sb("ones", [P, T])
        causal = sb("causal", [P, TB, T])
        blocks = sb("blocks", [P, LEVELS, P], U8)
        gates = sb("gates", [GATES, T])
        extra = sb("extra", [P, 4 * T])
        stat = sb("stat", [P, 64])

        yf = flat(y[:, :, :])
        values = split2(region[:, V_AT:REGION])
        conv_a, conv_g, gelu_g, ff_m = (split2(region[:, V_AT + k * 2 * T:V_AT + (k + 1) * 2 * T], 2)
                                        for k in range(4))
        y_sq = split2(region[:, V_AT:V_AT + 2 * T], 2)
        y_rstd = region[:, V_AT + 2 * T:V_AT + 3 * T]
        head_acc = yf[:, 0:D]
        x_rstd = region[:, V_AT + 3 * T:V_AT + 4 * T]
        x_sq = region[:, V_AT + 4 * T:V_AT + 12 * T].rearrange("p (b a t) -> p b a t", b=2, a=4)

        gate_t1 = region[0:GATES, MO * T:(MO + 1) * T]
        gate_t2 = region[0:GATES, (MO + 1) * T:(MO + 2) * T]
        gate_rows = extra[0:GATES, 0:T]

        def row(k):
            return extra[0:GATES, (1 + k) * T:(2 + k) * T]

        def fox_part(k, a, b):
            return region[:, (MO + 4 * k + a) * T:(MO + 4 * k + b) * T]

        def fox_q(k):
            return fox_part(k, 0, 1)

        def fox_v(k):
            return split2(fox_part(k, 1, 2))

        def fox_l(k):
            return split2(fox_part(k, 2, 4))

        def m_part(k, a, b):
            return region[:, (FQ + 5 * k + a) * T:(FQ + 5 * k + b) * T]

        def m_q(k):
            return m_part(k, 0, 1)

        def m_v(k):
            return split2(m_part(k, 1, 3))

        def m_l(k):
            return split2(m_part(k, 3, 5))

        pf = flat(piece[:, :, :])
        g_q, g_k, g_a, g_r = (pf[:, k * 2 * T:(k + 1) * 2 * T] for k in range(4))
        g_e = extra[:, 0:2 * T]
        g_s = split2(extra[:, 2 * T:4 * T])
        g_w2 = extra[0:G_RANK, :]
        g_abs = yf[:, 0:2 * T]
        g_rstd = causal[:, 0, :]
        g_v = split2(yf[:, 12 * T:16 * T])
        g_sq = yf[:, 12 * T:16 * T].rearrange("p (a t) -> p a t", a=4)

        def g_decay(h):
            return region[:, bass.ds((GR + 8 + 2 * h) * T, 2 * T)]

        def halves(ap, b, right):
            return ap.rearrange("p (n two c) -> p n two c", two=2, c=b)[:, :, right, :]

        bank = [ctx.enter_context(nc.psum_tensor(f"bank{k}", [P, 512], F32)) for k in range(8)]

        s_raw = [sem(f"raw_ready{j}") for j in range(RAW_SLOTS)]
        s_hi = sem("hi_ready")
        s_lo = sem("lo_ready")
        s_unit = sem("unit_done")
        s_evac = sem("tile_evacuated")
        s_piece = [sem(f"piece_ready{j}") for j in range(ADA_SLOTS)]
        s_head = [sem(f"head_piece_ready{j}") for j in range(HEAD_SLOTS)]
        s_mac = sem("piece_summed")
        s_red = sem("section_reduced")
        s_mod = sem("section_stored")
        s_in = {k: sem(f"loaded_{k}") for k in ("vec", "x", "ident", "causal", "blocks")}
        s_cond = sem("cond_ready")
        s_ones = sem("ones_ready")
        s_v = sem("vector_step")
        s_mean = sem("mean_square_ready")
        s_root = sem("root_ready")
        s_sq = sem("x_squares_ready")
        s_sqp = sem("x_squares_summed")
        s_ysq = sem("y_squares_ready")
        s_ysqp = sem("y_squares_summed")
        s_h = sem("normed_ready")
        s_hh = sem("act_hi_ready")
        s_act = [sem("act_ready"), sem("act_ready_pool")]
        s_gamma = sem("gamma_ready")
        s_alpha = sem("alpha_ready")
        s_ys = sem("y_scaled")
        s_xs = sem("x_scaled")
        s_x = sem("x_updated")
        s_gelu = sem("gelu_ready")
        s_mul = sem("ff_product_ready")
        s_mh = sem("mid_hi_ready")
        s_mid = sem("mid_ready")
        s_store = sem("stored")
        names = ("masks_ready", "pool_normed", "gate_abs_exp", "gate_log_ready", "gate_rows_ready",
                 "gate_transposed", "gate_columns_ready", "fox_queries_staged", "fox_values_staged",
                 "fox_row_ready", "fox_scores_ready", "fox_max_ready", "fox_exp_ready", "fox_weights_ready",
                 "fox_transposed", "fox_weights_staged", "fox_attended", "fox_stored",
                 "mlstm_queries_staged", "mlstm_values_staged", "mlstm_row_ready", "mlstm_scores_ready",
                 "mlstm_max_ready", "mlstm_exp_ready", "mlstm_weights_ready", "mlstm_transposed",
                 "mlstm_weights_staged", "mlstm_attended", "mlstm_squares_ready", "mlstm_squares_summed",
                 "mlstm_stored", "loaded_a_w2", "gla_values_staged", "gla_gate_projected",
                 "gla_gate_log_steps", "gla_decays_ready", "gla_head_staged", "gla_level_exponents",
                 "gla_level_decays", "gla_level_scaled", "gla_level_product", "gla_level_used",
                 "gla_attended", "gla_squares_ready", "gla_squares_summed", "gla_mean_ready",
                 "gla_root_ready", "gla_rstd_ready", "gla_stored", "output_gate_ready", "gated",
                 "gated_hi_ready", "gated_lo_ready")
        s = {k: sem(k) for k in names}

        block = ctx.enter_context(nc.Block())

        def unit(ph, i, j):
            return ph.n0 + i * ph.units + j

        def fox_pair(ph, i, j):
            return ph.side0 + (i if ph.units == 4 else j // 4), j % 4

        def tail(ph):
            return ((2, 3, 0, 1), (0, 1), MO, ACT.Sigmoid) if ph.layer == 0 else \
                ((0, 1, 2, 3), (0, 1, 2, 3), GR, ACT.Silu)

        @block.sync
        def _(sp):
            sp.dma_start(vec[:, :], vec_dram).then_inc(s_in["vec"], 16)

            def head_load(i, j):
                src = ada_dram[bass.ds(i * HEAD_SLOTS + j, 1)].rearrange("a p n -> p (a n)")
                sp.dma_start(region[:, j * PIECE:(j + 1) * PIECE], src).then_inc(s_head[j], 16)

            for j in range(HEAD_SLOTS):
                head_load(0, j)
            sp.dma_start(x[:, :, :], x_dram).then_inc(s_in["x"], 16)
            sp.dma_start(ident[:, :], ident_dram).then_inc(s_in["ident"], 16)
            with sp.Fori(1, 2 * PIECES // HEAD_SLOTS) as i:
                for j in range(HEAD_SLOTS):
                    sp.wait_ge(s_mac, (i - 1) * HEAD_SLOTS + j + 1)
                    head_load(i, j)

            def load_unit(n, slot):
                src = w_dram[bass.ds(n, 1)].rearrange("a p n -> p (a n)")
                sp.dma_start(raw[:, slot, :], src).then_inc(s_raw[slot], 16)

            def load_piece(a, slot):
                src = ada_dram[bass.ds(a, 1)].rearrange("a p n -> p (a n)")
                sp.dma_start(piece[:, slot, :], src).then_inc(s_piece[slot], 16)

            for n in range(RAW_SLOTS):
                load_unit(n, n)
            for a in range(ADA_SLOTS):
                load_piece(2 * PIECES + a, a)
            sp.dma_start(causal[:, :, :], causal_dram).then_inc(s_in["causal"], 16)
            sp.dma_start(extra[:, :], blocks_dram).then_inc(s_in["blocks"], 16)
            sp.wait_ge(s_lo, RAW_SLOTS + 1)
            load_unit(RAW_SLOTS, 0)

            for ph in PHASES:
                def body(i, ph=ph):
                    k = 0
                    for j in range(ph.units):
                        n = unit(ph, i, j)
                        if not isinstance(n, int) or n + RAW_SLOTS + 1 < UNITS:
                            sp.wait_ge(s_lo, RAW_SLOTS + n + 2)
                            load_unit(n + RAW_SLOTS + 1, (ph.n0 + j + 1) % RAW_SLOTS)
                        for _ in range(ph.ada[j]):
                            a = ph.a0 + i * ph.per_body + k
                            if not isinstance(a, int) or not (a + ADA_SLOTS >= SECTIONS * PIECES
                                                              or PAUSE <= a + ADA_SLOTS < PAUSE + ADA_SLOTS):
                                sp.wait_ge(s_mac, a + 1)
                                load_piece(a + ADA_SLOTS, k % ADA_SLOTS)
                            k += 1

                if ph.kind == "gates" and ph.layer == 1:
                    sp.wait_ge(s["mlstm_stored"], 2 + M_HEADS)
                    sp.dma_start(g_w2, w2_dram).then_inc(s["loaded_a_w2"], 16)
                if ph.a0 == PAUSE and ph.kind == "mixed":
                    sp.wait_ge(s["gla_stored"], G_HEADS)
                    for k in range(ADA_SLOTS):
                        load_piece(PAUSE + k, k)
                straight = ph.per_body > 0 and ph.a_end in (PAUSE, SECTIONS * PIECES)
                kept, ph.peel = ph.peel, max(ph.peel, int(straight))
                repeat(sp, ph, body)
                ph.peel = kept

            for c in range(4):
                sp.wait_ge(s_x, 8 * LAYERS - 3 + c)
                sp.dma_start(out_dram[:, 4 * c:4 * c + 4, :], x[:, 4 * c:4 * c + 4, :]).then_inc(s_store, 16)
            sp.wait_ge(s_store, 4 * 16)

        @block.scalar
        def _(sc):
            def split(n, slot, raw_slot, uses):
                sc.wait_ge(s_raw[raw_slot], 16 * uses)
                sc.wait_ge(s_unit, n + 1)
                sc.activation(hi[:, slot, :], raw[:, raw_slot, :], ACT.Copy).then_inc(s_hi, 1)

            def split_next(ph, i, j):
                m = ph.n0 + j + 1
                if isinstance(i, int) and unit(ph, i, j) + 1 >= UNITS:
                    return
                split(unit(ph, i, j) + 1, m % SPLIT_SLOTS, m % RAW_SLOTS,
                      m // RAW_SLOTS + i * (ph.units // RAW_SLOTS) + 1)

            sqp = Tally(s_sqp)
            ysq = Tally(s_ysq)
            xup = Tally(s_x)
            means = Tally(s_mean)

            def root(at_, scale=1.0):
                sc.wait_ge(s_mean, means.step())
                sc.activation(at_, at_, ACT.Sqrt, scale=scale).then_inc(s_root, 1)

            def by_weight(c):
                for k in range(4 * c, 4 * c + 4):
                    i_ = sc.activation(y[:, k, :], x[:, k, :], ACT.Copy, scale=alpha[:, k:k + 1])
                i_.then_inc(s_xs, 1)

            def pre_norm(layer, part, first):
                for b in range(4):
                    if xup.at == 0:
                        sc.wait_ge(s_in["x"], 16)
                    else:
                        sc.wait_ge(s_x, xup.at - 4 + b + 1)
                    if sqp.at + b >= 2:
                        sc.wait_ge(s_sqp, sqp.at + b - 1)
                    sc.activation(x_sq[:, b % 2], x[:, 4 * b:4 * b + 4, :], ACT.Square).then_inc(s_sq, 1)
                    if first:
                        continue
                    if b == 0:
                        sc.wait_ge(s_alpha, sqp.at // 4 + 1)
                    if b < 2:
                        by_weight(b)
                if first:
                    root(x_rstd)
                    split(0, 0, 0, 1)
                    split_next(PHASES[0], 0, 0)
                    sc.wait_ge(s_alpha, 1)
                    by_weight(0)
                    by_weight(1)
                else:
                    by_weight(2)
                    root(x_rstd)
                    by_weight(3)
                sh = 6 * layer + 3 * part
                for c in range(4):
                    if first and c in (1, 2):
                        by_weight(c + 1)
                    sc.wait_ge(s_h, sqp.at + c + 1)
                    for k in range(4 * c, 4 * c + 4):
                        sc.activation(act[:, k, 0:T], y[:, k, :], ACT.Identity, bias=mod[:, sh, k:k + 1])\
                          .then_inc(s_hh, 1)
                sqp.tick(4)

            def square_tile(ph, q, slot):
                sc.wait_ge(s_evac, 2 + ph.t0 + q + 1)
                if not isinstance(q, int) or ysq.at + q >= 2:
                    sc.wait_ge(s_ysqp, ysq.at + q - 1)
                tile_ = flat(y[:, bass.ds(q, 1), :])
                sc.activation(y_sq[:, slot, :], tile_, ACT.Square).then_inc(s_ysq, 1)
                sc.activation(tile_, tile_, ACT.Copy, scale=gamma[:, bass.ds(q, 1)]).then_inc(s_ys, 1)

            def gate_ln():
                sc.wait_ge(s_evac, 2 + 1)
                sc.activation(gate_t1, gates[:, :], ACT.Abs).then_inc(s["gate_abs_exp"], 1)
                sc.wait_ge(s["gate_abs_exp"], 1)
                sc.activation(gate_t1, gate_t1, ACT.Exp, scale=-1.0).then_inc(s["gate_abs_exp"], 1)
                sc.wait_ge(s["gate_abs_exp"], 2)
                sc.activation(gate_t1, gate_t1, ACT.Ln, bias=1.0).then_inc(s["gate_log_ready"], 1)

            def u_tile(k):
                return region[:, bass.ds(k * T, T)]

            def column(c):
                return stat[:, c:c + 1]

            def before_split(ph, i, j):
                if ph.side == "fox":
                    pair, r = fox_pair(ph, i, j)
                    if r == 0:
                        sc.wait_ge(s["gate_columns_ready"], 1)
                        for k in range(2):
                            sc.activation(fox_q(k), u_tile(FQ + 2 * pair + k), ACT.Copy,
                                          scale=float(F_DH) ** -0.5).then_inc(s["fox_queries_staged"], 1)
                if ph.side == "mlstm" and j == 0:
                    sc.wait_ge(s["fox_stored"], 2 + F_HEADS)
                    sc.wait_ge(s["mlstm_stored"], 2 * (i + 1))
                    for k in range(2):
                        sc.activation(m_q(k), u_tile(MQ + 2 * i + k), ACT.Copy,
                                      scale=float(M_DQK) ** -0.5).then_inc(s["mlstm_queries_staged"], 1)
                if ph.side == "gla" and j == 0:
                    h = ph.side0 + i
                    if first_body(h):
                        sc.wait_ge(s_mac, PAUSE)
                    else:
                        sc.wait_ge(s["gla_level_product"], h * (LEVELS + 1))
                        sc.wait_ge(s["gla_level_decays"], h * LEVELS)
                    sc.activation(g_q, region[:, bass.ds(GQ * T + h * 2 * T, 2 * T)], ACT.Copy)
                    sc.activation(g_k, region[:, bass.ds(GK * T + h * 2 * T, 2 * T)], ACT.Copy)
                    sc.wait_ge(s["gla_decays_ready"], G_HEADS)
                    sc.activation(g_a, g_decay(h), ACT.Copy).then_inc(s["gla_head_staged"], 1)

            def exps(h, lv):
                sc.wait_ge(s["gla_level_exponents"], h * LEVELS + lv)
                if lv == 1:
                    sc.wait_ge(s["gla_head_staged"], h + 1)
                if lv > 1 or not first_body(h):
                    sc.wait_ge(s["gla_level_scaled"], h * LEVELS + lv - 1)
                b = 1 << (lv - 1)
                sc.activation(g_e[:, 0:T].rearrange("p (n c) -> p n c", c=b), halves(g_a, b, 1), ACT.Exp,
                              scale=1.0 / G_TAU)
                sc.activation(g_e[:, T:2 * T].rearrange("p (n c) -> p n c", c=b), halves(g_r, b, 0), ACT.Exp,
                              scale=1.0 / G_TAU).then_inc(s["gla_level_decays"], 1)

            def after_split(ph, i, j):
                if ph.side == "fox":
                    pair, r = fox_pair(ph, i, j)
                    for k in range(2):
                        done = 2 * pair + k + 1
                        if r == 1:
                            sc.wait_ge(s["fox_max_ready"], done)
                            for tb in range(TB):
                                i_ = sc.activation(fox_l(k)[:, tb, :], fox_l(k)[:, tb, :], ACT.Exp,
                                                   bias=column(4 * k + tb), accum_out=column(4 * k + 2 + tb))
                            i_.then_inc(s["fox_exp_ready"], 1)
                        if r == 3:
                            sc.wait_ge(s["fox_transposed"], done)
                            sc.activation(fox_l(k)[:, 0, :], bank[4 + k][:, 0:T], ACT.Copy)
                            sc.activation(fox_l(k)[:, 1, P:T], bank[4 + k][:, T + P:2 * T], ACT.Copy)\
                              .then_inc(s["fox_weights_staged"], 1)
                if ph.side == "mlstm":
                    for k in range(2):
                        done = 2 * i + k + 1
                        if j == 1:
                            sc.wait_ge(s["mlstm_max_ready"], done)
                            for tb in range(TB):
                                sc.activation(column(8 * k + 4 + tb),
                                              stat[:, bass.ds(32 + tb * GATES + M_HEADS + 2 * i + k, 1)], ACT.Exp,
                                              bias=column(8 * k + tb), scale=-1.0)
                            for tb in range(TB):
                                i_ = sc.activation(m_l(k)[:, tb, :], m_l(k)[:, tb, :], ACT.Exp,
                                                   bias=column(8 * k + tb))
                            i_.then_inc(s["mlstm_exp_ready"], 1)
                        if j == 2:
                            sc.wait_ge(s["mlstm_transposed"], done)
                            sc.activation(m_l(k)[:, 0, :], bank[4 + 2 * k][:, 0:T], ACT.Copy)
                            sc.activation(m_l(k)[:, 1, P:T], bank[4 + 2 * k][:, T + P:2 * T], ACT.Copy)\
                              .then_inc(s["mlstm_weights_staged"], 1)
                        if j == 3:
                            sc.wait_ge(s["mlstm_attended"], done)
                            sc.activation(m_v(k), split2(bank[5 + 2 * k][:, :]), ACT.Square)\
                              .then_inc(s["mlstm_squares_ready"], 1)
                    if j == 3:
                        means.enter(i, 2)
                        for k in range(2):
                            root(m_q(k))
                        means.leave(0)
                if ph.side == "decay":
                    if j == 1:
                        if not first_body(i):
                            sc.wait_ge(s["gla_decays_ready"], i)
                        sc.wait_ge(s["gla_gate_projected"], i + 1)
                        for dh in range(2):
                            z_ps, bias = bank[4][:, dh * T:(dh + 1) * T], vec[:, bass.ds(V_AB + 2 * i + dh, 1)]
                            sc.activation(region[:, bass.ds((GR + 8 + 2 * i + dh) * T, T)], z_ps, ACT.Identity,
                                          bias=bias)
                            i_ = sc.activation(g_abs[:, dh * T:(dh + 1) * T], z_ps, ACT.Abs, bias=bias)
                        i_.then_inc(s["gla_gate_log_steps"], 1)
                    if j == 2:
                        sc.wait_ge(s["gla_gate_log_steps"], 3 * i + 1)
                        sc.activation(g_abs, g_abs, ACT.Exp, scale=-1.0).then_inc(s["gla_gate_log_steps"], 1)
                    if j == 3:
                        sc.wait_ge(s["gla_gate_log_steps"], 3 * i + 2)
                        sc.activation(g_abs, g_abs, ACT.Ln, bias=1.0).then_inc(s["gla_gate_log_steps"], 1)
                if ph.side == "gla":
                    h = ph.side0 + i
                    if j == 0:
                        exps(h, 1)
                    if j < 7:
                        exps(h, j + 2)
                    if j == 0 and not first_body(h):
                        gla_squares(h)
                    if j == 1 and not first_body(h):
                        gla_root(h)

            def gla_squares(heads):
                sc.wait_ge(s["gla_attended"], heads)
                for half in range(2):
                    i_ = sc.activation(g_sq[:, 2 * half:2 * half + 2, :], split2(bank[6 + half][:, :]), ACT.Square)
                i_.then_inc(s["gla_squares_ready"], 1)

            def gla_root(heads):
                sc.wait_ge(s["gla_mean_ready"], heads)
                sc.activation(g_rstd, g_rstd, ACT.Sqrt, scale=float(G_DK)).then_inc(s["gla_root_ready"], 1)

            def gate_tail(ph):
                order, gated, gate0, func = tail(ph)
                done = 2 * ph.layer

                def to_act(c):
                    sc.activation(act[:, 4 * c:4 * c + 4, 0:T], y[:, 4 * c:4 * c + 4, :], ACT.Copy)\
                      .then_inc(s["gated_hi_ready"], 1)

                for c in gated:
                    if c == 0:
                        sc.wait_ge(s_evac, 2 + ph.t0 - 4)
                    if c == gated[-1]:
                        sc.wait_ge(s_evac, 2 + ph.t0)
                    at_ = region[:, (gate0 + 4 * c) * T:(gate0 + 4 * c + 4) * T]
                    sc.activation(at_, at_, func).then_inc(s["output_gate_ready"], 1)
                sc.wait_ge(s_unit, SPLIT_SLOTS + ph.n0)
                if ph.layer == 0:
                    sc.wait_ge(s["fox_stored"], 2 + F_HEADS)
                    to_act(2)
                    to_act(3)
                for k, c in enumerate(gated):
                    if ph.layer == 1 and c == 3:
                        gla_squares(G_HEADS)
                        gla_root(G_HEADS)
                    sc.wait_ge(s["gated"], done + k + 1)
                    to_act(c)

            sc.wait_ge(s_in["vec"], 16)
            sc.activation(cond[:, :], vec[:, V_C:V_C + DK], ACT.Silu).then_inc(s_cond, 1)

            def gelu(ph, q, slot):
                sc.wait_ge(s_evac, 2 + ph.t0 + 2 * q + 2)
                sc.wait_ge(s_mul, ph.pairs + q + 1)
                sc.activation(gelu_g[:, slot, :], conv_g[:, slot, :], ACT.Gelu_apprx_tanh).then_inc(s_gelu, 1)

            def to_mid(ph, q, slot):
                sc.wait_ge(s_mul, ph.pairs + q + 3)
                sc.activation(flat(mid[:, bass.ds(q, 1), 0:T]), ff_m[:, slot, :], ACT.Copy).then_inc(s_mh, 1)

            for ph in PHASES:
                if ph.norms:
                    first = ph is PHASES[0]
                    if not first:
                        split_next(ph, 0, 0)
                    pre_norm(ph.layer, int(ph.kind == "ff_up"), first)
                if ph.kind == "values" and ph.layer == 0 and ph.side is None:
                    gate_ln()
                if ph.kind == "mixed":
                    gate_tail(ph)

                def body(i, ph=ph):
                    for j in range(ph.units):
                        before_split(ph, i, j)
                        if not (ph.norms and first_body(i) and j == 0):
                            split_next(ph, i, j)
                        after_split(ph, i, j)
                        if ph.kind == "ff_down" and first_body(i) and j == 0:
                            gelu(last_up, 2 * last_up.bodies - 1, 1)
                            to_mid(last_up, 2 * last_up.bodies - 1, 1)
                        if ph.kind == "ff_up" and not (first_body(i) and j < 2):
                            q = 2 * i + (j // 2 - 1)
                            (gelu if j % 2 == 0 else to_mid)(ph, q, (j // 2 + 1) % 2)
                        if ph.sums and not (first_body(i) and j == 0):
                            square_tile(ph, ph.units * i + j - 1, (j + 1) % 2)

                if ph.sums:
                    sc.wait_ge(s_gamma, ysq.at // DK + 1)
                if ph.kind == "ff_up" and ph.group > 0:
                    sc.wait_ge(s_unit, SPLIT_SLOTS + ph.n0)
                repeat(sc, ph, body)
                if ph.side == "mlstm":
                    means.tick(M_HEADS)
                last_up = ph
                if ph.sums:
                    square_tile(ph, DK - 1, 1)
                    ysq.tick(DK)
                    root(y_rstd)
                    xup.tick(4)

        @block.gpsimd
        def _(gp):
            gp.memset(ones[:, :], 1.0).then_inc(s_ones, 1)
            gp.sem_inc(s_mul, 2)
            hh = Tally(s_hh)

            for ph in PHASES:
                if ph.norms:
                    sh = 6 * ph.layer + (3 if ph.kind == "ff_up" else 0)
                    for c in range(4):
                        k, h = 4 * c + 3, x_sq[:, 0, c, :]
                        gp.wait_ge(s_h, hh.at // 4 + c + 1)
                        gp.tensor_scalar(h, y[:, k, :], mod[:, sh, k:k + 1], None, ALU.add)\
                          .then_inc(s["pool_normed"], 1)
                        gp.wait_ge(s["pool_normed"], hh.at // 4 + c + 1)
                        gp.wait_ge(s_hh, hh.at + k + 1)
                        gp.tensor_tensor(act[:, k, T:2 * T], h, act[:, k, 0:T].bitcast(F32), ALU.subtract)\
                          .then_inc(s_act[1], 1)
                    hh.tick(DK)
                if ph is PHASES[0]:
                    gp.wait_ge(s_in["blocks"], 16)
                    gp.tensor_copy(blocks[:, :, :].rearrange("p l t -> p (l t)"), extra[:, :])\
                      .then_inc(s["masks_ready"], 1)
                if ph.kind == "values" and ph.layer == 0 and ph.side is None:
                    gp.wait_ge(s_evac, 2 + ph.t0 + ph.tiles)
                    gp.wait_ge(s["gate_columns_ready"], 1)
                    with gp.Fori(0, F_HEADS // 2) as i:
                        gp.wait_ge(s["fox_attended"], 2 * (i + 1))
                        for k in range(2):
                            gp.tensor_copy(fox_v(k), values[:, :, bass.ds(M_HEADS * M_DV + 2 * P * i + P * k, P)])\
                              .then_inc(s["fox_values_staged"], 1)
                if ph.side == "mlstm":
                    gp.wait_ge(s_evac, 2 + ph.t0)
                    gp.wait_ge(s["fox_stored"], 2 + F_HEADS)
                    with gp.Fori(0, M_HEADS // 2) as i:
                        gp.wait_ge(s["mlstm_squares_summed"], 2 * (i + 1))
                        for k in range(2):
                            gp.tensor_copy(m_v(k), values[:, :, bass.ds(512 * i + 256 * k, 256)])\
                              .then_inc(s["mlstm_values_staged"], 1)
                if ph.side == "gla" and ph.side0 == 0:
                    def stage_values(h, ph=ph):
                        gp.wait_ge(s_evac, 2 + ph.t0 + h + 1)
                        if not first_body(h):
                            gp.wait_ge(s["gla_squares_summed"], h)
                        gp.tensor_copy(g_v, values[:, :, bass.ds(h * G_DV, G_DV)]).then_inc(s["gla_values_staged"], 1)

                    stage_values(0)
                    with gp.Fori(1, G_HEADS) as h:
                        stage_values(h)
                if ph.kind == "ff_up":
                    def body(i, ph=ph):
                        for slot in range(2):
                            p = ph.pairs + 2 * i + slot + 1
                            at_ = bass.ds(2 * i + slot, 1)
                            gp.wait_ge(s_gelu, p)
                            gp.tensor_tensor(ff_m[:, slot, :], conv_a[:, slot, :], gelu_g[:, slot, :],
                                             ALU.mult).then_inc(s_mul, 1)
                            gp.wait_ge(s_mh, p)
                            gp.tensor_tensor(flat(mid[:, at_, T:2 * T]), ff_m[:, slot, :],
                                             flat(mid[:, at_, 0:T].bitcast(F32)), ALU.subtract).then_inc(s_mid, 1)
                    repeat(gp, ph, body)

        @block.vector
        def _(ve):
            own = Tally(s_v)
            roots = Tally(s_root)

            def mine():
                ve.wait_ge(s_v, own.at)

            def split(n, slot, raw_slot):
                ve.wait_ge(s_hi, n + 1)
                ve.tensor_tensor(lo[:, slot, :], raw[:, raw_slot, :], hi[:, slot, :].bitcast(F32),
                                 ALU.subtract).then_inc(s_lo, 1)

            def split_next(ph, i, j):
                m = ph.n0 + j + 1
                if isinstance(i, int) and unit(ph, i, j) + 1 >= UNITS:
                    return
                split(unit(ph, i, j) + 1, m % SPLIT_SLOTS, m % RAW_SLOTS)

            def summed(src, half, kt, first, acc=acc):
                at_, weight = acc[:, half * PIECE:(half + 1) * PIECE], cond[:, bass.ds(kt, 1)]
                if first:
                    return ve.tensor_scalar(at_, src, weight, None, ALU.mult)
                return ve.scalar_tensor_tensor(out=at_, in0=src, scalar=weight, in1=at_, op0=ALU.mult, op1=ALU.add)

            def close_section(sec):
                ve.wait_ge(s_red, sec + 1)
                ve.tensor_tensor(mod[:, sec, :], bank[7][:, 0:DK], vec[:, V_ADAB + sec * DK:V_ADAB + (sec + 1) * DK],
                                 ALU.add).then_inc(s_mod, 1)

            sq_n = Tally(s_sqp)
            ysq_n = Tally(s_ysqp)
            hh = Tally(s_hh)

            def rstd(dst, src, width):
                ve.tensor_scalar(dst, src, 1.0 / width, EPS, ALU.mult, ALU.add).then_inc(s_mean, 1)
                ve.wait_ge(s_root, roots.step())
                ve.reciprocal(dst, dst).then_inc(s_v, own.tick())
                mine()

            def norm_weight(layer, part):
                scl = 6 * layer + 3 * part + 1
                w = V_NORM + (4 * layer + 2 * part) * DK
                ve.wait_ge(s_mod, scl + 1)
                ve.scalar_tensor_tensor(out=alpha[:, :], in0=mod[:, scl, :], scalar=1.0, in1=vec[:, w:w + DK],
                                        op0=ALU.add, op1=ALU.mult).then_inc(s_alpha, 1)

            def x_root():
                ve.wait_ge(s_sqp, sq_n.step(4))
                rstd(x_rstd, bank[4][:, 0:T], D)

            def pre_norm(layer, part):
                sh = 6 * layer + 3 * part

                def scaled(c):
                    four = y[:, 4 * c:4 * c + 4, :]
                    ve.wait_ge(s_xs, sq_n.at - 3 + c)
                    ve.tensor_tensor(four, four, x_rstd.unsqueeze(1).broadcast_to([P, 4, T]), ALU.mult)\
                      .then_inc(s_h, 1)

                scaled(0)
                for c in range(4):
                    if c < 3:
                        scaled(c + 1)
                    for k in range(4 * c, 4 * c + 3):
                        ve.wait_ge(s_hh, hh.at + k + 1)
                        ve.scalar_tensor_tensor(out=act[:, k, T:2 * T], in0=y[:, k, :], scalar=mod[:, sh, k:k + 1],
                                                in1=act[:, k, 0:T].bitcast(F32), op0=ALU.add, op1=ALU.subtract)\
                          .then_inc(s_act[0], 1)
                hh.tick(DK)

            def gate_weight(layer, part):
                w = V_NORM + (4 * layer + 2 * part + 1) * DK
                ve.wait_ge(s_mod, 6 * layer + 3 * part + 3)
                ve.tensor_tensor(gamma[:, :], mod[:, 6 * layer + 3 * part + 2, :], vec[:, w:w + DK],
                                 ALU.mult).then_inc(s_gamma, 1)

            def post_norm(between):
                ve.wait_ge(s_ysqp, ysq_n.step(DK))
                rstd(y_rstd, bank[4][:, 0:T], D)
                ve.wait_ge(s_ys, ysq_n.at)
                for c in range(4):
                    four, x_four = y[:, 4 * c:4 * c + 4, :], x[:, 4 * c:4 * c + 4, :]
                    ve.tensor_tensor(four, four, y_rstd.unsqueeze(1).broadcast_to([P, 4, T]), ALU.mult)\
                      .then_inc(s_v, own.tick())
                    mine()
                    ve.tensor_tensor(x_four, x_four, four, ALU.add).then_inc(s_x, 1)
                    if c == 0:
                        between()

            def gate_rows_ready():
                ve.wait_ge(s["gate_log_ready"], 1)
                ve.scalar_tensor_tensor(out=gate_t2, in0=gates[:, :], scalar=0.0, in1=gate_t1, op0=ALU.min,
                                        op1=ALU.subtract).then_inc(s_v, own.tick())
                mine()
                ve.wait_ge(s["masks_ready"], 1)
                ve.tensor_tensor_scan(gate_rows, ones[0:GATES, :], gate_t2, 0.0, ALU.mult, ALU.add)\
                  .then_inc(s_v, own.tick())
                mine()
                ve.tensor_copy(gate_rows[0:M_HEADS, :], gates[0:M_HEADS, :]).then_inc(s["gate_rows_ready"], 1)

            def row_of(k, head):
                ve.wait_ge(s["gate_rows_ready"], 1)
                return ve.tensor_scalar(row(k), gate_rows, vec[0:GATES, bass.ds(V_COEF + head, 1)], None, ALU.mult)

            def before_split(ph, i, j):
                if ph.side == "fox":
                    pair, r = fox_pair(ph, i, j)
                    if r == 0:
                        for k in range(2):
                            row_of(k, M_HEADS + 2 * pair + k).then_inc(s["fox_row_ready"], 1)
                if ph.side == "mlstm" and j == 0:
                    for k in range(2):
                        row_of(k, 2 * i + k).then_inc(s["mlstm_row_ready"], 1)
                if ph.side == "gla":
                    h = ph.side0 + i
                    if j == 0:
                        if first_body(h):
                            ve.wait_ge(s_mac, PAUSE)
                        else:
                            ve.wait_ge(s["gla_level_decays"], h * LEVELS)
                        ve.memset(g_r, 0.0).then_inc(s["gla_level_exponents"], 1)
                    if j >= 1:
                        scale(h, j + 1)
                        use(h, j)
                    if 1 <= j < 7:
                        grow(h, j + 2)

            def normed(l_, at_):
                ve.reciprocal(stat[:, at_:at_ + 2], stat[:, at_:at_ + 2]).then_inc(s_v, own.tick())
                mine()
                for tb in range(TB):
                    i_ = ve.tensor_scalar(l_[:, tb, :], l_[:, tb, :], stat[:, at_ + tb:at_ + tb + 1], None, ALU.mult)
                return i_

            def masked_max(l_, bank_, at_):
                ve.tensor_tensor(l_, split2(bank_[:, :]), causal[:, :, :], ALU.add).then_inc(s_v, own.tick())
                mine()
                ve.tensor_reduce(stat[:, at_:at_ + 2], l_, AX_X, ALU.max).then_inc(s_v, own.tick())
                mine()

            def grow(h, lv):
                c = 1 << (lv - 2)
                of = [P, T // c, c]
                ve.wait_ge(s["gla_level_exponents"], h * LEVELS + lv - 1)
                ve.tensor_tensor(halves(g_r, c, 0), halves(g_r, c, 0),
                                 halves(g_a, c, 1)[:, :, c - 1:c].broadcast_to(of), ALU.add)\
                  .then_inc(s_v, own.tick())
                mine()
                ve.tensor_tensor(halves(g_a, c, 1), halves(g_a, c, 1),
                                 halves(g_a, c, 0)[:, :, c - 1:c].broadcast_to(of), ALU.add)\
                                   .then_inc(s["gla_level_exponents"], 1)

            def scale(h, lv):
                b = 1 << (lv - 1)
                ve.wait_ge(s["gla_level_decays"], h * LEVELS + lv)
                ve.wait_ge(s["gla_level_product"], h * (LEVELS + 1) + lv)
                ve.tensor_tensor(halves(g_q, b, 1), halves(region[:, bass.ds(GQ * T + h * 2 * T, 2 * T)], b, 1),
                                 g_e[:, 0:T].rearrange("p (n c) -> p n c", c=b), ALU.mult)
                ve.tensor_tensor(halves(g_k, b, 0), halves(region[:, bass.ds(GK * T + h * 2 * T, 2 * T)], b, 0),
                                 g_e[:, T:2 * T].rearrange("p (n c) -> p n c", c=b), ALU.mult)\
                  .then_inc(s["gla_level_scaled"], 1)

            def use(h, lv):
                prod = split2(bank[5 - lv % 2][:, 0:TB * P])
                if lv == LEVELS:
                    ve.wait_ge(s["gla_level_product"], (h + 1) * (LEVELS + 1))
                    ve.tensor_copy(g_s[:, 0, P:T], prod[:, 0, :]).then_inc(s["gla_level_used"], 1)
                else:
                    ve.copy_predicated(g_s[:, :, 0:P], blocks[:, lv, :].unsqueeze(1).broadcast_to([P, TB, P]), prod)\
                      .then_inc(s["gla_level_used"], 1)

            def after_split(ph, i, j):
                if ph.side == "fox":
                    pair, r = fox_pair(ph, i, j)
                    for k in range(2):
                        done = 2 * pair + k + 1
                        if r == 1:
                            ve.wait_ge(s_in["causal"], 16)
                            ve.wait_ge(s["fox_scores_ready"], done)
                            masked_max(fox_l(k), bank[4 + k], 4 * k)
                            ve.tensor_scalar(stat[:, 4 * k:4 * k + 2], stat[:, 4 * k:4 * k + 2], -1.0, None, ALU.mult)\
                              .then_inc(s["fox_max_ready"], 1)
                        if r == 2:
                            ve.wait_ge(s["fox_exp_ready"], done)
                            normed(fox_l(k), 4 * k + 2).then_inc(s["fox_weights_ready"], 1)
                if ph.side == "mlstm" and j == 1:
                    for k in range(2):
                        ve.wait_ge(s["mlstm_scores_ready"], 2 * i + k + 1)
                        masked_max(m_l(k), bank[4 + 2 * k], 8 * k)
                        ve.tensor_scalar(stat[:, 8 * k:8 * k + 2], stat[:, 8 * k:8 * k + 2], -1.0, 0.0, ALU.mult,
                                         ALU.min).then_inc(s["mlstm_max_ready"], 1)
                    for k in range(2):
                        ve.wait_ge(s["mlstm_exp_ready"], 2 * i + k + 1)
                        for tb in range(TB):
                            i_ = ve.tensor_tensor_reduce(m_l(k)[:, tb, :], m_l(k)[:, tb, :],
                                                         bank[5 + 2 * k][:, tb * T:(tb + 1) * T], 1.0, 0.0, ALU.mult,
                                                         ALU.add, stat[:, 8 * k + 2 + tb:8 * k + 3 + tb])
                        i_.then_inc(s_v, own.tick())
                        mine()
                        den = stat[:, 8 * k + 2:8 * k + 4]
                        ve.scalar_tensor_tensor(out=den, in0=den, scalar=-1.0, in1=den, op0=ALU.mult, op1=ALU.max)\
                          .then_inc(s_v, own.tick())
                        mine()
                        ve.tensor_tensor(den, den, stat[:, 8 * k + 4:8 * k + 6], ALU.max).then_inc(s_v, own.tick())
                        mine()
                        normed(m_l(k), 8 * k + 2).then_inc(s["mlstm_weights_ready"], 1)
                if ph.side == "gla":
                    h = ph.side0 + i
                    if j == 0:
                        if not first_body(h):
                            ve.wait_ge(s["gla_attended"], h)
                        ve.memset(g_s[:, :, :], 0.0).then_inc(s_v, own.tick())
                        mine()
                        scale(h, 1)
                        use(h, 0)
                        grow(h, 2)
                    if j == 1 and not first_body(h):
                        gla_store(h)
                    if j == 7:
                        use(h, 8)

            def gla_store(heads):
                ve.wait_ge(s["gla_squares_summed"], heads)
                ve.tensor_scalar(g_rstd, bank[5][:, T:2 * T], 1.0 / (G_DV * G_DK), EPS, ALU.mult, ALU.add)\
                  .then_inc(s["gla_mean_ready"], 1)
                ve.wait_ge(s["gla_root_ready"], heads)
                ve.reciprocal(g_rstd, g_rstd).then_inc(s["gla_rstd_ready"], 1)
                ve.wait_ge(s["gla_rstd_ready"], heads)
                for dv in range(4):
                    t = 4 * (heads - 1) + dv
                    i_ = ve.scalar_tensor_tensor(out=flat(y[:, bass.ds(t, 1), :]),
                                                 in0=bank[6 + dv // 2][:, (dv % 2) * T:(dv % 2 + 1) * T],
                                                 scalar=vec[:, bass.ds(V_GNORM + t, 1)], in1=g_rstd,
                                                 op0=ALU.mult, op1=ALU.mult)
                i_.then_inc(s["gla_stored"], 1)

            def after_evac(ph, i, j):
                if ph.side == "fox":
                    pair, r = fox_pair(ph, i, j)
                    if r == 3:
                        for k in range(2):
                            ve.wait_ge(s["fox_attended"], 2 + 2 * pair + k + 1)
                            ve.tensor_copy(flat(y[:, bass.ds(8 + 2 * pair + k, 1), :]), bank[4 + k][:, 0:T])\
                              .then_inc(s["fox_stored"], 1)
                if ph.side == "mlstm" and j == 3:
                    for k in range(2):
                        ve.wait_ge(s["mlstm_squares_summed"], 2 + 2 * i + k + 1)
                        rstd(m_q(k), bank[4 + 2 * k][:, 0:T], M_DV)
                        for dv in range(2):
                            t = 4 * i + 2 * k + dv
                            i_ = ve.scalar_tensor_tensor(out=flat(y[:, bass.ds(t, 1), :]),
                                                         in0=bank[5 + 2 * k][:, dv * T:(dv + 1) * T],
                                                         scalar=vec[:, bass.ds(V_MNORM + t, 1)], in1=m_q(k),
                                                         op0=ALU.mult, op1=ALU.mult)
                        i_.then_inc(s["mlstm_stored"], 1)
                if ph.side == "decay" and j == 3:
                    ve.wait_ge(s["gla_gate_log_steps"], 3 * i + 3)
                    ve.scalar_tensor_tensor(out=g_decay(i), in0=g_decay(i), scalar=0.0, in1=g_abs, op0=ALU.min,
                                            op1=ALU.subtract).then_inc(s["gla_decays_ready"], 1)

            def gate_tail(ph):
                order, gated, gate0, _ = tail(ph)

                def gate(k, c):
                    ve.wait_ge(s["output_gate_ready"], 2 * ph.layer + k + 1)
                    four = y[:, 4 * c:4 * c + 4, :]
                    ve.tensor_tensor(four, four, split2(region[:, (gate0 + 4 * c) * T:(gate0 + 4 * c + 4) * T], 4),
                                     ALU.mult).then_inc(s["gated"], 1)

                def low_part(k, c):
                    ve.wait_ge(s["gated_hi_ready"], 4 * ph.layer + k + 1)
                    ve.tensor_tensor(act[:, 4 * c:4 * c + 4, T:2 * T], y[:, 4 * c:4 * c + 4, :],
                                     act[:, 4 * c:4 * c + 4, 0:T].bitcast(F32), ALU.subtract)\
                                       .then_inc(s["gated_lo_ready"], 1)

                if ph.layer == 0:
                    ve.wait_ge(s["mlstm_stored"], 2 + M_HEADS)
                    for k, c in enumerate(gated):
                        gate(k, c)
                    for k, c in enumerate(order):
                        low_part(k, c)
                else:
                    ve.wait_ge(s["gla_stored"], G_HEADS - 1)
                    for c in range(3):
                        gate(c, c)
                    for c in range(3):
                        low_part(c, c)
                    gla_store(G_HEADS)
                    ve.wait_ge(s["gla_stored"], G_HEADS)
                    gate(3, 3)
                    low_part(3, 3)

            ve.sem_inc(s_lo, RAW_SLOTS)
            ve.sem_inc(s_evac, 2)
            ve.sem_inc(s["fox_stored"], 2)
            ve.sem_inc(s["mlstm_stored"], 2)
            ve.wait_ge(s_cond, 1)
            for sec in range(2):
                trips = PIECES // HEAD_SLOTS

                def eight_pieces(i, sec=sec, trips=trips):
                    for j in range(HEAD_SLOTS):
                        ve.wait_ge(s_head[j], 16 * (i + sec * trips + 1))
                        if j >= 2 or not (sec == 0 and first_body(i)):
                            ve.wait_ge(s_mac, sec * PIECES + i * HEAD_SLOTS + j - 1)
                        summed(region[:, j * PIECE:(j + 1) * PIECE], j % 2, i * (HEAD_SLOTS // 2) + j // 2,
                               first_body(i) and j < 2, (acc, head_acc)[sec]).then_inc(s_mac, 1)

                eight_pieces(0)
                if sec > 0:
                    x_root()
                    close_section(0)
                with ve.Fori(1, trips) as i:
                    eight_pieces(i)
            split(0, 0, 0)
            split_next(PHASES[0], 0, 0)
            close_section(1)
            norm_weight(0, 0)

            for ph in PHASES:
                if ph.norms:
                    if ph is not PHASES[0]:
                        split_next(ph, 0, 0)
                        x_root()
                    pre_norm(ph.layer, int(ph.kind == "ff_up"))
                if ph.kind == "values" and ph.layer == 0 and ph.side is None:
                    gate_rows_ready()
                if ph.side == "fox" and ph.side0 == 0:
                    ve.wait_ge(s["gate_transposed"], 1)
                    ve.tensor_copy(stat[:, 32:32 + TB * GATES], bank[7][:, 0:TB * GATES])\
                      .then_inc(s["gate_columns_ready"], 1)
                if ph.kind == "mixed":
                    gate_tail(ph)
                if ph.sums:
                    gate_weight(ph.layer, int(ph.kind == "ff_down"))

                def body(i, ph=ph):
                    k = 0

                    def sum_piece(k):
                        a = ph.a0 + i * ph.per_body + k
                        done = (ph.a0 + ph.now * ph.per_body + k) % PIECES - ph.now * ph.per_body
                        first = isinstance(a, int) and a % PIECES < 2
                        if first and a % PIECES == 0 and (k > 0 or ph.side == "mlstm" or not first_body(i)):
                            close_section(a // PIECES - 1)
                        ve.wait_ge(s_piece[k % ADA_SLOTS],
                                   16 * ((ph.a0 - 2 * PIECES + k) // ADA_SLOTS + i * (ph.per_body // ADA_SLOTS) + 1))
                        ve.wait_ge(s_mac, a - 1)
                        kt = a % PIECES // 2 if isinstance(a, int) else (done - k % 2) // 2 + i * (ph.per_body // 2)
                        summed(piece[:, k % ADA_SLOTS, :], k % 2, kt, first).then_inc(s_mac, 1)

                    for j in range(ph.units):
                        before_split(ph, i, j)
                        if not (ph.norms and first_body(i) and j == 0):
                            split_next(ph, i, j)
                        after_split(ph, i, j)
                        if ph.ada[j] > 0:
                            sum_piece(k)
                        n = unit(ph, i, j)
                        tile_no = ph.t0 + (j // 4 if ph.kind == "values" else j)
                        tile_ps = bank[2 * (tile_no % 2)][:, 0:T]
                        if ph.kind != "values" or j % 4 == 3:
                            ve.wait_ge(s_unit, SPLIT_SLOTS + n + 1)
                        if ph.kind == "values" and j % 4 == 3:
                            at_ = bass.ds(ph.dest + i * ph.units * P + (j // 4) * 512, 512)
                            for tb in range(TB):
                                i_ = ve.tensor_copy(values[:, tb, at_], bank[2 * (tile_no % 2) + tb][:, :])
                            i_.then_inc(s_evac, 1)
                        elif ph.kind == "gates":
                            bias = vec[0:GATES, V_GATEB:V_GATEB + 1] if ph.layer == 0 else 0.0
                            ve.tensor_scalar(gates[:, :], tile_ps[0:GATES], bias, None, ALU.add).then_inc(s_evac, 1)
                        elif ph.kind == "columns":
                            ve.tensor_copy(region[:, bass.ds((ph.dest + ph.units * i + j) * T, T)], tile_ps)\
                              .then_inc(s_evac, 1)
                        elif ph.kind == "mixed" or (ph.kind == "ff_down" and ph.group == 0):
                            ve.tensor_copy(flat(y[:, bass.ds(4 * i + j, 1), :]), tile_ps).then_inc(s_evac, 1)
                        elif ph.kind == "ff_down":
                            at_ = flat(y[:, bass.ds(4 * i + j, 1), :])
                            ve.tensor_tensor(at_, at_, tile_ps, ALU.add).then_inc(s_evac, 1)
                        elif ph.kind == "ff_up":
                            slot, is_g = j // 2, j % 2
                            out_ = (conv_g if is_g else conv_a)[:, slot, :]
                            ch = V_CONV + (ph.layer * FF_TILES + 2 * sum(FF_GROUPS[:ph.group]) + j) * (CONV_W + 1)
                            ch = ch + i * ph.units * (CONV_W + 1)
                            if not is_g:
                                ve.wait_ge(s_mul, (ph.pairs + slot + 1) + 2 * i)
                            ve.tensor_scalar(out_, tile_ps, vec[:, bass.ds(ch + 2, 1)], vec[:, bass.ds(ch + 3, 1)],
                                             ALU.mult, ALU.add).then_inc(s_v, own.tick())
                            mine()
                            ve.scalar_tensor_tensor(out=out_[:, 1:T], in0=tile_ps[:, 0:T - 1],
                                                    scalar=vec[:, bass.ds(ch + 1, 1)], in1=out_[:, 1:T],
                                                    op0=ALU.mult, op1=ALU.add).then_inc(s_v, own.tick())
                            mine()
                            ve.scalar_tensor_tensor(out=out_[:, 2:T], in0=tile_ps[:, 0:T - 2],
                                                    scalar=vec[:, bass.ds(ch, 1)], in1=out_[:, 2:T],
                                                    op0=ALU.mult, op1=ALU.add).then_inc(s_evac, 1)
                        after_evac(ph, i, j)
                        for more in range(1, ph.ada[j]):
                            sum_piece(k + more)
                        k += ph.ada[j]

                per = OWN.get((ph.kind, ph.side), 0)
                roots_per = 2 if ph.side == "mlstm" else 0
                base, roots_base = own.at, roots.at

                def counted(i, base=base, roots_base=roots_base, per=per, roots_per=roots_per):
                    own.at, own.extra, roots.at = base + i * per, 0, roots_base + i * roots_per
                    body(i)
                    assert own.extra == per, (ph.kind, ph.side, own.extra)
                repeat(ve, ph, counted)
                own.at, roots.at = base + per * ph.bodies, roots_base + roots_per * ph.bodies

                def between(ph=ph):
                    if ph.closes and ph.side != "fox":
                        close_section(ph.a_end // PIECES - 1)
                    if ph.sums and ph is not PHASES[-1]:
                        norm_weight(*((ph.layer, 1) if ph.kind == "mixed" else (ph.layer + 1, 0)))

                if ph.sums:
                    post_norm(between)
                else:
                    between()

        @block.tensor
        def _(pe):
            sqn = Tally(s_sq)
            ysqn = Tally(s_ysq)
            actn = Tally(s_act[1])

            def sum_x_squares():
                for b in range(4):
                    pe.wait_ge(s_sq, sqn.step())
                    for k in range(4):
                        i_ = pe.matmul(bank[4][:, 0:T], ones[:, 0:P], x_sq[:, b % 2, k, :], start=(b == 0 and k == 0),
                                       stop=(b == 3 and k == 3))
                    i_.then_inc(s_sqp, 1)

            def sum_y_square(q, slot):
                pe.wait_ge(s_ysq, ysqn.at + q + 1)
                first, last = isinstance(q, int) and q == 0, isinstance(q, int) and q == DK - 1
                pe.matmul(bank[4][:, 0:T], ones[:, 0:P], y_sq[:, slot, :], start=first, stop=last).then_inc(s_ysqp, 1)

            def reduce_section(sec, acc=acc):
                if sec > 0:
                    pe.wait_ge(s_mod, sec)
                pe.wait_ge(s_mac, (sec + 1) * PIECES)
                for j in range(DK):
                    i_ = pe.matmul(bank[7][:, j:j + 1], acc[:, j * P:(j + 1) * P], ones[:, 0:1], start=True, stop=True)
                i_.then_inc(s_red, 1)

            def transposes(dst, src):
                for tb, sb_ in ((0, 0), (1, 0), (1, 1)):
                    i_ = pe.transpose(dst[:, sb_ * T + tb * P:sb_ * T + (tb + 1) * P],
                                      src[:, tb, sb_ * P:(sb_ + 1) * P], ident[:, :])
                return i_

            def fox_work(ph, i, j):
                pair, r = fox_pair(ph, i, j)
                for k in range(2):
                    done = 2 * pair + k + 1
                    if r == 0:
                        pe.wait_ge(s["fox_stored"], 2 * (pair + 1))
                        pe.wait_ge(s["fox_queries_staged"], done)
                        pe.wait_ge(s["fox_row_ready"], done)
                        for tb in range(TB):
                            dst = bank[4 + k][:, tb * T:(tb + 1) * T]
                            pe.matmul(dst, fox_q(k)[:, tb * P:(tb + 1) * P],
                                      region[:, bass.ds((FK + k + 2 * pair) * T, T)], start=True, stop=False)
                            i_ = pe.matmul(dst, ones[0:GATES, 0:P], row(k), start=False, stop=True)
                        i_.then_inc(s["fox_scores_ready"], 1)
                    if r == 2:
                        pe.wait_ge(s["fox_weights_ready"], done)
                        transposes(bank[4 + k], fox_l(k)).then_inc(s["fox_transposed"], 1)
                    if r == 3:
                        pe.wait_ge(s["fox_values_staged"], done)
                        pe.wait_ge(s["fox_weights_staged"], done)
                        pe.matmul(bank[4 + k][:, 0:T], fox_v(k)[:, 0, :], fox_l(k)[:, 0, :], start=True, stop=False)
                        pe.matmul(bank[4 + k][:, P:T], fox_v(k)[:, 1, :], fox_l(k)[:, 1, P:T], start=False, stop=True)\
                          .then_inc(s["fox_attended"], 1)

            def mlstm_work(ph, i, j):
                for k in range(2):
                    done = 2 * i + k + 1
                    if j == 0:
                        pe.wait_ge(s["mlstm_stored"], 2 * (i + 1))
                        if k == 1:
                            pe.wait_ge(s_mod, 4)
                        pe.wait_ge(s["mlstm_queries_staged"], done)
                        pe.wait_ge(s["mlstm_row_ready"], done)
                        for tb in range(TB):
                            pe.matmul(bank[4 + 2 * k][:, tb * T:(tb + 1) * T], ones[0:GATES, 0:P], row(k),
                                      start=True, stop=True)
                            i_ = pe.matmul(bank[5 + 2 * k][:, tb * T:(tb + 1) * T], m_q(k)[:, tb * P:(tb + 1) * P],
                                           region[:, bass.ds((MK + k) * T + i * 2 * T, T)], start=True, stop=True)
                        i_.then_inc(s["mlstm_scores_ready"], 1)
                    if j == 1:
                        pe.wait_ge(s["mlstm_weights_ready"], done)
                        transposes(bank[4 + 2 * k], m_l(k)).then_inc(s["mlstm_transposed"], 1)
                    if j == 2:
                        pe.wait_ge(s["mlstm_values_staged"], done)
                        pe.wait_ge(s["mlstm_weights_staged"], done)
                        for dv in range(2):
                            dst = bank[5 + 2 * k][:, dv * T:(dv + 1) * T]
                            pe.matmul(dst, m_v(k)[:, 0, dv * P:(dv + 1) * P], m_l(k)[:, 0, :], start=True, stop=False)
                            i_ = pe.matmul(dst[:, P:T], m_v(k)[:, 1, dv * P:(dv + 1) * P], m_l(k)[:, 1, P:T],
                                           start=False, stop=True)
                        i_.then_inc(s["mlstm_attended"], 1)
                    if j == 3:
                        pe.wait_ge(s["mlstm_squares_ready"], done)
                        for dv in range(2):
                            i_ = pe.matmul(bank[4 + 2 * k][:, 0:T], ones[:, 0:P], m_v(k)[:, dv, :], start=dv == 0,
                                           stop=dv == 1)
                        i_.then_inc(s["mlstm_squares_summed"], 1)

            def product(h, lv):
                if lv > 0:
                    pe.wait_ge(s["gla_level_scaled"], h * LEVELS + lv)
                if lv == 2 and not first_body(h):
                    pe.wait_ge(s["gla_mean_ready"], h)
                if lv > 1:
                    pe.wait_ge(s["gla_level_used"], h * (LEVELS + 1) + lv - 1)
                dst = bank[5 - lv % 2]
                for tb in range(1 if lv == LEVELS else TB):
                    t0 = P if lv == LEVELS else tb * P
                    for dh in range(2):
                        i_ = pe.matmul(dst[:, tb * P:(tb + 1) * P], g_k[:, dh * T + tb * P:dh * T + (tb + 1) * P],
                                       g_q[:, dh * T + t0:dh * T + t0 + P], start=dh == 0, stop=dh == 1)
                i_.then_inc(s["gla_level_product"], 1)

            def decay_work(ph, i, j):
                if j == 0:
                    pe.wait_ge(s["loaded_a_w2"], 16)
                    pe.wait_ge(s_evac, 2 + ph.t0)
                    if not first_body(i):
                        pe.wait_ge(s["gla_gate_log_steps"], 3 * i)
                    for dh in range(2):
                        i_ = pe.matmul(bank[4][:, dh * T:(dh + 1) * T],
                                       g_w2[:, bass.ds((2 * i + dh) * P, P)], gates[:, :], start=True, stop=True)
                    i_.then_inc(s["gla_gate_projected"], 1)

            def gla_midway(ph, i, j):
                h = ph.side0 + i
                if j == 0:
                    pe.wait_ge(s["gla_head_staged"], h + 1)
                    product(h, 0)
                if j == 7:
                    product(h, 8)

            def gla_work(ph, i, j):
                h = ph.side0 + i
                if j == 0 and not first_body(h):
                    gla_sums(h)
                if j < 7:
                    product(h, j + 1)
                else:
                    pe.wait_ge(s["gla_level_used"], (h + 1) * (LEVELS + 1))
                    pe.wait_ge(s["gla_values_staged"], h + 1)
                    if not first_body(h):
                        pe.wait_ge(s["gla_stored"], h)
                    for dv in range(4):
                        dst = bank[6 + dv // 2][:, (dv % 2) * T:(dv % 2 + 1) * T]
                        pe.matmul(dst, g_v[:, 0, dv * P:(dv + 1) * P], g_s[:, 0, :], start=True, stop=False)
                        i_ = pe.matmul(dst[:, P:T], g_v[:, 1, dv * P:(dv + 1) * P], g_s[:, 1, 0:P], start=False,
                                       stop=True)
                    i_.then_inc(s["gla_attended"], 1)

            def gla_sums(heads):
                pe.wait_ge(s["gla_squares_ready"], heads)
                if not (isinstance(heads, int) and heads == G_HEADS):
                    pe.wait_ge(s["gla_level_used"], heads * (LEVELS + 1) + 1)
                for dv in range(4):
                    i_ = pe.matmul(bank[5][:, T:2 * T], ones[:, 0:P], g_sq[:, dv, :], start=dv == 0, stop=dv == 3)
                i_.then_inc(s["gla_squares_summed"], 1)

            pe.sem_inc(s_unit, SPLIT_SLOTS)
            pe.sem_inc(s["fox_attended"], 2)
            pe.sem_inc(s["mlstm_squares_summed"], 2)
            pe.wait_ge(s_ones, 1)
            pe.wait_ge(s_in["ident"], 16)
            sum_x_squares()
            reduce_section(0)
            reduce_section(1, head_acc)

            for ph in PHASES:
                if ph.norms and ph is not PHASES[0]:
                    sum_x_squares()
                if ph.side == "fox" and ph.side0 == 0:
                    pe.wait_ge(s["gate_rows_ready"], 1)
                    pe.wait_ge(s_mod, 3)
                    for tb in range(TB):
                        i_ = pe.transpose(bank[7][:, tb * GATES:(tb + 1) * GATES], gate_rows[:, tb * P:(tb + 1) * P],
                                          ident[0:GATES, 0:GATES])
                    i_.then_inc(s["gate_transposed"], 1)
                if ph.kind == "mixed" and ph.layer == 1:
                    gla_sums(G_HEADS)

                def columns(ph, i, j, slot):
                    pe.wait_ge(s_evac, ph.t0 + i * ph.tiles + j + 1)
                    dst = bank[2 * ((ph.t0 + j) % 2)][:, 0:T]
                    src = mid if ph.kind == "ff_down" else act
                    order = list(range(FF_GROUPS[ph.group] if ph.kind == "ff_down" else DK))
                    if ph.kind == "mixed" and first_body(i) and j == 0:
                        order = [4 * c + k for c in tail(ph)[0] for k in range(4)]
                    for at, kt in enumerate(order):
                        if ph.kind == "ff_down" and first_body(i) and j == 0:
                            pe.wait_ge(s_mid, ph.pairs - len(order) + kt + 1)
                        if first_body(i) and j == 0:
                            if ph.norms:
                                own, k = divmod(kt, 4)
                                if k < 3:
                                    pe.wait_ge(s_act[0], 3 * (actn.at + own) + k + 1)
                                else:
                                    pe.wait_ge(s_act[1], actn.at + own + 1)
                            if ph.kind == "mixed" and at % 4 == 0:
                                pe.wait_ge(s["gated_lo_ready"], 4 * ph.layer + at // 4 + 1)
                        if ph.side == "gla" and at == DK // 2:
                            gla_midway(ph, i, j)
                        w_hi, w_lo = hi[:, slot, kt * P:(kt + 1) * P], lo[:, slot, kt * P:(kt + 1) * P]
                        pe.matmul(dst, w_hi, src[:, kt, 0:T], start=at == 0, stop=False)
                        pe.matmul(dst, w_hi, src[:, kt, T:2 * T], start=False, stop=False)
                        i_ = pe.matmul(dst, w_lo, src[:, kt, 0:T], start=False, stop=at == len(order) - 1)
                    return i_

                def tokens(ph, i, j, slot):
                    tile_no = ph.t0 + j // 4
                    if j % 4 == 0:
                        pe.wait_ge(s_evac, ph.t0 + i * ph.tiles + j // 4 + 1)
                    for q in range(4):
                        kt = 4 * (j % 4) + q
                        if ph.side == "gla" and q == 2:
                            gla_midway(ph, i, j)
                        w_hi, w_lo = hi[:, slot, q * 512:(q + 1) * 512], lo[:, slot, q * 512:(q + 1) * 512]
                        for tb in range(TB):
                            dst = bank[2 * (tile_no % 2) + tb][:, :]
                            x_hi = act[:, kt, tb * P:(tb + 1) * P]
                            x_lo = act[:, kt, T + tb * P:T + (tb + 1) * P]
                            pe.matmul(dst, x_hi, w_hi, start=kt == 0, stop=False)
                            pe.matmul(dst, x_hi, w_lo, start=False, stop=False)
                            i_ = pe.matmul(dst, x_lo, w_hi, start=False, stop=kt == DK - 1)
                    return i_

                def body(i, ph=ph):
                    for j in range(ph.units):
                        slot = (ph.n0 + j) % SPLIT_SLOTS
                        pe.wait_ge(s_lo, RAW_SLOTS + unit(ph, i, j) + 1)
                        (tokens if ph.kind == "values" else columns)(ph, i, j, slot).then_inc(s_unit, 1)
                        if ph.side is not None:
                            {"fox": fox_work, "mlstm": mlstm_work, "decay": decay_work, "gla": gla_work}[ph.side](ph, i, j)
                        a = ph.a0 + i * ph.per_body + sum(ph.ada[:j])
                        if isinstance(a, int):
                            for last in range(a, min(a + ph.ada[j], ph.a_end - 1)):
                                if last % PIECES == PIECES - 1:
                                    reduce_section(last // PIECES)
                        if ph.sums and not (first_body(i) and j == 0):
                            sum_y_square(ph.units * i + j - 1, (j + 1) % 2)

                if ph.side == "decay":
                    ph.head = ph.bodies
                repeat(pe, ph, body)
                if ph.norms:
                    actn.tick(DK // 4)
                if ph.sums:
                    sum_y_square(DK - 1, 1)
                    ysqn.tick(DK)
                if ph.closes:
                    if ph.side == "fox":
                        pe.wait_ge(s["gate_columns_ready"], 1)
                    reduce_section(ph.a_end // PIECES - 1)


def columns_unit(w, cols):
    return w[:, cols].reshape(-1, P, P).transpose(1, 0, 2).reshape(P, -1)


def values_units(w):
    return w.reshape(4, 4, P, -1, 512).transpose(3, 0, 2, 1, 4).reshape(-1, P, UNIT)


def per_channel(v):
    return v.reshape(-1, P).T


def kernel(x, c, ada_w, ada_b, norm_w, even_in_w, m_gate_b, m_norm_w, fox_f_b, even_out_w, odd_in_w, gla_a_w2,
           gla_a_b, gla_norm_w, odd_out_w, ffn_in_w, ffn_conv_w, ffn_conv_b, ffn_out_w):
    from concourse import bacc
    from concourse.bass_utils import run_bass_kernel_spmd

    (x, c, ada_w, ada_b, norm_w, even_in_w, m_gate_b, m_norm_w, fox_f_b, even_out_w, odd_in_w, gla_a_w2, gla_a_b,
     gla_norm_w, odd_out_w, ffn_in_w, ffn_conv_w, ffn_conv_b, ffn_out_w) = (
        np.asarray(v) for v in (x, c, ada_w, ada_b, norm_w, even_in_w, m_gate_b, m_norm_w, fox_f_b, even_out_w,
                                odd_in_w, gla_a_w2, gla_a_b, gla_norm_w, odd_out_w, ffn_in_w, ffn_conv_w,
                                ffn_conv_b, ffn_out_w))
    even, odd = even_in_w[0], odd_in_w[0]
    parts = [[("gates", (3072, 3080), (6152, 6160)), ("columns", (3080, 4104), (4104, 5128)), ("values", (5128, 6152)),
              ("columns", (0, 512), (512, 1024)), ("values", (1024, 2048)), ("columns", (2048, 3072))],
             [("gates", (6144, 6160)), ("columns", (0, 1024), (1024, 2048)), ("values", (2048, 4096)),
              ("columns", (4096, 6144))]]
    units = np.zeros((UNITS, P, UNIT), np.float32)
    n = 0
    for layer in range(LAYERS):
        w = (even, odd)[layer]
        for kind, *spans in parts[layer]:
            cols = np.concatenate([w[:, a:b] for a, b in spans], axis=1)
            if kind == "gates":
                units[n].reshape(P, DK, P)[:, :, 0:GATES] = cols.reshape(DK, P, GATES).transpose(1, 0, 2)
                n += 1
            elif kind == "columns":
                for k in range(0, cols.shape[1], P):
                    units[n] = columns_unit(cols, slice(k, k + P))
                    n += 1
            else:
                got = values_units(cols)
                units[n:n + len(got)] = got
                n += len(got)
        w = (even_out_w, odd_out_w)[layer][0]
        for m in range(DK):
            units[n] = columns_unit(w, slice(m * P, (m + 1) * P))
            n += 1
        first = 0
        for tiles in FF_GROUPS:
            for k in range(first, first + tiles):
                for part in range(2):
                    at = part * D_FF + k * P
                    units[n] = columns_unit(ffn_in_w[layer], slice(at, at + P))
                    n += 1
            rows = ffn_out_w[layer][first * P:(first + tiles) * P]
            for m in range(DK):
                units[n][:, 0:tiles * P] = columns_unit(rows, slice(m * P, (m + 1) * P))
                n += 1
            first += tiles
    assert n == UNITS

    ada = ada_w.reshape(LAYERS, DK, P, 6, 2, PIECE).transpose(0, 3, 1, 4, 2, 5).reshape(-1, P, PIECE)
    conv = np.concatenate([ffn_conv_w.reshape(LAYERS, CONV_W, 2, D_FF // P, P),
                           ffn_conv_b.reshape(LAYERS, 1, 2, D_FF // P, P)], axis=1)
    conv = conv.transpose(4, 0, 3, 2, 1).reshape(P, -1)
    vec = np.zeros((P, V_END), np.float32)
    vec[:, V_C:V_ADAB] = per_channel(c)
    vec[:, V_ADAB:V_NORM] = per_channel(ada_b)
    vec[:, V_NORM:V_MNORM] = per_channel(norm_w)
    vec[:, V_MNORM:V_GNORM] = per_channel(m_norm_w)
    vec[:, V_GNORM:V_AB] = per_channel(gla_norm_w)
    vec[:, V_AB:V_GATEB] = per_channel(gla_a_b)
    vec[0:GATES, V_GATEB] = np.concatenate([m_gate_b[0], fox_f_b[0]])
    for h in range(M_HEADS):
        vec[h, V_COEF + h] = 1.0
        vec[M_HEADS + h, V_COEF + h] = -1.0
    for h in range(F_HEADS):
        vec[2 * M_HEADS + h, V_COEF + M_HEADS + h] = -1.0
    vec[:, V_CONV:V_END] = conv

    tok = np.arange(T)
    causal = np.zeros((P, TB, T), np.float32)
    for tb in range(TB):
        causal[:, tb][tok[None, :] > (tok[tb * P:(tb + 1) * P])[:, None]] = NEG
    blocks = np.zeros((P, LEVELS, P), np.float32)
    a, b = np.arange(P)[:, None], np.arange(P)[None, :]
    blocks[:, 0][a == b] = 1
    for lv in range(1, LEVELS):
        size = 1 << (lv - 1)
        blocks[:, lv][(a // size % 2 == 0) & (b // size == a // size + 1)] = 1

    arrays = {
        "w_units": units,
        "ada_pieces": np.ascontiguousarray(ada),
        "vectors": vec,
        "x_in": np.ascontiguousarray(x[0].T.reshape(DK, P, T).transpose(1, 0, 2)),
        "identity": np.eye(P, dtype=np.float32),
        "causal_in": causal,
        "blocks_in": blocks.reshape(P, -1),
        "a_w2": np.ascontiguousarray(gla_a_w2[0]),
    }
    nc = bacc.Bacc("TRN2", target_bir_lowering=False, num_devices=1)
    aps = [nc.dram_tensor(k, v.shape, mybir.dt.from_np(v.dtype), kind="ExternalInput").ap()
           for k, v in arrays.items()]
    out = nc.dram_tensor("x_out", (P, DK, T), F32, kind="ExternalOutput").ap()
    program(nc, *aps, out)
    got = run_bass_kernel_spmd(nc, [arrays], core_ids=[0]).results[0]["x_out"]
    return np.ascontiguousarray(got.transpose(1, 0, 2).reshape(1, D, T).transpose(0, 2, 1))
```
